# Optimizing a Trainium2 kernel written in Bass

```python
import math
import jax, jax.numpy as jnp
from jax import lax
import numpy as np

D_MODEL = 2048
BATCH = 1
SEQ = 256
DEPTH = 1
DEC_BATCH = 8
DEC_SEQ = 4
PAST_LEN = 256
PAGE_SIZE = 128

N_HEADS = 16
HEAD_DIM = 128
N_KV_HEADS = 4
GROUP = N_HEADS // N_KV_HEADS
IDX_HEADS = 16
IDX_DIM = 128
TOPK_MAX = 256
ROPE_THETA = 10000.0
Q_BLOCK = 128
POOL_WINDOWS = (2, 4, 8, 16)
N_POOL_GROUPS = 4
POOL_GROUP_DIM = 256
D_POOL = N_POOL_GROUPS * POOL_GROUP_DIM
POOL_OUT_DIM = D_MODEL // N_POOL_GROUPS
POOL_STATE = max(POOL_WINDOWS) - 1
PEER_HEADS = 8
PEER_N_KEYS = 128
PEER_N_EXPERTS = PEER_N_KEYS * PEER_N_KEYS
PEER_D_KEY = 256
PEER_HALF = PEER_D_KEY // 2
PEER_TOPK = 16
TOK_BLOCK = 128
EPS = 1e-6
Q_COLS = N_HEADS * HEAD_DIM
KV_COLS = N_KV_HEADS * HEAD_DIM
IDXQ_COLS = IDX_HEADS * IDX_DIM
W_IN_COLS = Q_COLS + 2 * KV_COLS + IDXQ_COLS + IDX_DIM + IDX_HEADS + D_POOL + 2 * D_MODEL

kernel_name = 'dsa_pool_peer_adaln_hybrid_step'

def split_points():
    widths = (Q_COLS, KV_COLS, KV_COLS, IDXQ_COLS, IDX_DIM, IDX_HEADS, D_POOL, D_MODEL)
    pts, acc = [], 0
    for w in widths:
        acc += w
        pts.append(acc)
    return tuple(pts)

def rms_norm(x, g):
    xf = x.astype(jnp.float32)
    y = xf * lax.rsqrt(jnp.mean(xf * xf, axis=-1, keepdims=True) + EPS)
    return (y * g.astype(jnp.float32)).astype(x.dtype)

def rope(x, pos):
    half = x.shape[-1] // 2
    freqs = ROPE_THETA ** (-jnp.arange(half, dtype=jnp.float32) / half)
    ang = pos.astype(jnp.float32)[:, None] * freqs[None, :]
    cos = jnp.cos(ang)[:, None, :]
    sin = jnp.sin(ang)[:, None, :]
    xf = x.astype(jnp.float32)
    x1, x2 = xf[..., :half], xf[..., half:]
    return jnp.concatenate([x1 * cos - x2 * sin, x1 * sin + x2 * cos], axis=-1).astype(x.dtype)

def modulation(c, w_mod, b_mod):
    m = jax.nn.silu(c) @ w_mod + b_mod
    m = m.reshape(c.shape[0], 6, D_MODEL)[:, :, None, :]
    return m[:, 0], m[:, 1], m[:, 2], m[:, 3], m[:, 4], m[:, 5]

def mixer_inputs(x, shift, scale, pos, norm1_g, w_in, q_norm_g, k_norm_g):
    B, T, _ = x.shape
    h = rms_norm(x, norm1_g) * (1 + scale) + shift
    proj = h @ w_in
    q, k, v, iq, ik, iw, p_in, ga, gb = jnp.split(proj, split_points(), axis=-1)
    q = rope(rms_norm(q.reshape(B, T, N_HEADS, HEAD_DIM), q_norm_g), pos)
    k = rope(rms_norm(k.reshape(B, T, N_KV_HEADS, HEAD_DIM), k_norm_g), pos)
    v = v.reshape(B, T, N_KV_HEADS, HEAD_DIM)
    iq = rope(iq.reshape(B, T, IDX_HEADS, IDX_DIM), pos)
    ik = rope(ik[:, :, None, :], pos)[:, :, 0, :]
    iw = iw * (IDX_HEADS ** -0.5 * IDX_DIM ** -0.5)
    return q, k, v, iq, ik, iw, p_in, ga, gb

def take_rows(rows, sel):
    return jax.vmap(lambda r, i: r[i])(rows, sel)

def sparse_attend(q, iq, iw, pos_q, k_idx_all, gather_kv, k_sel):
    L = k_idx_all.shape[1]
    dots = jax.nn.relu(jnp.einsum('bqhd,bsd->bqhs', iq.astype(jnp.float32), k_idx_all.astype(jnp.float32)))
    score = jnp.einsum('bqh,bqhs->bqs', iw.astype(jnp.float32), dots)
    valid = jnp.arange(L)[None, :] <= pos_q[:, None]
    score = jnp.where(valid[None], score, -jnp.inf)
    _, sel = lax.top_k(score, k_sel)
    ks, vs = gather_kv(sel)
    B, Tq = q.shape[:2]
    qg = q.reshape(B, Tq, N_KV_HEADS, GROUP, HEAD_DIM)
    logits = jnp.einsum('bqhgd,bqshd->bqhgs', qg, ks).astype(jnp.float32) * (HEAD_DIM ** -0.5)
    sel_ok = sel <= pos_q[None, :, None]
    logits = jnp.where(sel_ok[:, :, None, None, :], logits, -jnp.inf)
    probs = jax.nn.softmax(logits, axis=-1).astype(vs.dtype)
    out = jnp.einsum('bqhgs,bqshd->bqhgd', probs, vs)
    return out.reshape(B, Tq, N_HEADS * HEAD_DIM)

def prompt_attention(q, iq, iw, k, v, ik, k_sel):
    B, S = q.shape[:2]
    nb = S // Q_BLOCK

    def blocks(a):
        return jnp.moveaxis(a.reshape((B, nb, Q_BLOCK) + a.shape[2:]), 1, 0)

    def gather(sel):
        return take_rows(k, sel), take_rows(v, sel)

    def body(args):
        qb, iqb, iwb, posb = args
        return sparse_attend(qb, iqb, iwb, posb, ik, gather, k_sel)

    pos_blocks = jnp.arange(S).reshape(nb, Q_BLOCK)
    out = lax.map(body, (blocks(q), blocks(iq), blocks(iw), pos_blocks))
    return jnp.moveaxis(out, 0, 1).reshape(B, S, N_HEADS * HEAD_DIM)

def sample_attention(q, iq, iw, k_new, v_new, ik_new, cache_k, cache_v, cache_idx_k, page_table, pos, k_sel):
    Bd, T = q.shape[:2]
    past = page_table.shape[1] * PAGE_SIZE
    ik_past = cache_idx_k[page_table].reshape(Bd, past, IDX_DIM)
    ik_all = jnp.concatenate([ik_past, ik_new.astype(ik_past.dtype)], axis=1)
    k_pool = cache_k.reshape(-1, N_KV_HEADS, HEAD_DIM)
    v_pool = cache_v.reshape(-1, N_KV_HEADS, HEAD_DIM)

    def gather(sel):
        in_past = (sel < past)[..., None, None]
        lp = jnp.minimum(sel, past - 1)
        phys = jax.vmap(lambda pt, p: pt[p])(page_table, lp // PAGE_SIZE) * PAGE_SIZE + lp % PAGE_SIZE
        new_i = jnp.clip(sel - past, 0, T - 1)
        ks = jnp.where(in_past, k_pool[phys], take_rows(k_new, new_i).astype(k_pool.dtype))
        vs = jnp.where(in_past, v_pool[phys], take_rows(v_new, new_i).astype(v_pool.dtype))
        return ks, vs

    return sparse_attend(q, iq, iw, pos, ik_all, gather, k_sel)

def multiscale_pool(p_in, prefix, pos, w_pool, pool_scale):
    B, T, _ = p_in.shape
    padded = jnp.concatenate([prefix.astype(p_in.dtype), p_in], axis=1)
    cs = jnp.cumsum(padded.astype(jnp.float32), axis=1)
    cs = jnp.concatenate([jnp.zeros((B, 1, D_POOL), jnp.float32), cs], axis=1)
    end = cs[:, POOL_STATE + 1:, :]
    means = []
    for g, w in enumerate(POOL_WINDOWS):
        lo, hi = g * POOL_GROUP_DIM, (g + 1) * POOL_GROUP_DIM
        start = cs[:, POOL_STATE + 1 - w:POOL_STATE + 1 - w + T, lo:hi]
        cnt = jnp.minimum(pos + 1, w).astype(jnp.float32)[None, :, None]
        means.append((end[..., lo:hi] - start) / cnt)
    mean = jnp.stack(means, axis=2)
    pooled = (mean - p_in.reshape(B, T, N_POOL_GROUPS, POOL_GROUP_DIM).astype(jnp.float32)).astype(p_in.dtype)
    out = jnp.einsum('btgc,gcd->btgd', pooled, w_pool).reshape(B, T, D_MODEL) * pool_scale
    return out, padded[:, -POOL_STATE:, :]

def peer(h, w_peer_q, peer_keys, peer_u, peer_v):
    B, T, D = h.shape
    xt = h.reshape(-1, D)
    n = xt.shape[0]
    nb = -(-n // TOK_BLOCK)
    xt = jnp.pad(xt, ((0, nb * TOK_BLOCK - n), (0, 0))).reshape(nb, TOK_BLOCK, D)

    def blk(xb):
        q = (xb @ w_peer_q).reshape(TOK_BLOCK, PEER_HEADS, 2, PEER_HALF)
        s = jnp.einsum('nhpc,hpkc->nhpk', q, peer_keys).astype(jnp.float32)
        s1, i1 = lax.top_k(s[:, :, 0], PEER_TOPK)
        s2, i2 = lax.top_k(s[:, :, 1], PEER_TOPK)
        cand = (s1[..., :, None] + s2[..., None, :]).reshape(TOK_BLOCK, PEER_HEADS, PEER_TOPK * PEER_TOPK)
        cidx = (i1[..., :, None] * PEER_N_KEYS + i2[..., None, :]).reshape(TOK_BLOCK, PEER_HEADS, PEER_TOPK * PEER_TOPK)
        top_s, where = lax.top_k(cand, PEER_TOPK)
        eidx = jnp.take_along_axis(cidx, where, axis=-1)
        g = jax.nn.softmax(top_s, axis=-1)
        act = jax.nn.gelu(jnp.einsum('nhkd,nd->nhk', peer_u[eidx], xb).astype(jnp.float32), approximate=False)
        return jnp.einsum('nhk,nhkd->nd', (g * act).astype(xb.dtype), peer_v[eidx])

    out = lax.map(blk, xt).reshape(-1, D)[:n]
    return out.reshape(B, T, D)

def setup_inputs(seed: int = 0) -> dict:
    key = jax.random.key(seed)
    ks = jax.random.split(key, 24)
    f32 = jnp.float32
    n_pages = PAST_LEN // PAGE_SIZE
    n_used = DEC_BATCH * n_pages
    n_pool = n_used + (n_used + 3) // 4

    def nrm(k, shape, s=1.0):
        return jax.random.normal(k, shape, f32) * s

    page_table = jax.random.permutation(ks[0], n_pool)[:n_used].reshape(DEC_BATCH, n_pages).astype(jnp.int32)
    return {
        'x_prompt': nrm(ks[1], (BATCH, SEQ, D_MODEL)),
        'x_sample': nrm(ks[2], (DEC_BATCH, DEC_SEQ, D_MODEL)),
        'cache_k': nrm(ks[3], (n_pool, PAGE_SIZE, N_KV_HEADS, HEAD_DIM)),
        'cache_v': nrm(ks[4], (n_pool, PAGE_SIZE, N_KV_HEADS, HEAD_DIM)),
        'cache_idx_k': nrm(ks[5], (n_pool, PAGE_SIZE, IDX_DIM)),
        'state_pool': nrm(ks[6], (DEC_BATCH, POOL_STATE, D_POOL)),
        'page_table': page_table,
        'c_prompt': nrm(ks[7], (BATCH, D_MODEL)),
        'c_sample': nrm(ks[8], (DEC_BATCH, D_MODEL)),
        'norm1_g': 1.0 + nrm(ks[9], (D_MODEL,), 0.02),
        'norm2_g': 1.0 + nrm(ks[10], (D_MODEL,), 0.02),
        'w_mod': nrm(ks[11], (D_MODEL, 6 * D_MODEL), D_MODEL ** -0.5),
        'b_mod': nrm(ks[12], (6 * D_MODEL,), 0.02),
        'w_in': nrm(ks[13], (D_MODEL, W_IN_COLS), D_MODEL ** -0.5),
        'q_norm_g': 1.0 + nrm(ks[14], (HEAD_DIM,), 0.02),
        'k_norm_g': 1.0 + nrm(ks[15], (HEAD_DIM,), 0.02),
        'w_attn_proj': nrm(ks[16], (Q_COLS, D_MODEL), Q_COLS ** -0.5),
        'w_pool': nrm(ks[17], (N_POOL_GROUPS, POOL_GROUP_DIM, POOL_OUT_DIM), POOL_GROUP_DIM ** -0.5),
        'pool_scale': 1.0 + nrm(ks[18], (D_MODEL,), 0.02),
        'w_out': nrm(ks[19], (D_MODEL, D_MODEL), D_MODEL ** -0.5),
        'w_peer_q': nrm(ks[20], (D_MODEL, PEER_HEADS * PEER_D_KEY), D_MODEL ** -0.5),
        'peer_keys': nrm(ks[21], (PEER_HEADS, 2, PEER_N_KEYS, PEER_HALF), PEER_HALF ** -0.5),
        'peer_u': nrm(ks[22], (PEER_N_EXPERTS, D_MODEL), D_MODEL ** -0.5),
        'peer_v': nrm(ks[23], (PEER_N_EXPERTS, D_MODEL), PEER_HEADS ** -0.5),
    }

def reference(x_prompt, x_sample, cache_k, cache_v, cache_idx_k, state_pool, page_table, c_prompt, c_sample,
              norm1_g, norm2_g, w_mod, b_mod, w_in, q_norm_g, k_norm_g, w_attn_proj, w_pool, pool_scale,
              w_out, w_peer_q, peer_keys, peer_u, peer_v):
    S = x_prompt.shape[1]
    T = x_sample.shape[1]
    past = page_table.shape[1] * PAGE_SIZE

    def merge(x, attn, pool_out, ga, gb, gate1):
        merged = jax.nn.sigmoid(ga) * (attn @ w_attn_proj) + jax.nn.sigmoid(gb) * pool_out
        return x + gate1 * (merged @ w_out)

    def channel(x, shift2, scale2, gate2):
        h = rms_norm(x, norm2_g) * (1 + scale2) + shift2
        return x + gate2 * peer(h, w_peer_q, peer_keys, peer_u, peer_v)

    sh1, sc1, g1, sh2, sc2, g2 = modulation(c_prompt, w_mod, b_mod)
    pos_p = jnp.arange(S)
    q, k_p, v_p, iq, ik_p, iw, p_in, ga, gb = mixer_inputs(x_prompt, sh1, sc1, pos_p, norm1_g, w_in, q_norm_g, k_norm_g)
    attn_p = prompt_attention(q, iq, iw, k_p, v_p, ik_p, min(TOPK_MAX, S // 4))
    prefix_p = jnp.zeros((x_prompt.shape[0], POOL_STATE, D_POOL), p_in.dtype)
    pool_p, pool_state_p = multiscale_pool(p_in, prefix_p, pos_p, w_pool, pool_scale)
    h_p = merge(x_prompt, attn_p, pool_p, ga, gb, g1)
    y_prompt = channel(h_p, sh2, sc2, g2)

    sh1, sc1, g1, sh2, sc2, g2 = modulation(c_sample, w_mod, b_mod)
    pos_s = past + jnp.arange(T)
    q, k_s, v_s, iq, ik_s, iw, p_in, ga, gb = mixer_inputs(x_sample, sh1, sc1, pos_s, norm1_g, w_in, q_norm_g, k_norm_g)
    attn_s = sample_attention(q, iq, iw, k_s, v_s, ik_s, cache_k, cache_v, cache_idx_k, page_table, pos_s,
                              min(TOPK_MAX, (past + T) // 4))
    pool_s, pool_state_s = multiscale_pool(p_in, state_pool, pos_s, w_pool, pool_scale)
    h_s = merge(x_sample, attn_s, pool_s, ga, gb, g1)
    y_sample = channel(h_s, sh2, sc2, g2)

    return (y_prompt, y_sample, k_p, v_p, ik_p, pool_state_p, k_s, v_s, ik_s, pool_state_s)


_drawn_inputs = setup_inputs


def setup_inputs(seed=0):
    import zlib

    import numpy as np

    out = dict(_drawn_inputs(seed))
    spreads = {}
    factors = {'norm1_g': 3.067,
     'norm2_g': 20.24,
     'q_norm_g': 23.706,
     'k_norm_g': 7.846,
     'pool_scale': 4.703}
    for name, (base, spread) in spreads.items():
        noise = np.random.default_rng([zlib.crc32(name.encode()), seed]).standard_normal(out[name].shape)
        drawn = base * np.exp(spread * noise) if base else spread * noise
        out[name] = __import__('jax').numpy.asarray(drawn.astype(out[name].dtype))
    for name, factor in factors.items():
        out[name] = (out[name] * factor).astype(out[name].dtype)
    return out
```

```python
import math
from contextlib import ExitStack, contextmanager

import numpy as np

import concourse.bass as bass
from concourse import mybir

F32 = mybir.dt.float32
BF16 = mybir.dt.bfloat16
I32 = mybir.dt.int32
U32 = mybir.dt.uint32
ALU = mybir.AluOpType
ACT = mybir.ActivationFunctionType
AX = mybir.AxisListType

P = 128
D = 2048
KT = D // P
TP = 256
NB, NT = 8, 4
TS = NB * NT
T = TP + TS
TILES = [(0, 128), (128, 128), (256, 32)]
HQ, HK, GR = 16, 4, 4
PAST = 256
LS = PAST + NT
KSEL_P, KSEL_S = TP // 4, LS // 4
NC = 1 + NB
POOL_W = (2, 4, 8, 16)
NPRE = 15
CT = 8
PADP = NPRE + TP
PADS = NPRE + NT
PADT = PADP + NB * PADS
NE = 128
PH, PK = 8, 16
EPS = 1e-6
NEG = -1e30
TAKEN = -3e38
ATT_SCALE = 128 ** -0.5
IW_SCALE = 16 ** -0.5 * 128 ** -0.5
C_Q, C_K, C_V, C_IQ, C_IK, C_P = 0, 2048, 2560, 3072, 5120, 5264
C_GA, C_GB = 6288, 8336

U_MOD, U_IK, U_K, U_V, U_IQ, U_Q, U_P, U_POOL, U_GB, U_GA, U_PROJ, U_OUT, U_PQ = (
    0, 48, 50, 54, 58, 74, 90, 98, 114, 130, 146, 162, 178)
K_MOD, K_IK, K_K, K_V, K_IQ, K_Q, K_P, K_POOL, K_GB, K_GA, K_PROJ, K_OUT, K_PQ = (
    0, 48, 49, 51, 53, 61, 69, 73, 74, 82, 90, 98, 106)


def units_done(chunk):
    if chunk < K_IK:
        return chunk + 1
    if chunk < K_POOL:
        return U_IK + 2 * (chunk - K_IK + 1)
    if chunk == K_POOL:
        return U_GB
    return U_GB + 2 * (chunk - K_GB + 1)


class Chain:

    def __init__(self, eng, sem):
        self.eng, self.sem, self.n, self.base = eng, sem, 0, 0

    def __call__(self, ins):
        ins.then_inc(self.sem, 1)
        self.n += 1
        self.eng.wait_ge(self.sem, self.n + self.base)

    @contextmanager
    def loop(self, count, per):
        start = self.n
        with self.eng.Fori(0, count) as i:
            self.base = i * per if per else 0
            yield i
            assert self.n - start == per, (self.n - start, per)
            self.base = 0
        self.n = start + per * count


def constants():
    f = np.float32
    keep = np.zeros((P, 388), f)
    keep[:, 0:128] = np.eye(P)
    keep[:, 128:256] = 1.0
    keep[:, 256:384] = np.arange(P)[None]
    keep[:, 384] = EPS
    pos = np.concatenate([np.arange(TP), np.tile(PAST + np.arange(NT), NB)]).astype(f)
    half = 64
    freqs = (f(10000.0) ** (-np.arange(half, dtype=f) / f(half))).astype(f)
    ang = (pos[None, :] * freqs[:, None]).astype(f)
    mix = np.zeros((P, MIX), f)
    for k in range(half):
        mix[k + half, M_ROT + k] = -1.0
        mix[k, M_ROT + k + half] = 1.0
    mix[:, M_COS:M_COS + T] = np.concatenate([np.cos(ang)] * 2)
    mix[:, M_SIN:M_SIN + T] = np.concatenate([np.sin(ang)] * 2)
    for g, w in enumerate(POOL_W):
        mix[:, M_CNT + 16 * g:M_CNT + 16 * (g + 1)] = 1.0 / np.minimum(np.arange(16) + 1, w)
    mix[:, M_TRI:M_TRI + P] = np.where(np.arange(P)[None] > np.arange(P)[:, None], NEG, 0.0)
    q = np.arange(TS)
    s = np.arange(LS)
    mix[0:TS, M_SMASK:M_SMASK + LS] = np.where(s[None] > PAST + (q % NT)[:, None], NEG, 0.0)
    r = np.arange(P)
    for b in range(NB):
        hit = (q[:, None] == NT * b + (r % NT)[None]) & ((r % 32) < 16)[None]
        mix[0:TS, M_REP + P * b:M_REP + P * (b + 1)] = hit
    for h in range(16):
        mix[h, M_E16 + NT * h:M_E16 + NT * (h + 1)] = 1.0
    for k in range(64):
        mix[k, M_DT + k % NT] = 1.0
    return keep, mix


M_ROT, M_COS, M_SIN, M_CNT, M_TRI, M_SMASK, M_REP, M_E16, M_DT = (
    0, 128, 416, 704, 768, 896, 1156, 2180, 2244)
MIX = 2248


def layer_kernel(nc, x_p, x_s, cache_k, cache_v, cache_ik, state, ptab, c_p, c_s, norm1_g, norm2_g,
                 w_mod, b_mod, w_in, q_g, k_g, w_proj, w_pool, pool_scale, w_out, w_pq, pkeys,
                 peer_u, peer_v, keep_d, mix_d,
                 y_p, y_s, k_p, v_p, ik_p, ps_p, k_s, v_s, ik_s, ps_s):
    PAGES = ptab.shape[0] * ptab.shape[1]
    NPOOL = cache_k.shape[0]

    class Map:
        def __init__(self, at):
            self.at = at

        def __call__(self, name, shape, dt=F32):
            n = int(np.prod(shape[1:])) * (2 if dt == BF16 else 4)
            n = -(-n // 32) * 32
            t = nc.alloc_sbuf_tensor_at(name, list(shape), dt, offset=self.at)
            self.at += n
            return t

        def skip(self, n):
            at = self.at
            self.at += n
            return Map(at)

    top = Map(16896)
    keep = top("keep", [P, 388])
    ident, ones, iota = keep[:, 0:128], keep[:, 128:256], keep[:, 256:384]
    eps = keep[:, 384:385]
    X = top("X", [P, KT, T])
    h_at = top.at
    H = top("H", [P, KT, T])
    MOD = top("MOD", [P, 6 * KT, NC])
    AM = top("AM", [P, KT, NC])
    VEC = top("VEC", [P, 146])
    pages = top("pages", [1, 64], I32)
    n_x = top("n_x", [P, TS])
    norm_at = top.at
    n_s, n_v, n_y, n_t = (top(f"n_{c}", [P, T]) for c in "svyt")
    top.at = norm_at + 4 * 1152
    free_at = top.at
    mix = top("mix", [P, MIX])
    s_at = top.at
    S1 = top("S1", [P, KT, T])
    s2_at = top.at
    S2 = top("S2", [P, KT, T])
    s3_at = top.at
    S3 = top("S3", [P, KT, T])
    ring = [top(f"ring{n}", [P, KT, 256]) for n in range(4)]
    kv_at = top.at
    kTt = top("kTt", [P, HK, T])
    vTt = top("vTt", [P, HK, T])
    ikT = top("ikT", [P, T])
    iwT = top("iwT", [16, T])
    vN = top("vN", [P, 2, 512])
    tmp_at = top.at
    END = 229368
    assert END - tmp_at >= 17424, END - tmp_at

    m = Map(h_at)
    XTOK = [m("xtok0", [P, D]), m("xtok1", [P, D])]
    m = Map(tmp_at)
    XTOK.append(m("xtok2", [P, D]))
    VA, VB, CT_ = m("VA", [98, P]), m("VB", [48, P]), m("CT_", [P, KT, NC])
    CSIL = m("CSIL", [P, KT, NC])
    CTOK = Map(kv_at)("CTOK", [NC, D])
    MROW = Map(s_at)("MROW", [NC, 6 * D])

    m = Map(tmp_at)
    raw = [m(f"raw{n}", [P, T]) for n in range(2)]
    sq = [m(f"sq{n}", [P, T]) for n in range(2)]
    qks = [m(f"qks{n}", [P, T]) for n in range(2)]
    ra, rb_ = m("ra", [P, T]), m("rb_", [P, T])
    rv, ry, rt = m("rv", [P, T]), m("ry", [P, T]), m("rt", [P, T])
    stage = m("stage", [P, 512])
    iwN = m("iwN", [P, 2, 16])
    m = Map(tmp_at)
    kpg = [m(f"kpg{n}", [P, 2, 512]) for n in range(2)]
    vpg = [m(f"vpg{n}", [P, 2, 512]) for n in range(2)]
    smb = m("smb", [TS, LS])

    m = Map(s3_at)
    MB = m("MB", [P, 2, TP])
    QG = m("QG", [P, GR, T])
    VG = m("VG", [P, 2, P])
    E4 = m("E4", [P, GR, TP])
    PT = m("PT", [P, 2, GR, P])
    st1, st2 = m("st1", [P, GR]), m("st2", [P, GR])
    mx8 = m("mx8", [P, 2, 8])
    rsc = m("rsc", [P, TP])
    IPG = Map(s3_at + 2048 + 4608 + 1024)("IPG", [P, 2 * NB, P])
    m = Map(s2_at)
    IKB = [m(f"IKB{n}", [P, LS]) for n in range(2)]
    IQB = [m(f"IQB{n}", [P, 64]) for n in range(2)]
    RL = [m(f"RL{n}", [64, LS]) for n in range(2)]
    WZ = m("WZ", [64, 288])
    SSC = m("SSC", [TS, LS])
    smx = m("smx", [TS, 8])
    m = Map(s3_at + 2048)
    KTB = m("KTB", [P, HK, LS])
    QSB = [m(f"QSB{n}", [P, HK, 32]) for n in range(2)]
    EN = m("EN", [P, LS])
    PTB = m("PTB", [P, 2, P])
    PTN = m("PTN", [NT, P])
    VNB = m("VNB", [NT, 512])
    sb1, sb2 = m("sb1", [P, 1]), m("sb2", [P, 1])
    assert m.at <= s3_at + 18432

    PA = Map(s2_at)("PA", [P, CT, PADT])
    PB = Map(tmp_at)("PB", [P, CT, PADT])
    PC = Map(s3_at)("PC", [P, CT, PADT])
    POOLED = Map(kv_at)("POOLED", [P, CT, T])
    STT = Map(kv_at)("STT", [NB * NPRE, CT * P])
    PNEW = Map(kv_at + 9216)("PNEW", [P, CT, TS])
    PST = Map(kv_at + 10240)("PST", [P, CT * P])
    m = Map(tmp_at)
    SG = [m(f"SG{n}", [P, T]) for n in range(2)]
    og = m("og", [P, TS])

    m = Map(s2_at)
    KNAT = m("KNAT", [P, 16, P])
    KEYT = m("KEYT", [P, 16, P])
    SS = m("SS", [P, 16, NE])
    EQ = m("EQ", [P, PH * PK, PK])
    m = Map(kv_at)
    CAND = m("CAND", [P, PH, PK * PK])
    pv = m("pv", [P, 16, PK])
    pi = m("pi", [P, 16, PK], U32)
    pif = m("pif", [P, 16, PK])
    wv = m("wv", [P, PH, PK])
    wi = m("wi", [P, PH, PK], U32)
    wa = m("wa", [P, PH, PK], U32)
    waf = m("waf", [P, PH, PK])
    wbf = m("wbf", [P, PH, PK])
    ei = m("ei", [P, PH * PK])
    ej = m("ej", [P, PH * PK])
    s8 = m("s8", [P, PH])
    m = Map(END - 5 * 576 - 8)
    m.at = END - 5 * 576 - 8 - (END - 5 * 576 - 8) % 32
    IB, JB = m("IB", [P, T], BF16), m("JB", [P, T], BF16)
    GP = [m(f"GP{n}", [P, T], BF16) for n in range(3)]
    slots_at = END - 5 * 576 - 40
    GF = Map(norm_at)("GF", [P, T])
    GRr = Map(norm_at + 1152)("GRr", [P, T])
    assert tmp_at + 3000 < slots_at

    m = Map(free_at)
    GH = m("GH", [P, 64, T])
    UB = [m(f"UB{n}", [P, D]) for n in range(4)]
    ut_at = m.at
    UT = [m(f"UT{n}", [P, KT, P]) for n in range(2)]
    VBUF = [m(f"VBUF{n}", [P, D]) for n in range(4)]
    gt = [m(f"gt{n}", [P, T]) for n in range(2)]
    assert m.at <= slots_at, (m.at, slots_at)
    AJ = [Map(norm_at + 1152 * n)(f"AJ{n}", [P, T]) for n in range(4)]
    m = Map(ut_at)
    OA = [m(f"OA{n}", [P, 8, P], BF16) for n in range(2)]
    OQ = m("OQ", [P, 8, 64], BF16)
    OBp = [[m(f"OBp{n}_{k}", [P, 8, 64], BF16) for k in range(3)] for n in range(2)]
    iob = m("iob", [P, P], BF16)
    YS = [Map(free_at + 8192 * n)(f"YS{n}", [P, D]) for n in range(2)]

    ctx = ExitStack()
    bank = [ctx.enter_context(nc.psum_tensor(f"bank{n}", [P, 512], F32)) for n in range(8)]

    def sem(name):
        return ctx.enter_context(nc.semaphore(name))

    keep_in, mix_in, x_in, c_in, vec_in = (sem(n) for n in ("keep_in", "mix_in", "x_in", "c_in", "vec_in"))
    pages_in = sem("pages_in")
    wload = [sem(f"wload{n}") for n in range(4)]
    gemm_done, gemm_evac = sem("gemm_done"), sem("gemm_evac")
    x_turned, x_copied = sem("x_turned"), sem("x_copied")
    v_turned, v_copied = sem("v_turned"), sem("v_copied")
    c_turned, c_silu = sem("c_turned"), sem("c_silu")
    mod_turned, mod_done = sem("mod_turned"), sem("mod_done")
    sq_done, ssq_done, std_done, norm_done = sem("sq_done"), sem("ssq_done"), sem("std_done"), sem("norm_done")
    rot_done, qk_std, rope_done = sem("rot_done"), sem("qk_std"), sem("rope_done")
    iw_turned, iw_done = sem("iw_turned"), sem("iw_done")
    wz_mm, wz_done = sem("wz_mm"), sem("wz_done")
    ipg_in, ik_turned, ikb_done = sem("ipg_in"), sem("ik_turned"), sem("ikb_done")
    sl_done, sl_relu, ssc_mm = sem("sl_done"), sem("sl_relu"), sem("ssc_mm")
    smb_done, smb_ch = sem("smb_done"), sem("smb_ch")
    qg_ready, il_done, il_used = sem("qg_ready"), sem("il_done"), sem("il_used")
    mb_done = sem("mb_done")
    ag_ready, al_done, al_used, al_shift, al_exp, al_prob = (
        sem(n) for n in ("ag_ready", "al_done", "al_used", "al_shift", "al_exp", "al_prob"))
    pt_turned, pt_copied, ao_done, ao_copied = (sem(n) for n in ("pt_turned", "pt_copied", "ao_done", "ao_copied"))
    kv_turned, kv_staged = sem("kv_turned"), sem("kv_staged")
    kv_out = sem("kv_out")
    kvp_in = [sem(f"kvp_in{n}") for n in range(2)]
    sk_turned, sk_copied, sq_ready = sem("sk_turned"), sem("sk_copied"), sem("sq_ready")
    sal_done, sal_max, sal_exp, sal_prob = (sem(n) for n in ("sal_done", "sal_max", "sal_exp", "sal_prob"))
    sp_turned, sp_copied, so_done, so_copied = (sem(n) for n in ("sp_turned", "sp_copied", "so_done", "so_copied"))
    zero_done = sem("zero_done")
    st_in, st_turned, st_copied = sem("st_in"), sem("st_turned"), sem("st_copied")
    ps_turned, ps_staged, ps_out = sem("ps_turned"), sem("ps_staged"), sem("ps_out")
    pooled_done = sem("pooled_done")
    sig_done, sig_used = sem("sig_done"), sem("sig_used")
    keys_in, keys_turned, keys_copied = sem("keys_in"), sem("keys_turned"), sem("keys_copied")
    psc_done, psc_copied, psel_done, pex_done, pw_done = (
        sem(n) for n in ("psc_done", "psc_copied", "psel_done", "pex_done", "pw_done"))
    sl_turned, slot_copied, slots_done = sem("sl_turned"), sem("slot_copied"), sem("slots_done")
    oh_ready, oh_used, gh_copied = sem("oh_ready"), sem("oh_used"), sem("gh_copied")
    u_in = [sem(f"u_in{n}") for n in range(4)]
    vv_in = [sem(f"vv_in{n}") for n in range(4)]
    u_turned, ut_act, ut_dve = sem("u_turned"), sem("ut_act"), sem("ut_dve")
    s_done, gelu_done, aj_done = sem("s_done"), sem("gelu_done"), sem("aj_done")
    o_done, o_added = sem("o_done"), sem("o_added")
    y_turned, y_act, y_dve = sem("y_turned"), sem("y_act"), sem("y_dve")
    y_out = [sem(f"y_out{n}") for n in range(2)]
    dve_ch, act_ch, pool_ch = sem("dve_ch"), sem("act_ch"), sem("pool_ch")

    w_in_v = w_in.rearrange("(k p) c -> p k c", p=P)
    w_mod_v = w_mod.rearrange("(k p) c -> p k c", p=P)
    w_proj_v = w_proj.rearrange("(k p) c -> p k c", p=P)
    w_out_v = w_out.rearrange("(k p) c -> p k c", p=P)
    w_pq_v = w_pq.rearrange("(k p) c -> p k c", p=P)
    u_v = peer_u.rearrange("(i j) d -> j i d", j=NE)
    v_v = peer_v.rearrange("(i j) d -> j i d", j=NE)

    GROUPS = 16
    BATCHES = T // 8
    ROPES = 37

    block = ctx.enter_context(nc.Block())

    @block.sync
    def _(sp):
        for u in range(4):
            sp.dma_start(ring[u][:], w_mod_v[:, :, 256 * u:256 * (u + 1)]).then_inc(wload[u], 16)
        with sp.Fori(1, 12) as i:
            for u in range(4):
                sp.wait_ge(gemm_done, 4 * i + u - 3)
                sp.dma_start(ring[u][:], w_mod_v[:, :, bass.ds((4 * i + u) * 256, 256)]).then_inc(wload[u], 16)

        def chunk(n, src):
            sp.wait_ge(gemm_done, units_done(n - 4))
            w = src.shape[2]
            sp.dma_start(ring[n % 4][:, 0:src.shape[1], 0:w], src).then_inc(wload[n % 4], 16)

        def cols(first, col, count, src=w_in_v):
            for c in range(count):
                chunk(first + c, src[:, :, col + 256 * c:col + 256 * (c + 1)])

        chunk(K_IK, w_in_v[:, :, C_IK:C_IK + 144])
        cols(K_K, C_K, 2)
        cols(K_V, C_V, 2)
        cols(K_IQ, C_IQ, 8)
        cols(K_Q, C_Q, 8)
        cols(K_P, C_P, 4)
        sp.wait_ge(gemm_done, units_done(K_POOL - 4))
        slot = ring[K_POOL % 4][:].rearrange("p k c -> p (k c)").rearrange("p (g c) -> p g c", g=8)
        sp.dma_start(slot, w_pool.rearrange("g (k p) c -> p (g k) c", p=P)).then_inc(wload[K_POOL % 4], 16)
        cols(K_GB, C_GB, 8)
        cols(K_GA, C_GA, 8)
        cols(K_PROJ, 0, 8, w_proj_v)
        cols(K_OUT, 0, 8, w_out_v)
        cols(K_PQ, 0, 8, w_pq_v)
        sp.wait_ge(slots_done, 5)
        sp.wait_ge(gemm_done, U_PQ + 16)

        def experts(buf, table, tile):
            return buf[:], table[bass.ds(tile, 1)].rearrange("a i d -> (a i) d")

        for jj in range(4):
            sp.dma_start(UB[jj][:], u_v[jj]).then_inc(u_in[jj], 16)
        for jj in range(4):
            sp.dma_start(VBUF[jj][:], v_v[jj]).then_inc(vv_in[jj], 16)
        with sp.Fori(1, 2 * GROUPS) as i:
            for jj in range(4):
                sp.wait_ge(u_turned, 4 * i + jj - 3)
                sp.dma_start(*experts(UB[jj], u_v, 4 * i + jj)).then_inc(u_in[jj], 16)
            sp.wait_ge(o_done, 16 * i)
            for jj in range(4):
                sp.dma_start(*experts(VBUF[jj], v_v, 4 * i + jj)).then_inc(vv_in[jj], 16)

    @block.gpsimd
    def _(pool):
        pool.dma_start(keep[:], keep_d).then_inc(keep_in, 16)
        pool.dma_start(XTOK[0][:], x_p[0, 0:128]).then_inc(x_in, 16)
        pool.dma_start(XTOK[1][:], x_p[0, 128:256]).then_inc(x_in, 16)
        pool.dma_start(XTOK[2][0:TS], x_s.rearrange("b t d -> (b t) d")).then_inc(x_in, 16)
        pool.dma_start(CTOK[0:1], c_p).then_inc(c_in, 16)
        pool.dma_start(CTOK[1:NC], c_s).then_inc(c_in, 16)
        pool.dma_start(VA[0:96], b_mod.rearrange("(a b) -> a b", b=P)).then_inc(vec_in, 16)
        pool.dma_start(VA[96:97], q_g.rearrange("(a b) -> a b", b=P)).then_inc(vec_in, 16)
        pool.dma_start(VA[97:98], k_g.rearrange("(a b) -> a b", b=P)).then_inc(vec_in, 16)
        for n, v in enumerate((norm1_g, norm2_g, pool_scale)):
            pool.dma_start(VB[16 * n:16 * (n + 1)], v.rearrange("(a b) -> a b", b=P)).then_inc(vec_in, 16)
        pool.dma_start(mix[:], mix_d).then_inc(mix_in, 16)
        pool.dma_start(pages[:, 0:PAGES], ptab.rearrange("b n -> (b n)").rearrange("(a n) -> a n", a=1)).then_inc(pages_in, 16)
        pool.wait_ge(pages_in, 16)
        pool.wait_ge(mod_done, 2)
        page = []
        for n in range(PAGES):
            page.append(pool.value_load(pages[0:1, n:n + 1], min_val=0, max_val=NPOOL - 1))
            pool.dma_start(IPG[:, n], cache_ik[bass.ds(page[n], 1)].rearrange("a s d -> (a s) d")).then_inc(ipg_in, 16)
        n = 0
        for tt, (t0, nt) in enumerate(TILES):
            for which in range(3):
                n += 1
                pool.wait_ge(kv_staged, n)
                src = vN[:, tt] if which == 1 and tt < 2 else stage[:]
                if tt < 2:
                    dst = ((k_p, v_p)[which][0, t0:t0 + nt].rearrange("s h d -> s (h d)") if which < 2
                           else ik_p[0, t0:t0 + nt])
                else:
                    dst = ((k_s, v_s)[which].rearrange("b t h d -> (b t) (h d)") if which < 2
                           else ik_s.rearrange("b t d -> (b t) d"))
                pool.dma_start(dst, src[0:nt, 0:dst.shape[1]]).then_inc(kv_out, 16)
        pool.wait_ge(kv_out, 16 * 9)
        pool.wait_ge(rope_done, ROPES)
        for b in range(NB):
            if b >= 2:
                pool.wait_ge(so_done, b - 1)
            for n in range(2):
                at = bass.ds(page[2 * b + n], 1)
                pool.dma_start(kpg[b % 2][:, n], cache_k[at].rearrange("a s h d -> (a s) (h d)")).then_inc(kvp_in[b % 2], 16)
                pool.dma_start(vpg[b % 2][:, n], cache_v[at].rearrange("a s h d -> (a s) (h d)")).then_inc(kvp_in[b % 2], 16)
        pool.wait_ge(so_copied, NB)
        pool.dma_start(STT[0:NB * NPRE], state.rearrange("b s c -> (b s) c")).then_inc(st_in, 16)
        for b in range(NB):
            pool.dma_start(ps_s[b, 0:NPRE - NT], state[b, NT:NPRE]).then_inc(ps_out, 16)
        pool.wait_ge(ps_staged, 1)
        pool.dma_start(ps_p[0], PST[0:NPRE]).then_inc(ps_out, 16)
        pool.wait_ge(ps_out, 16 * (NB + 1))
        pool.wait_ge(ps_staged, 2)
        for b in range(NB):
            pool.dma_start(ps_s[b, NPRE - NT:NPRE], PST[NT * b:NT * (b + 1)]).then_inc(ps_out, 16)
        pool.wait_ge(ps_out, 16 * (2 * NB + 1))
        pool.wait_ge(gemm_evac, U_OUT + 16)
        pool.dma_start(KNAT[:], pkeys.rearrange("h p k c -> k (h p) c")).then_inc(keys_in, 16)
        for tt, (t0, nt) in enumerate(TILES):
            pool.wait_ge(y_act, tt + 1)
            pool.wait_ge(y_dve, tt + 1)
            dst = y_p[0, t0:t0 + nt] if tt < 2 else y_s.rearrange("b t d -> (b t) d")
            pool.dma_start(dst, YS[tt % 2][0:nt]).then_inc(y_out[tt % 2], 16)
        pool.wait_ge(y_out[0], 32)
        pool.wait_ge(y_out[1], 16)

    @block.tensor
    def _(pe):
        mm, turn = nc.tensor.matmul, nc.tensor.transpose

        def product(unit, out, lhs, rhs, steps):
            for k in range(steps):
                last = mm(out, lhs(k), rhs(k), start=(k == 0), stop=(k == steps - 1))
            return last

        def gemm(unit0, chunk0, u, i, rhs):
            if u % 2 == 0:
                c = chunk0 + u // 2
                pe.wait_ge(wload[c % 4], 16 * (c // 4 + 1) + 16 * i)
            pe.wait_ge(gemm_evac, unit0 + u - 3 + 8 * i)
            slot = ring[(chunk0 + u // 2) % 4]
            c0 = 128 * (u % 2)
            product(u, bank[(unit0 + u) % 4][:, 0:T], lambda k: slot[:, k, c0:c0 + 128],
                    lambda k: rhs[:, k], KT).then_inc(gemm_done, 1)

        pe.wait_ge(keep_in, 16)
        pe.wait_ge(x_in, 48)
        n = 0
        for tt, (t0, nt) in enumerate(TILES):
            for q in range(4):
                if n >= 2:
                    pe.wait_ge(x_copied, n - 1)
                for a in range(4):
                    last = turn(bank[4 + n % 2][:].rearrange("p (a t) -> p a t", a=4)[:, a, 0:nt],
                                XTOK[tt][0:nt, 128 * (4 * q + a):128 * (4 * q + a + 1)], ident[0:nt, 0:nt])
                last.then_inc(x_turned, 1)
                n += 1
        pe.wait_ge(vec_in, 96)
        turn(bank[6][:, 0:98], VA[0:98], ident[0:98, 0:98])
        turn(bank[6][:, 98:146], VB[0:48], ident[0:48, 0:48]).then_inc(v_turned, 1)
        pe.wait_ge(c_in, 32)
        for k in range(KT):
            last = turn(bank[7][:, NC * k:NC * (k + 1)], CTOK[0:NC, 128 * k:128 * (k + 1)], ident[0:NC, 0:NC])
        last.then_inc(c_turned, 1)

        pe.wait_ge(c_silu, 2)
        for u in range(4):
            pe.wait_ge(wload[u], 16)
            product(u, bank[u][0:NC, 0:256], lambda k: CSIL[:, k], lambda k: ring[u][:, k], KT).then_inc(gemm_done, 1)
        with pe.Fori(1, 12) as i:
            for u in range(4):
                pe.wait_ge(wload[u], 16 * i + 16)
                pe.wait_ge(gemm_evac, 4 * i + u - 3)
                product(u, bank[u][0:NC, 0:256], lambda k: CSIL[:, k], lambda k: ring[u][:, k], KT).then_inc(gemm_done, 1)
        pe.wait_ge(gemm_evac, 48)
        for half in range(2):
            for f in range(48):
                last = turn(bank[4 + half][:, NC * f:NC * (f + 1)],
                            MROW[0:NC, 128 * (48 * half + f):128 * (48 * half + f + 1)], ident[0:NC, 0:NC])
            last.then_inc(mod_turned, 1)

        def norm_sum(n):
            pe.wait_ge(sq_done, n + 1)
            product(0, bank[6][:, 0:T], lambda k: ones, lambda k: H[:, k], KT).then_inc(ssq_done, 1)

        norm_sum(0)
        pe.wait_ge(norm_done, 1)
        pe.wait_ge(mix_in, 16)

        def rotary(r, unit, normed, off=0):
            pe.wait_ge(gemm_evac, unit + 1)
            mm(bank[4 + r % 2][:, 0:T], mix[:, M_ROT:M_ROT + 128], raw[r % 2][:], start=True, stop=True)\
                .then_inc(rot_done, 1)
            if normed:
                mm(bank[6 + r % 2][:, 0:T], ones, sq[r % 2][:], start=True, stop=True).then_inc(rot_done, 1)

        c = K_IK
        pe.wait_ge(wload[c % 4], 16 * (c // 4 + 1))
        pe.wait_ge(gemm_evac, U_IK - 3)
        product(0, bank[U_IK % 4][:, 0:T], lambda k: ring[c % 4][:, k, 0:128], lambda k: H[:, k], KT).then_inc(gemm_done, 1)
        product(0, bank[(U_IK + 1) % 4][0:16, 0:T], lambda k: ring[c % 4][:, k, 128:144], lambda k: H[:, k], KT)\
            .then_inc(gemm_done, 1)
        rotary(0, U_IK, False)
        for u in range(4):
            gemm(U_K, K_K, u, 0, H)
            rotary(1 + u, U_K + u, True)
        for u in range(4):
            gemm(U_V, K_V, u, 0, H)
        pe.wait_ge(gemm_evac, U_IK + 2)
        pe.wait_ge(rope_done, 5)
        for tt in range(2):
            last = turn(bank[7][:, 16 * tt:16 * (tt + 1)], iwT[0:16, 128 * tt:128 * (tt + 1)], ident[0:16, 0:16])
        last.then_inc(iw_turned, 1)
        pe.wait_ge(iw_done, 1)
        mm(bank[7][0:64, 0:TS], mix[0:16, M_E16:M_E16 + 64], iwT[0:16, TP:T], start=True, stop=True).then_inc(wz_mm, 1)
        n = 0
        for tt, (t0, nt) in enumerate(TILES):
            for which in range(3):
                if n == 0:
                    pe.wait_ge(rope_done, 5)
                    pe.wait_ge(gemm_evac, U_V + 4)
                if n >= 1:
                    pe.wait_ge(kv_staged, n)
                for g in range(1 if which == 2 else 4):
                    src = (kTt[:, g], vTt[:, g], ikT[:])[which]
                    last = turn(bank[6][0:nt, 128 * g:128 * (g + 1)], src[:, t0:t0 + nt], ident)
                last.then_inc(kv_turned, 1)
                n += 1
        pe.wait_ge(wz_done, 2)
        pe.wait_ge(kv_staged, 9)

        with pe.Fori(0, 2) as i:
            for u in range(8):
                gemm(U_IQ, K_IQ, u, i, H)
                pe.wait_ge(gemm_evac, U_IQ + u + 1 + 8 * i)
                pe.wait_ge(rope_done, 4 + u + 8 * i)
                mm(bank[4 + (5 + u) % 2][:, 0:T], mix[:, M_ROT:M_ROT + 128], raw[(5 + u) % 2][:], start=True, stop=True)\
                    .then_inc(rot_done, 1)
        pe.wait_ge(rope_done, 21)

        for b in range(NB):
            if b == 0:
                pe.wait_ge(ipg_in, 16 * PAGES)
            else:
                pe.wait_ge(ikb_done, 3 * b)
            for n in range(2):
                last = turn(bank[4][:, 128 * n:128 * (n + 1)], IPG[:, 2 * b + n], ident)
            last.then_inc(ik_turned, 1)
            pe.wait_ge(ikb_done, 3 * (b + 1))
            if b:
                pe.wait_ge(sl_relu, b)
            mm(bank[5][0:64, 0:LS], IQB[b % 2][:], IKB[b % 2][:], start=True, stop=True)\
                .then_inc(sl_done, 1)
            pe.wait_ge(sl_relu, b + 1)
            mm(bank[6][0:TS, 0:LS], WZ[:, 32 * b:32 * (b + 1)], RL[b % 2][:], start=(b == 0), stop=(b == NB - 1))\
                .then_inc(ssc_mm, 1)
        with pe.Fori(0, 4) as i:
            pe.wait_ge(qg_ready, i + 1)
            for tt in range(2):
                pe.wait_ge(il_used, 2 * i + tt)
                for a in range(4):
                    last = mm(bank[4 + a // 2][:, 256 * (a % 2):256 * (a % 2 + 1)], QG[:, a, 128 * tt:128 * (tt + 1)],
                              ikT[:, 0:TP], start=True, stop=True)
                last.then_inc(il_done, 1)
        pe.wait_ge(il_used, 8)

        with pe.Fori(0, 2) as i:
            for u in range(8):
                gemm(U_Q, K_Q, u, i, H)
                pe.wait_ge(gemm_evac, U_Q + u + 1 + 8 * i)
                pe.wait_ge(rope_done, 20 + u + 8 * i)
                r = 21 + u
                mm(bank[4 + r % 2][:, 0:T], mix[:, M_ROT:M_ROT + 128], raw[r % 2][:], start=True, stop=True)
                mm(bank[6 + r % 2][:, 0:T], ones, sq[r % 2][:], start=True, stop=True).then_inc(rot_done, 1)
        pe.wait_ge(rope_done, ROPES)

        with pe.Fori(0, 4) as g:
            pe.wait_ge(ag_ready, 2 * g + 2)
            for tt in range(2):
                S = 128 * (tt + 1)
                pe.wait_ge(al_used, 2 * g + tt)
                for a in range(4):
                    last = mm(bank[4 + a // 2][:, 256 * (a % 2):256 * (a % 2) + S], QG[:, a, 128 * tt:128 * (tt + 1)],
                              kTt[:, bass.ds(g, 1), 0:S].rearrange("p a s -> p (a s)"), start=True, stop=True)
                last.then_inc(al_done, 1)
                pe.wait_ge(al_prob, 2 * g + tt + 1)
                for sb in range(tt + 1):
                    pe.wait_ge(pt_copied, 3 * g + tt + sb)
                    for a in range(4):
                        last = turn(bank[6][:, 128 * a:128 * (a + 1)], E4[:, a, 128 * sb:128 * (sb + 1)], ident)
                    last.then_inc(pt_turned, 1)
                pe.wait_ge(pt_copied, 3 * g + 2 * tt + 1)
                pe.wait_ge(ao_copied, 2 * g + tt)
                for sb in range(tt + 1):
                    last = mm(bank[7][:], VG[:, sb], PT[:, sb].rearrange("p a t -> p (a t)"),
                              start=(sb == 0), stop=(sb == tt))
                last.then_inc(ao_done, 1)
        pe.wait_ge(ao_copied, 8)

        for b in range(NB):
            pe.wait_ge(kvp_in[b % 2], 64 * (b // 2 + 1))
            if b:
                pe.wait_ge(sp_copied, b)
                pe.wait_ge(so_copied, b)
            for n in range(2):
                for g in range(4):
                    last = turn(bank[4 + n][:, 128 * g:128 * (g + 1)], kpg[b % 2][:, n, 128 * g:128 * (g + 1)], ident)
                last.then_inc(sk_turned, 1)
            pe.wait_ge(sk_copied, 3 * (b + 1))
            pe.wait_ge(sq_ready, b + 1)
            mm(bank[6][:, 0:LS], mix[0:TS, M_REP + 128 * b:M_REP + 128 * (b + 1)], smb[:], start=True, stop=False,
               skip_group_check=True)
            for g in range(4):
                last = mm(bank[6][32 * g:32 * g + 32, 0:LS], QSB[b % 2][:, g], KTB[:, g], start=False, stop=True,
                          skip_group_check=True)
            last.then_inc(sal_done, 1)
            for g in range(4):
                last = turn(bank[5][0:NT, 128 * g:128 * (g + 1)], vTt[:, g, TP + NT * b:TP + NT * (b + 1)], ident)
            pe.wait_ge(sal_prob, b + 1)
            for n in range(2):
                turn(bank[7][:, 128 * n:128 * (n + 1)], EN[:, 128 * n:128 * (n + 1)], ident)
            turn(bank[7][0:NT, 256:384], EN[:, PAST:LS], ident).then_inc(sp_turned, 1)
            pe.wait_ge(sp_copied, b + 1)
            for g in range(4):
                o = bank[4][:, 16 * g:16 * (g + 1)]
                for n in range(2):
                    mm(o, vpg[b % 2][:, n, 128 * g:128 * (g + 1)], PTB[:, n, 32 * g:32 * g + 16], start=(n == 0), stop=False)
                last = mm(o, VNB[0:NT, 128 * g:128 * (g + 1)], PTN[0:NT, 32 * g:32 * g + 16], start=False, stop=True)
            last.then_inc(so_done, 1)

        for u in range(8):
            gemm(U_P, K_P, u, 0, H)
        pe.wait_ge(st_in, 16)
        for n in range(2):
            for a in range(4):
                last = turn(bank[4 + n][:, 120 * a:120 * (a + 1)], STT[0:120, 128 * (4 * n + a):128 * (4 * n + a + 1)], ident[0:120, 0:120])
            last.then_inc(st_turned, 1)
        pe.wait_ge(gemm_evac, U_P + 8)
        pe.wait_ge(st_copied, 2)
        for a in range(8):
            last = turn(bank[6 + a // 4][0:NPRE, 128 * (a % 4):128 * (a % 4 + 1)], PA[:, a, PADP - NPRE:PADP], ident)
        last.then_inc(ps_turned, 1)
        for a in range(8):
            last = turn(bank[4 + a // 4][0:TS, 128 * (a % 4):128 * (a % 4 + 1)], PNEW[:, a], ident)
        last.then_inc(ps_turned, 1)
        pe.wait_ge(pooled_done, 1)
        pe.wait_ge(wload[K_POOL % 4], 16 * (K_POOL // 4 + 1))
        slot = ring[K_POOL % 4][:].rearrange("p k c -> p (k c)").rearrange("p (g k c) -> p g k c", g=4, k=2)
        for u in range(16):
            g = u // 4
            pe.wait_ge(gemm_evac, U_POOL + u - 3)
            product(u, bank[(U_POOL + u) % 4][:, 0:T], lambda k: slot[:, g, k, 128 * (u % 4):128 * (u % 4 + 1)],
                    lambda k: POOLED[:, 2 * g + k], 2).then_inc(gemm_done, 1)
        for u0, c0, rhs in ((U_GB, K_GB, H), (U_GA, K_GA, H), (U_PROJ, K_PROJ, S1), (U_OUT, K_OUT, S3)):
            if u0 == U_OUT:
                pe.wait_ge(gemm_evac, U_OUT)
            with pe.Fori(0, 2) as i:
                for u in range(8):
                    gemm(u0, c0, u, i, rhs)
        norm_sum(1)
        pe.wait_ge(norm_done, 2)
        with pe.Fori(0, 2) as i:
            for u in range(8):
                gemm(U_PQ, K_PQ, u, i, H)

        pe.wait_ge(keys_in, 16)
        for n in range(4):
            for a in range(4):
                last = turn(bank[4 + n][:, 128 * a:128 * (a + 1)], KNAT[:, 4 * n + a], ident)
        last.then_inc(keys_turned, 1)
        pe.wait_ge(gemm_evac, U_PQ + 16)
        pe.wait_ge(keys_copied, 1)
        for tt, (t0, nt) in enumerate(TILES):
            if tt:
                pe.wait_ge(slot_copied, 3 * tt)
            for a in range(16):
                last = mm(bank[4 + a // 4][0:nt, 128 * (a % 4):128 * (a % 4 + 1)], S1[:, a, t0:t0 + nt], KEYT[:, a],
                          start=True, stop=True)
            last.then_inc(psc_done, 1)
            pe.wait_ge(pw_done, tt + 1)
            for n, src in enumerate((ei, ej, wv)):
                flat = src[0:nt].rearrange("t h k -> t (h k)") if n == 2 else src[0:nt]
                last = turn(bank[n][:, 0:nt], flat, ident[0:nt, 0:nt])
            last.then_inc(sl_turned, 1)
        pe.wait_ge(slots_done, 5)
        turn(bank[3][:, 0:128], ident, ident).then_inc(oh_used, 1)

        for half in range(2):
            nb0 = BATCHES * half
            with pe.Fori(0, BATCHES // 2) as i:
                for par in range(2):
                    pe.wait_ge(oh_ready, nb0 + 2 * i + par + 1)
                    pe.wait_ge(gh_copied, nb0 + 2 * i + par)
                    out = bank[par][:].rearrange("p (t j) -> p t j", t=8)
                    for t in range(8):
                        for k in range(3):
                            last = mm(out[:, t], OA[par][:, t], OBp[par][k][:, t], start=(k == 0), stop=(k == 2))
                    last.then_inc(oh_used, 1)
            pe.wait_ge(gh_copied, nb0 + BATCHES + 1)
            with pe.Fori(0, GROUPS) as i:
                n0 = 64 * half + 4 * i
                g0 = GROUPS * half + i

                def turn_u(jj):
                    pe.wait_ge(u_in[jj], 16 * g0 + 16)
                    pe.wait_ge(ut_act, n0 + jj)
                    pe.wait_ge(ut_dve, n0 + jj)
                    for k in range(KT):
                        last = turn(bank[k // 4][:, 128 * (k % 4):128 * (k % 4 + 1)], UB[jj][:, 128 * k:128 * (k + 1)], ident)
                    last.then_inc(u_turned, 1)

                def score(jj):
                    pe.wait_ge(ut_act, n0 + jj + 1)
                    pe.wait_ge(ut_dve, n0 + jj + 1)
                    pe.wait_ge(gelu_done, n0 + max(jj - 1, 0))
                    product(jj, bank[4 + jj % 2][:, 0:T], lambda k: UT[jj % 2][:, k], lambda k: H[:, k], KT)\
                        .then_inc(s_done, 1)

                turn_u(0)
                turn_u(1)
                score(0)
                turn_u(2)
                score(1)
                turn_u(3)
                score(2)
                score(3)
                for jj in range(4):
                    pe.wait_ge(vv_in[jj], 16 * g0 + 16)
                pe.wait_ge(aj_done, n0 + 4)
                for m_ in range(KT):
                    pe.wait_ge(o_added, 16 * g0 + max(m_ - 1, 0))
                    product(m_, bank[6 + m_ % 2][:, 0:T], lambda k: VBUF[k][:, 128 * m_:128 * (m_ + 1)],
                            lambda k: AJ[k][:], 4).then_inc(o_done, 1)
        pe.wait_ge(o_added, 16 * 2 * GROUPS)
        for tt, (t0, nt) in enumerate(TILES):
            if tt:
                pe.wait_ge(y_act, tt)
                pe.wait_ge(y_dve, tt)
            for k in range(KT):
                last = turn(bank[k // 4][0:nt, 128 * (k % 4):128 * (k % 4 + 1)], X[:, k, t0:t0 + nt], ident)
            last.then_inc(y_turned, 1)

    @block.scalar
    def _(act):
        ch = Chain(act, act_ch)
        run = nc.scalar.activation

        def evac(unit, out, src, func=ACT.Copy, **kw):
            act.wait_ge(gemm_done, unit + 1)
            run(out, src, func, **kw).then_inc(gemm_evac, 1)

        n = 0
        for tt, (t0, nt) in enumerate(TILES):
            for q in range(4):
                act.wait_ge(x_turned, n + 1)
                run(X[:, 4 * q:4 * q + 4, t0:t0 + nt],
                    bank[4 + n % 2][:].rearrange("p (a t) -> p a t", a=4)[:, :, 0:nt], ACT.Copy).then_inc(x_copied, 1)
                n += 1
        act.wait_ge(v_turned, 1)
        run(VEC[:], bank[6][:, 0:146], ACT.Copy).then_inc(v_copied, 1)
        act.wait_ge(c_turned, 1)
        run(CT_[:], bank[7][:, 0:NC * KT].rearrange("p (k c) -> p k c", c=NC), ACT.Sigmoid).then_inc(c_silu, 1)
        with act.Fori(0, 12) as i:
            for u in range(4):
                act.wait_ge(gemm_done, 4 * i + u + 1)
                run(MROW[0:NC, bass.ds((4 * i + u) * 256, 256)], bank[u][0:NC, 0:256], ACT.Copy).then_inc(gemm_evac, 1)

        def norm_squares(n):
            if n == 0:
                act.wait_ge(x_copied, 12)
            else:
                act.wait_ge(gemm_evac, U_OUT + 16)
                act.wait_ge(gemm_done, U_GA + 16)
            run(H[:], X[:], ACT.Square).then_inc(sq_done, 1)
            act.wait_ge(ssq_done, n + 1)
            run(n_s[:], bank[6][:, 0:T], ACT.Sqrt, bias=eps, scale=1.0 / D).then_inc(std_done, 1)

        norm_squares(0)

        def raw_unit(r, unit, g=None):
            act.wait_ge(gemm_done, unit + 1)
            if g is not None:
                run(sq[r % 2][:], bank[unit % 4][:, 0:T], ACT.Square)
                run(raw[r % 2][:], bank[unit % 4][:, 0:T], ACT.Copy, scale=g).then_inc(gemm_evac, 1)
            else:
                run(raw[r % 2][:], bank[unit % 4][:, 0:T], ACT.Copy).then_inc(gemm_evac, 1)

        raw_unit(0, U_IK)
        evac(U_IK + 1, iwT[:], bank[(U_IK + 1) % 4][0:16, 0:T], scale=IW_SCALE)
        for u in range(4):
            if u >= 1:
                act.wait_ge(rope_done, u)
            raw_unit(1 + u, U_K + u, VEC[:, 97:98])
            act.wait_ge(rot_done, 1 + 2 * (u + 1))
            run(qks[(1 + u) % 2][:], bank[6 + (1 + u) % 2][:, 0:T], ACT.Sqrt, bias=eps, scale=1.0 / 128).then_inc(qk_std, 1)
        for u in range(4):
            evac(U_V + u, vTt[:, u], bank[(U_V + u) % 4][:, 0:T])
        act.wait_ge(iw_turned, 1)
        run(iwN[:], bank[7][:, 0:32].rearrange("p (a b) -> p a b", a=2), ACT.Copy).then_inc(iw_done, 1)
        n = 0
        for tt, (t0, nt) in enumerate(TILES):
            for which in range(3):
                act.wait_ge(kv_turned, n + 1)
                if n:
                    act.wait_ge(kv_out, 16 * n)
                w = 128 if which == 2 else 512
                dst = vN[:, tt] if which == 1 and tt < 2 else stage[:]
                run(dst[0:nt, 0:w], bank[6][0:nt, 0:w], ACT.Copy).then_inc(kv_staged, 1)
                n += 1
        with act.Fori(0, 2) as i:
            for u in range(8):
                r = 5 + u
                act.wait_ge(gemm_done, U_IQ + u + 1 + 8 * i)
                act.wait_ge(rope_done, 4 + u + 8 * i)
                run(raw[r % 2][:], bank[(U_IQ + u) % 4][:, 0:T], ACT.Copy).then_inc(gemm_evac, 1)
        for b in range(NB):
            act.wait_ge(ik_turned, b + 1)
            if b >= 2:
                act.wait_ge(sl_done, b - 1)
            run(IKB[b % 2][:, 0:PAST], bank[4][:, 0:256], ACT.Copy).then_inc(ikb_done, 1)
            if b == 0:
                act.wait_ge(rope_done, 21)
            run(IQB[b % 2][:].rearrange("p (h t) -> p h t", h=HQ), S1[:, :, TP + NT * b:TP + NT * (b + 1)], ACT.Copy)\
                .then_inc(ikb_done, 1)
            run(IKB[b % 2][:, PAST:LS], ikT[:, TP + NT * b:TP + NT * (b + 1)], ACT.Copy).then_inc(ikb_done, 1)
            act.wait_ge(sl_done, b + 1)
            if b >= 2:
                act.wait_ge(ssc_mm, b - 1)
            run(RL[b % 2][:], bank[5][0:64, 0:LS], ACT.Relu).then_inc(sl_relu, 1)
        with act.Fori(0, 2) as i:
            for u in range(8):
                r = 21 + u
                act.wait_ge(gemm_done, U_Q + u + 1 + 8 * i)
                act.wait_ge(rope_done, 20 + u + 8 * i)
                run(sq[r % 2][:], bank[(U_Q + u) % 4][:, 0:T], ACT.Square)
                run(raw[r % 2][:], bank[(U_Q + u) % 4][:, 0:T], ACT.Copy, scale=VEC[:, 96:97]).then_inc(gemm_evac, 1)
                act.wait_ge(rot_done, 25 + u + 1 + 8 * i)
                run(qks[r % 2][:], bank[6 + r % 2][:, 0:T], ACT.Sqrt, bias=eps, scale=1.0 / 128).then_inc(qk_std, 1)
        with act.Fori(0, 4) as g:
            act.wait_ge(ao_done, 2 * g)
            run(VG[:], vN[:, :, bass.ds(128 * g, 128)], ACT.Copy).then_inc(ag_ready, 1)
            for tt in range(2):
                S = 128 * (tt + 1)
                act.wait_ge(al_shift, 2 * g + tt + 1)
                run(E4[:, :, 0:S], E4[:, :, 0:S], ACT.Exp, scale=ATT_SCALE).then_inc(al_exp, 1)
                for sb in range(tt + 1):
                    act.wait_ge(pt_turned, 3 * g + tt + sb + 1)
                    act.wait_ge(ao_done, 2 * g + tt)
                    run(PT[:, sb], bank[6][:].rearrange("p (a t) -> p a t", a=4), ACT.Copy).then_inc(pt_copied, 1)
        for b in range(NB):
            for n in range(2):
                act.wait_ge(sk_turned, 2 * b + n + 1)
                if b:
                    act.wait_ge(sal_done, b)
                elif n == 0:
                    act.wait_ge(ao_copied, 8)
                run(KTB[:, :, 128 * n:128 * (n + 1)], bank[4 + n][:].rearrange("p (g s) -> p g s", g=4), ACT.Copy)\
                    .then_inc(sk_copied, 1)
            run(KTB[:, :, PAST:LS], kTt[:, :, TP + NT * b:TP + NT * (b + 1)], ACT.Copy).then_inc(sk_copied, 1)
            act.wait_ge(sal_max, b + 1)
            run(EN[:], bank[6][:, 0:LS], ACT.Exp, bias=sb1[:], scale=ATT_SCALE, accum_out=sb2[:]).then_inc(sal_exp, 1)
            act.wait_ge(sp_turned, b + 1)
            if b:
                act.wait_ge(so_done, b)
            run(VNB[:], bank[5][0:NT, :], ACT.Copy)
            run(PTN[:], bank[7][0:NT, 256:384], ACT.Copy)
            run(PTB[:], bank[7][:, 0:256].rearrange("p (n r) -> p n r", n=2), ACT.Copy).then_inc(sp_copied, 1)
        act.wait_ge(ao_copied, 8)
        act.wait_ge(so_copied, NB)
        for u in range(8):
            act.wait_ge(gemm_done, U_P + u + 1)
            b_ = bank[(U_P + u) % 4]
            run(PA[:, u, NPRE:PADP], b_[:, 0:TP], ACT.Copy)
            run(PNEW[:, u], b_[:, TP:T], ACT.Copy)
            run(PA[:, u, PADP:PADT].rearrange("p (b s) -> p b s", b=NB)[:, :, NPRE:PADS],
                b_[:, TP:T].rearrange("p (b t) -> p b t", b=NB), ACT.Copy).then_inc(gemm_evac, 1)
        for n in range(2):
            act.wait_ge(st_turned, n + 1)
            for a in range(4):
                last = run(PA[:, 4 * n + a, PADP:PADT].rearrange("p (b s) -> p b s", b=NB)[:, :, 0:NPRE],
                           bank[4 + n][:, 120 * a:120 * (a + 1)].rearrange("p (b s) -> p b s", b=NB), ACT.Copy)
            last.then_inc(st_copied, 1)
        act.wait_ge(ps_turned, 1)
        run(PST[0:NPRE, 0:512], bank[6][0:NPRE, :], ACT.Copy)
        run(PST[0:NPRE, 512:1024], bank[7][0:NPRE, :], ACT.Copy).then_inc(ps_staged, 1)
        act.wait_ge(ps_turned, 2)
        act.wait_ge(ps_out, 16 * (NB + 1))
        run(PST[0:TS, 0:512], bank[4][0:TS, :], ACT.Copy)
        run(PST[0:TS, 512:1024], bank[5][0:TS, :], ACT.Copy).then_inc(ps_staged, 1)
        act.wait_ge(pooled_done, 1)
        for u in range(16):
            evac(U_POOL + u, S3[:, u], bank[(U_POOL + u) % 4][:, 0:T], scale=VEC[:, 130 + u:131 + u])
        with act.Fori(0, 2) as i:
            for u in range(8):
                act.wait_ge(gemm_done, U_GB + u + 1 + 8 * i)
                act.wait_ge(sig_used, 8 * i + max(u - 1, 0))
                run(SG[u % 2][:], bank[(U_GB + u) % 4][:, 0:T], ACT.Sigmoid).then_inc(gemm_evac, 1)
        with act.Fori(0, 2) as i:
            for u in range(8):
                act.wait_ge(gemm_done, U_GA + u + 1 + 8 * i)
                run(S2[:, bass.ds(8 * i + u, 1)].rearrange("p a t -> p (a t)"), bank[(U_GA + u) % 4][:, 0:T], ACT.Sigmoid).then_inc(gemm_evac, 1)
        norm_squares(1)
        with act.Fori(0, 2) as i:
            for u in range(8):
                act.wait_ge(gemm_done, U_PQ + u + 1 + 8 * i)
                run(S1[:, bass.ds(8 * i + u, 1)].rearrange("p a t -> p (a t)"), bank[(U_PQ + u) % 4][:, 0:T], ACT.Copy).then_inc(gemm_evac, 1)
        act.wait_ge(keys_turned, 1)
        for n in range(4):
            last = run(KEYT[:, 4 * n:4 * n + 4], bank[4 + n][:].rearrange("p (a k) -> p a k", a=4), ACT.Copy)
        last.then_inc(keys_copied, 1)
        for tt, (t0, nt) in enumerate(TILES):
            act.wait_ge(psc_done, tt + 1)
            act.wait_ge(psel_done, tt)
            for n in range(4):
                last = run(SS[0:nt, 4 * n:4 * n + 4], bank[4 + n][0:nt].rearrange("p (a k) -> p a k", a=4), ACT.Copy)
            last.then_inc(psc_copied, 1)
            act.wait_ge(pex_done, 2 * tt + 1)
            run(wv[0:nt], wv[0:nt], ACT.Exp).then_inc(pex_done, 1)
            act.wait_ge(sl_turned, tt + 1)
            run(IB[:, t0:t0 + nt], bank[0][:, 0:nt], ACT.Copy).then_inc(slot_copied, 1)
            run(JB[:, t0:t0 + nt], bank[1][:, 0:nt], ACT.Copy).then_inc(slot_copied, 1)
            run(GF[:, t0:t0 + nt], bank[2][:, 0:nt], ACT.Copy).then_inc(slot_copied, 1)
        act.wait_ge(slots_done, 5)
        run(gt[0][:, 0:1], eps, ACT.Copy).then_inc(gh_copied, 1)
        for half in range(2):
            nb0 = BATCHES * half
            if half:
                act.wait_ge(aj_done, 64)
            with act.Fori(0, BATCHES // 2) as i:
                for par in range(2):
                    act.wait_ge(oh_used, nb0 + 2 * i + par + 2)
                    run(GH[:, :, bass.ds(16 * i + 8 * par, 8)].rearrange("p j t -> p t j"),
                        bank[par][:].rearrange("p (t j) -> p t j", t=8), ACT.Copy).then_inc(gh_copied, 1)
            with act.Fori(0, GROUPS) as i:
                n0 = 64 * half + 4 * i

                def evac_u(jj):
                    act.wait_ge(u_turned, n0 + jj + 1)
                    act.wait_ge(s_done, n0 + max(jj - 1, 0))
                    run(UT[jj % 2][:, 0:4], bank[0][:].rearrange("p (k i) -> p k i", k=4), ACT.Copy)
                    run(UT[jj % 2][:, 4:8], bank[1][:].rearrange("p (k i) -> p k i", k=4), ACT.Copy).then_inc(ut_act, 1)

                def gelu(jj):
                    act.wait_ge(s_done, n0 + jj + 1)
                    act.wait_ge(aj_done, n0 + max(jj - 1, 0))
                    run(gt[jj % 2][:], bank[4 + jj % 2][:, 0:T], ACT.Gelu).then_inc(gelu_done, 1)

                evac_u(0)
                evac_u(1)
                gelu(0)
                evac_u(2)
                gelu(1)
                evac_u(3)
                gelu(2)
                gelu(3)
        for tt, (t0, nt) in enumerate(TILES):
            act.wait_ge(y_turned, tt + 1)
            if tt == 2:
                act.wait_ge(y_out[0], 16)
            for n in range(2):
                last = run(YS[tt % 2][0:nt, 512 * n:512 * (n + 1)], bank[n][0:nt, :], ACT.Copy)
            last.then_inc(y_act, 1)

    @block.vector
    def _(dve):
        v = nc.vector
        ch = Chain(dve, dve_ch)

        def b3(ap, shape):
            return ap.broadcast_to(shape)

        def inverse_root(s_, var_ps, inv_n, va, y, t):
            ch(v.tensor_scalar(va, var_ps, inv_n, EPS, ALU.mult, ALU.add))
            ch(v.reciprocal(y, s_))
            ch(v.tensor_tensor(t, y, y, ALU.mult))
            ch(v.tensor_tensor(t, t, va, ALU.mult))
            ch(v.tensor_scalar(t, t, -0.5, 1.5, ALU.mult, ALU.add))
            ch(v.tensor_tensor(y, y, t, ALU.mult))

        dve.wait_ge(c_silu, 1)
        v.tensor_tensor(CSIL[:], CT_[:], bank[7][:, 0:NC * KT].rearrange("p (k c) -> p k c", c=NC), ALU.mult).then_inc(c_silu, 1)
        dve.wait_ge(v_copied, 1)
        for half in range(2):
            dve.wait_ge(mod_turned, half + 1)
            v.tensor_tensor(MOD[:, 48 * half:48 * (half + 1)], bank[4 + half][:, 0:48 * NC].rearrange("p (f c) -> p f c", c=NC),
                            b3(VEC[:, 48 * half:48 * (half + 1)].unsqueeze(2), [P, 48, NC]), ALU.add).then_inc(mod_done, 1)
        dve.wait_ge(mod_done, 2)

        def norm(n):
            m0 = 48 * n
            ch(v.tensor_scalar(AM[:], MOD[:, m0 + 16:m0 + 32], 1.0, None, ALU.add))
            ch(v.tensor_tensor(AM[:], AM[:], b3(VEC[:, 98 + 16 * n:114 + 16 * n].unsqueeze(2), [P, KT, NC]), ALU.mult))
            dve.wait_ge(std_done, n + 1)
            inverse_root(n_s[:], bank[6][:, 0:T], 1.0 / D, n_v[:], n_y[:], n_t[:])
            ch(v.tensor_tensor(H[:], X[:], b3(n_y[:].unsqueeze(1), [P, KT, T]), ALU.mult))
            hp = H[:, :, 0:TP]
            hs = H[:, :, TP:T].rearrange("p k (b t) -> p k b t", b=NB)
            for op, w in ((ALU.mult, AM[:]), (ALU.add, MOD[:, m0:m0 + 16])):
                ch(v.tensor_tensor(hp, hp, b3(w[:, :, 0:1], [P, KT, TP]), op))
                last = v.tensor_tensor(hs, hs, b3(w[:, :, 1:NC].unsqueeze(3), [P, KT, NB, NT]), op)
                if op == ALU.mult:
                    ch(last)
            last.then_inc(norm_done, 1)

        norm(0)
        dve.wait_ge(mix_in, 16)
        cos, sin = mix[:, M_COS:M_COS + T], mix[:, M_SIN:M_SIN + T]

        def rotate(par, out, done):
            ch(v.tensor_tensor(ra[:], raw[par][:], cos, ALU.mult))
            ch(v.tensor_tensor(rb_[:], bank[4 + par][:, 0:T], sin, ALU.mult))
            last = v.tensor_tensor(out, ra[:], rb_[:], ALU.add)
            if done:
                last.then_inc(rope_done, 1)
            else:
                ch(last)

        def rotate_normed(par, out):
            inverse_root(qks[par][:], bank[6 + par][:, 0:T], 1.0 / 128, rv[:], ry[:], rt[:])
            rotate(par, ra[:], False)
            v.tensor_tensor(out, ra[:], ry[:], ALU.mult).then_inc(rope_done, 1)

        dve.wait_ge(rot_done, 1)
        rotate(0, ikT[:], True)
        for u in range(4):
            dve.wait_ge(qk_std, u + 1)
            dve.wait_ge(rope_done, u + 1)
            rotate_normed((1 + u) % 2, kTt[:, u])
        ch(v.memset(WZ[:], 0.0))
        dve.wait_ge(wz_mm, 1)
        v.tensor_tensor(WZ[:].rearrange("p (b c) -> p b c", b=NB)[:, :, 0:NT],
                        bank[7][0:64, 0:TS].rearrange("p (b t) -> p b t", b=NB),
                        b3(mix[0:64, M_DT:M_DT + NT].unsqueeze(1), [64, NB, NT]), ALU.mult).then_inc(wz_done, 2)
        with ch.loop(2, 16) as i:
            for u in range(8):
                dve.wait_ge(rot_done, 10 + u + 8 * i)
                dve.wait_ge(rope_done, 5 + u + 8 * i)
                rotate((5 + u) % 2, S1[:, bass.ds(8 * i + u, 1)].rearrange("p a t -> p (a t)"), True)
        dve.wait_ge(rope_done, 21)
        dve.wait_ge(ssc_mm, NB)
        ch(v.tensor_tensor(SSC[:], bank[6][0:TS, 0:LS], mix[0:TS, M_SMASK:M_SMASK + LS], ALU.add))
        for n in range(-(-KSEL_S // 8)):
            left = KSEL_S - 8 * n
            ch(v.max(smx[:], SSC[:]))
            if left < 8:
                ch(v.memset(smx[:, left:8], TAKEN))
            ch(v.match_replace(SSC[:], smx[:], SSC[:], TAKEN))
        ch(v.tensor_scalar(SSC[:], SSC[:], -2e38, NEG, ALU.is_gt, ALU.mult))
        ch(v.tensor_tensor(smb[:], SSC[:], mix[0:TS, M_SMASK:M_SMASK + LS], ALU.add))
        for tt in range(2):
            if tt:
                ch(v.memset(MB[:, 1, 0:128], 0.0))
            ch(v.tensor_copy(MB[:, tt, 128 * tt:128 * (tt + 1)], mix[:, M_TRI:M_TRI + P]))
        ch(v.memset(MB[:, 0, 128:256], NEG))
        with ch.loop(4, 6) as i:
            dve.wait_ge(il_done, 2 * i)
            v.tensor_copy(QG[:], S1[:, bass.ds(4 * i, 4)]).then_inc(qg_ready, 1)
            for tt in range(2):
                dve.wait_ge(il_done, 2 * i + tt + 1)
                for n in range(2):
                    ch(v.scalar_tensor_tensor(out=E4[:, 2 * n:2 * n + 2], in0=bank[4 + n][:].rearrange("p (a s) -> p a s", a=2),
                                              scalar=0.0, in1=b3(iwN[:, tt, bass.ds(4 * i + 2 * n, 2)].unsqueeze(2), [P, 2, TP]),
                                              op0=ALU.max, op1=ALU.mult))
                ch(v.tensor_reduce(rsc[:], E4[:].rearrange("p a s -> p s a"), AX.X, ALU.add))
                v.tensor_tensor(MB[:, tt], MB[:, tt], rsc[:], ALU.add).then_inc(il_used, 1)
        dve.wait_ge(il_used, 8)
        for n in range(KSEL_P // 8):
            for tt in range(2):
                ch(v.max(mx8[:, tt], MB[:, tt]))
                ch(v.match_replace(MB[:, tt], mx8[:, tt], MB[:, tt], TAKEN))
        ch(v.tensor_scalar(MB[:], MB[:], -2e38, NEG, ALU.is_gt, ALU.mult))
        for tt in range(2):
            ch(v.tensor_tensor(MB[:, tt, 128 * tt:128 * (tt + 1)], MB[:, tt, 128 * tt:128 * (tt + 1)],
                               mix[:, M_TRI:M_TRI + P], ALU.add))
        with ch.loop(2, 9 * 8) as i:
            for u in range(8):
                par = (21 + u) % 2
                dve.wait_ge(qk_std, 4 + u + 1 + 8 * i)
                dve.wait_ge(rope_done, 21 + u + 8 * i)
                rotate_normed(par, S2[:, bass.ds(8 * i + u, 1)].rearrange("p a t -> p (a t)"))
        dve.wait_ge(rope_done, ROPES)
        with ch.loop(4, 8) as g:
            dve.wait_ge(al_done, 2 * g)
            v.tensor_copy(QG[:], S2[:, bass.ds(4 * g, 4)]).then_inc(ag_ready, 1)
            for tt in range(2):
                S = 128 * (tt + 1)
                dve.wait_ge(al_done, 2 * g + tt + 1)
                dve.wait_ge(pt_turned, 3 * g + tt)
                for n in range(2):
                    last = v.tensor_tensor(E4[:, 2 * n:2 * n + 2, 0:S],
                                           bank[4 + n][:].rearrange("p (a s) -> p a s", a=2)[:, :, 0:S],
                                           b3(MB[:, tt:tt + 1, 0:S], [P, 2, S]), ALU.add)
                    if n == 0:
                        ch(last)
                last.then_inc(al_used, 1)
                dve.wait_ge(al_used, 2 * g + tt + 1)
                ch(v.tensor_reduce(st1[:], E4[:, :, 0:S], AX.X, ALU.max))
                v.tensor_tensor(E4[:, :, 0:S], E4[:, :, 0:S], b3(st1[:].unsqueeze(2), [P, GR, S]), ALU.subtract).then_inc(al_shift, 1)
                dve.wait_ge(al_exp, 2 * g + tt + 1)
                ch(v.tensor_reduce(st2[:], E4[:, :, 0:S], AX.X, ALU.add))
                ch(v.reciprocal(st2[:], st2[:]))
                v.tensor_tensor(E4[:, :, 0:S], E4[:, :, 0:S], b3(st2[:].unsqueeze(2), [P, GR, S]), ALU.mult).then_inc(al_prob, 1)
                dve.wait_ge(ao_done, 2 * g + tt + 1)
                v.tensor_copy(S1[:, bass.ds(4 * g, 4), 128 * tt:128 * (tt + 1)],
                              bank[7][:].rearrange("p (a t) -> p a t", a=4)).then_inc(ao_copied, 1)
        dve.wait_ge(ao_copied, 8)
        for n in range(2):
            ch(v.memset(QSB[n][:], 0.0))
        for b in range(NB):
            if b >= 2:
                dve.wait_ge(sal_done, b - 1)
            v.tensor_copy(QSB[b % 2][:, :, 0:16].rearrange("p g (h t) -> p g h t", h=4),
                          S2[:, :, TP + NT * b:TP + NT * (b + 1)].rearrange("p (g h) t -> p g h t", g=4)).then_inc(sq_ready, 1)
            dve.wait_ge(sal_done, b + 1)
            ch(v.tensor_reduce(sb2[:], bank[6][:, 0:LS], AX.X, ALU.max))
            v.tensor_scalar(sb1[:], sb2[:], -ATT_SCALE, None, ALU.mult).then_inc(sal_max, 1)
            dve.wait_ge(sal_exp, b + 1)
            ch(v.reciprocal(sb1[:], sb2[:]))
            v.tensor_scalar(EN[:], EN[:], sb1[:], None, ALU.mult).then_inc(sal_prob, 1)
            dve.wait_ge(so_done, b + 1)
            v.tensor_copy(S1[:, :, TP + NT * b:TP + NT * (b + 1)],
                          bank[4][:, 0:64].rearrange("p (h t) -> p h t", h=16)).then_inc(so_copied, 1)
        ch(v.memset(PA[:, :, 0:NPRE], 0.0))
        dve.wait_ge(st_copied, 2)
        dve.wait_ge(gemm_evac, U_P + 8)
        for n, (dst, src) in enumerate(((PB, PA), (PC, PB), (PB, PC), (PC, PB))):
            sh = 1 << n
            c0 = 2 * n
            ch(v.tensor_tensor(dst[:, c0:CT, 2 * sh - 1:PADT], src[:, c0:CT, 2 * sh - 1:PADT],
                               src[:, c0:CT, sh - 1:PADT - sh], ALU.add))
            cs = slice(c0, c0 + 2)
            w = POOL_W[n]
            o_p = POOLED[:, cs, 0:TP]
            ch(v.tensor_scalar(o_p[:, :, 16:TP], dst[:, cs, NPRE + 16:PADP], 1.0 / w, None, ALU.mult))
            ch(v.tensor_tensor(o_p[:, :, 0:16], dst[:, cs, NPRE:NPRE + 16],
                               b3(mix[:, M_CNT + 16 * n:M_CNT + 16 * (n + 1)].unsqueeze(1), [P, 2, 16]), ALU.mult))
            ch(v.tensor_tensor(o_p, o_p, PA[:, cs, NPRE:PADP], ALU.subtract))
            for c in range(c0, c0 + 2):
                d_s = dst[:, c, PADP:PADT].rearrange("p (b s) -> p b s", b=NB)[:, :, NPRE:PADS]
                a_s = PA[:, c, PADP:PADT].rearrange("p (b s) -> p b s", b=NB)[:, :, NPRE:PADS]
                last = v.scalar_tensor_tensor(out=POOLED[:, c, TP:T].rearrange("p (b t) -> p b t", b=NB), in0=d_s,
                                              scalar=1.0 / w, in1=a_s, op0=ALU.mult, op1=ALU.subtract)
                if (n, c) != (3, 7):
                    ch(last)
        last.then_inc(pooled_done, 1)
        with ch.loop(2, 0) as i:
            for u in range(8):
                dve.wait_ge(gemm_evac, U_GB + u + 1 + 8 * i)
                s3u = S3[:, bass.ds(8 * i + u, 1)].rearrange("p a t -> p (a t)")
                v.tensor_tensor(s3u, s3u, SG[u % 2][:], ALU.mult).then_inc(sig_used, 1)
        dve.wait_ge(sig_used, 16)
        with ch.loop(2, 8) as i:
            for u in range(8):
                dve.wait_ge(gemm_done, U_PROJ + u + 1 + 8 * i)
                dve.wait_ge(gemm_evac, U_PROJ + u + 8 * i)
                s3u = S3[:, bass.ds(8 * i + u, 1)].rearrange("p a t -> p (a t)")
                ch(v.tensor_tensor(SG[u % 2][:], bank[(U_PROJ + u) % 4][:, 0:T],
                                   S2[:, bass.ds(8 * i + u, 1)].rearrange("p a t -> p (a t)"), ALU.mult))
                v.tensor_tensor(s3u, s3u, SG[u % 2][:], ALU.add).then_inc(gemm_evac, 1)
        with ch.loop(2, 16) as i:
            for u in range(8):
                f = 32 + u
                dve.wait_ge(gemm_done, U_OUT + u + 1 + 8 * i)
                xu = X[:, bass.ds(8 * i + u, 1)].rearrange("p a t -> p (a t)")
                ch(v.scalar_tensor_tensor(out=xu[:, 0:TP], in0=bank[(U_OUT + u) % 4][:, 0:TP],
                                          scalar=MOD[:, bass.ds(8 * i + f, 1), 0:1].rearrange("p a b -> p (a b)"),
                                          in1=xu[:, 0:TP], op0=ALU.mult, op1=ALU.add))
                ch(v.tensor_tensor(og[:].rearrange("p (b t) -> p b t", b=NB),
                                   bank[(U_OUT + u) % 4][:, TP:T].rearrange("p (b t) -> p b t", b=NB),
                                   b3(MOD[:, bass.ds(8 * i + f, 1), 1:NC].rearrange("p a b -> p (a b)").unsqueeze(2), [P, NB, NT]), ALU.mult))
                v.tensor_tensor(xu[:, TP:T], xu[:, TP:T], og[:], ALU.add).then_inc(gemm_evac, 1)
        norm(1)

        for tt, (t0, nt) in enumerate(TILES):
            dve.wait_ge(psc_copied, tt + 1)
            if tt:
                dve.wait_ge(sl_turned, tt)
            s_ = slice(0, nt)
            for a in range(16):
                for r in range(2):
                    k8 = slice(8 * r, 8 * r + 8)
                    ch(v.max(pv[s_, a, k8], SS[s_, a]))
                    ch(v.max_index(pi[s_, a, k8], pv[s_, a, k8], SS[s_, a]))
                    if r == 0:
                        ch(v.match_replace(SS[s_, a], pv[s_, a, k8], SS[s_, a], TAKEN))
            last = v.tensor_copy(pif[s_], pi[s_])
            ch(last)
            halves = pv[s_].rearrange("t (h q) k -> t h q k", q=2)
            ch(v.tensor_tensor(CAND[s_].rearrange("t h (a b) -> t h a b", a=PK),
                               b3(halves[:, :, 0].unsqueeze(3), [nt, PH, PK, PK]),
                               b3(halves[:, :, 1].unsqueeze(2), [nt, PH, PK, PK]), ALU.add))
            for h in range(PH):
                for r in range(2):
                    k8 = slice(8 * r, 8 * r + 8)
                    ch(v.max(wv[s_, h, k8], CAND[s_, h]))
                    ch(v.max_index(wi[s_, h, k8], wv[s_, h, k8], CAND[s_, h]))
                    if r == 0:
                        ch(v.match_replace(CAND[s_, h], wv[s_, h, k8], CAND[s_, h], TAKEN))
            ch(v.tensor_copy(s8[s_], wv[s_, :, 0]))
            v.tensor_tensor(wv[s_], wv[s_], b3(s8[s_].unsqueeze(2), [nt, PH, PK]), ALU.subtract).then_inc(pex_done, 1)
            ch(v.tensor_scalar(wa[s_], wi[s_], 4, None, ALU.logical_shift_right))
            ch(v.tensor_copy(waf[s_], wa[s_]))
            ch(v.tensor_scalar(wa[s_], wi[s_], 15, None, ALU.bitwise_and))
            ch(v.tensor_copy(wbf[s_], wa[s_]))
            idx = pif[s_].rearrange("t (h q) k -> t h q k", q=2)
            for q, (wf, out) in enumerate(((waf, ei), (wbf, ej))):
                ch(v.tensor_tensor(EQ[s_], b3(wf[s_].rearrange("t h k -> t (h k)").unsqueeze(2), [nt, PH * PK, PK]),
                                   b3(iota[s_, 0:PK].unsqueeze(1), [nt, PH * PK, PK]), ALU.is_equal))
                e4 = EQ[s_].rearrange("t (h k) a -> t h k a", h=PH)
                ch(v.tensor_tensor(e4, e4, b3(idx[:, :, q].unsqueeze(2), [nt, PH, PK, PK]), ALU.mult))
                last = v.tensor_reduce(out[s_], EQ[s_], AX.X, ALU.add)
                if q == 0:
                    ch(last)
            last.then_inc(psel_done, 1)
            dve.wait_ge(psel_done, tt + 1)
            dve.wait_ge(pex_done, 2 * tt + 2)
            ch(v.tensor_reduce(s8[s_], wv[s_], AX.X, ALU.add))
            ch(v.reciprocal(s8[s_], s8[s_]))
            v.tensor_tensor(wv[s_], wv[s_], b3(s8[s_].unsqueeze(2), [nt, PH, PK]), ALU.mult).then_inc(pw_done, 1)
        dve.wait_ge(slot_copied, 9)
        v.tensor_copy(GP[0][:], GF[:]).then_inc(slots_done, 1)
        dve.wait_ge(slots_done, 1)
        v.tensor_tensor(GRr[:], GF[:], GP[0][:], ALU.subtract).then_inc(slots_done, 1)
        dve.wait_ge(slots_done, 2)
        v.tensor_copy(GP[1][:], GRr[:]).then_inc(slots_done, 1)
        dve.wait_ge(slots_done, 3)
        v.tensor_tensor(GRr[:], GRr[:], GP[1][:], ALU.subtract).then_inc(slots_done, 1)
        dve.wait_ge(slots_done, 4)
        v.tensor_copy(GP[2][:], GRr[:]).then_inc(slots_done, 1)
        dve.wait_ge(slots_done, 5)

        for half in range(2):
            nb0 = BATCHES * half
            if half:
                dve.wait_ge(s_done, 64)
            ch(v.tensor_copy(iob[:], iota))
            with ch.loop(BATCHES // 2, 8) as i:
                for par in range(2):
                    dve.wait_ge(oh_used, nb0 + 2 * i + par)
                    at = bass.ds(16 * i + 8 * par, 8)
                    ch(v.tensor_tensor(OA[par][:], b3(iob[:].unsqueeze(1), [P, 8, P]),
                                       b3(IB[:, at].unsqueeze(2), [P, 8, P]), ALU.is_equal))
                    ch(v.tensor_tensor(OQ[:], b3(iob[:, 64 * half:64 * half + 64].unsqueeze(1), [P, 8, 64]),
                                       b3(JB[:, at].unsqueeze(2), [P, 8, 64]), ALU.is_equal))
                    for k in range(3):
                        last = v.tensor_tensor(OBp[par][k][:], OQ[:], b3(GP[k][:, at].unsqueeze(2), [P, 8, 64]), ALU.mult)
                        if k < 2:
                            ch(last)
                    last.then_inc(oh_ready, 1)
            dve.wait_ge(gh_copied, nb0 + BATCHES + 1)
            with ch.loop(GROUPS, 2 * KT) as i:
                n0 = 64 * half + 4 * i
                g0 = GROUPS * half + i

                def evac_u(jj):
                    dve.wait_ge(u_turned, n0 + jj + 1)
                    dve.wait_ge(s_done, n0 + max(jj - 1, 0))
                    v.tensor_copy(UT[jj % 2][:, 8:12], bank[2][:].rearrange("p (k i) -> p k i", k=4))
                    v.tensor_copy(UT[jj % 2][:, 12:16], bank[3][:].rearrange("p (k i) -> p k i", k=4)).then_inc(ut_dve, 1)

                def weigh(jj):
                    dve.wait_ge(gelu_done, n0 + jj + 1)
                    if jj == 0:
                        dve.wait_ge(o_done, 16 * g0)
                    v.tensor_tensor(AJ[jj][:], gt[jj % 2][:], GH[:, bass.ds(4 * i + jj, 1)].rearrange("p a t -> p (a t)"),
                                    ALU.mult).then_inc(aj_done, 1)

                evac_u(0)
                evac_u(1)
                weigh(0)
                evac_u(2)
                weigh(1)
                evac_u(3)
                weigh(2)
                weigh(3)
                dve.wait_ge(o_added, 16 * g0)
                for m_ in range(KT):
                    dve.wait_ge(o_done, 16 * g0 + m_ + 1)
                    o = bank[6 + m_ % 2]
                    ch(v.scalar_tensor_tensor(out=X[:, m_, 0:TP], in0=o[:, 0:TP], scalar=MOD[:, 80 + m_, 0:1],
                                              in1=X[:, m_, 0:TP], op0=ALU.mult, op1=ALU.add))
                    ch(v.tensor_tensor(n_x[:, 0:TS].rearrange("p (b t) -> p b t", b=NB),
                                       o[:, TP:T].rearrange("p (b t) -> p b t", b=NB),
                                       b3(MOD[:, 80 + m_, 1:NC].unsqueeze(2), [P, NB, NT]), ALU.mult))
                    v.tensor_tensor(X[:, m_, TP:T], X[:, m_, TP:T], n_x[:, 0:TS], ALU.add).then_inc(o_added, 1)
        for tt, (t0, nt) in enumerate(TILES):
            dve.wait_ge(y_turned, tt + 1)
            if tt == 2:
                dve.wait_ge(y_out[0], 16)
            for n in range(2, 4):
                last = v.tensor_copy(YS[tt % 2][0:nt, 512 * n:512 * (n + 1)], bank[n][0:nt, :])
            last.then_inc(y_dve, 1)

    ctx.close()


_INS = ['x_prompt', 'x_sample', 'cache_k', 'cache_v', 'cache_idx_k', 'state_pool', 'page_table', 'c_prompt', 'c_sample',
        'norm1_g', 'norm2_g', 'w_mod', 'b_mod', 'w_in', 'q_norm_g', 'k_norm_g', 'w_attn_proj', 'w_pool', 'pool_scale',
        'w_out', 'w_peer_q', 'peer_keys', 'peer_u', 'peer_v']
_OUTS = [(1, 256, 2048), (8, 4, 2048), (1, 256, 4, 128), (1, 256, 4, 128), (1, 256, 128), (1, 15, 1024),
         (8, 4, 4, 128), (8, 4, 4, 128), (8, 4, 128), (8, 15, 1024)]


def kernel(**inputs):
    import concourse.bacc as _bacc
    from concourse.bass_utils import run_bass_kernel_spmd as _run

    nc = _bacc.Bacc("TRN2", target_bir_lowering=False, num_devices=1)
    arrays, args = {}, []
    for name in _INS:
        a = np.ascontiguousarray(inputs[name])
        arrays[f"in_{name}"] = a
        args.append(nc.dram_tensor(f"in_{name}", a.shape, mybir.dt.from_np(a.dtype), kind="ExternalInput").ap())
    for name, a in zip(("keep", "mix"), constants()):
        arrays[f"in_{name}"] = a
        args.append(nc.dram_tensor(f"in_{name}", a.shape, F32, kind="ExternalInput").ap())
    for i, shape in enumerate(_OUTS):
        args.append(nc.dram_tensor(f"out_{i}", shape, F32, kind="ExternalOutput").ap())
    layer_kernel(nc, *args)
    r = _run(nc, [arrays], core_ids=[0])
    return tuple(r.results[0][f"out_{i}"] for i in range(len(_OUTS)))
```

```python
import math
from contextlib import ExitStack, contextmanager

import numpy as np

import concourse.bass as bass
from concourse import mybir

F32 = mybir.dt.float32
BF16 = mybir.dt.bfloat16
F32R = mybir.dt.float32r
I32 = mybir.dt.int32
U32 = mybir.dt.uint32
ALU = mybir.AluOpType
ACT = mybir.ActivationFunctionType
AX = mybir.AxisListType

P = 128
D = 2048
KT = D // P
TP = 256
NB, NT = 8, 4
TS = NB * NT
T = TP + TS
TILES = [(0, 128), (128, 128), (256, 32)]
HQ, HK, GR = 16, 4, 4
PAST = 256
LS = PAST + NT
KSEL_P, KSEL_S = TP // 4, LS // 4
NC = 1 + NB
POOL_W = (2, 4, 8, 16)
NPRE = 15
CT = 8
PADP = NPRE + TP
PADS = NPRE + NT
PADT = PADP + NB * PADS
NE = 128
PH, PK = 8, 16
EPS = 1e-6
GTOK = 72
NEG = -1e30
TAKEN = -3e38
ATT_SCALE = 128 ** -0.5
IW_SCALE = 16 ** -0.5 * 128 ** -0.5
C_Q, C_K, C_V, C_IQ, C_IK, C_P = 0, 2048, 2560, 3072, 5120, 5264
C_GA, C_GB = 6288, 8336

U_MOD, U_IK, U_K, U_V, U_IQ, U_Q, U_P, U_POOL, U_GB, U_GA, U_PROJ, U_OUT, U_PQ = (
    0, 48, 50, 54, 58, 74, 90, 98, 114, 130, 146, 162, 178)
K_MOD, K_IK, K_K, K_V, K_IQ, K_Q, K_P, K_POOL, K_GB, K_GA, K_PROJ, K_OUT, K_PQ = (
    0, 48, 49, 51, 53, 61, 69, 73, 74, 90, 106, 122, 138)


def units_done(chunk):
    if chunk < K_IK:
        return chunk + 1
    if chunk < K_POOL:
        return U_IK + 2 * (chunk - K_IK + 1)
    if chunk == K_POOL:
        return U_GB
    return U_GB + chunk - K_GB + 1


class Chain:

    def __init__(self, eng, sem):
        self.eng, self.sem, self.n, self.base = eng, sem, 0, 0

    def __call__(self, ins):
        ins.then_inc(self.sem, 1)
        self.n += 1
        self.eng.wait_ge(self.sem, self.n + self.base)

    @contextmanager
    def loop(self, count, per):
        start = self.n
        with self.eng.Fori(0, count) as i:
            self.base = i * per if per else 0
            yield i
            assert self.n - start == per, (self.n - start, per)
            self.base = 0
        self.n = start + per * count


def constants():
    f = np.float32
    keep = np.zeros((P, 388), f)
    keep[:, 0:128] = np.eye(P)
    keep[:, 128:256] = 1.0
    keep[:, 256:384] = np.arange(P)[None]
    keep[:, 384] = EPS
    pos = np.concatenate([np.arange(TP), np.tile(PAST + np.arange(NT), NB)]).astype(f)
    half = 64
    freqs = (f(10000.0) ** (-np.arange(half, dtype=f) / f(half))).astype(f)
    ang = (pos[None, :] * freqs[:, None]).astype(f)
    mix = np.zeros((P, MIX), f)
    for k in range(half):
        mix[k + half, M_ROT + k] = -1.0
        mix[k, M_ROT + k + half] = 1.0
    mix[:, M_COS:M_COS + T] = np.concatenate([np.cos(ang)] * 2)
    mix[:, M_SIN:M_SIN + T] = np.concatenate([np.sin(ang)] * 2)
    for g, w in enumerate(POOL_W):
        mix[:, M_CNT + 16 * g:M_CNT + 16 * (g + 1)] = 1.0 / np.minimum(np.arange(16) + 1, w)
    mix[:, M_TRI:M_TRI + P] = np.where(np.arange(P)[None] > np.arange(P)[:, None], NEG, 0.0)
    q = np.arange(TS)
    s = np.arange(LS)
    mix[0:TS, M_SMASK:M_SMASK + LS] = np.where(s[None] > PAST + (q % NT)[:, None], NEG, 0.0)
    r = np.arange(P)
    for b in range(NB):
        hit = (q[:, None] == NT * b + (r % NT)[None]) & ((r % 32) < 16)[None]
        mix[0:TS, M_REP + P * b:M_REP + P * (b + 1)] = hit
    for h in range(16):
        mix[h, M_E16 + NT * h:M_E16 + NT * (h + 1)] = 1.0
    for k in range(64):
        mix[k, M_DT + k % NT] = 1.0
    return keep, mix


M_ROT, M_COS, M_SIN, M_CNT, M_TRI, M_SMASK, M_REP, M_E16, M_DT = (
    0, 128, 416, 704, 768, 896, 1156, 2180, 2244)
MIX = 2248


def layer_kernel(nc, x_p, x_s, cache_k, cache_v, cache_ik, state, ptab, c_p, c_s, norm1_g, norm2_g,
                 w_mod, b_mod, w_in, q_g, k_g, w_proj, w_pool, pool_scale, w_out, w_pq, pkeys,
                 peer_u, peer_v, keep_d, mix_d,
                 y_p, y_s, k_p, v_p, ik_p, ps_p, k_s, v_s, ik_s, ps_s):
    PAGES = ptab.shape[0] * ptab.shape[1]
    NPOOL = cache_k.shape[0]

    class Map:
        def __init__(self, at):
            self.at = at

        def __call__(self, name, shape, dt=F32):
            n = int(np.prod(shape[1:])) * (2 if dt == BF16 else 4)
            n = -(-n // 32) * 32
            t = nc.alloc_sbuf_tensor_at(name, list(shape), dt, offset=self.at)
            self.at += n
            return t

        def skip(self, n):
            at = self.at
            self.at += n
            return Map(at)

    top = Map(16896)
    keep = top("keep", [P, 388])
    ident, ones, iota = keep[:, 0:128], keep[:, 128:256], keep[:, 256:384]
    eps = keep[:, 384:385]
    X = top("X", [P, KT, T])
    h_at = top.at
    H = top("H", [P, KT, T])
    MOD = top("MOD", [P, 6 * KT, NC])
    AM = top("AM", [P, KT, NC])
    VEC = top("VEC", [P, 146])
    pages = top("pages", [1, 64], I32)
    n_x = top("n_x", [P, TS])
    norm_at = top.at
    n_s, n_v, n_y, n_t = (top(f"n_{c}", [P, T]) for c in "svyt")
    top.at = norm_at + 4 * 1152
    free_at = top.at
    mix = top("mix", [P, MIX])
    s_at = top.at
    S1 = top("S1", [P, KT, T])
    s2_at = top.at
    S2 = top("S2", [P, KT, T])
    s3_at = top.at
    S3 = top("S3", [P, KT, T])
    ring_at = top.at
    ring = [top(f"ring{n}", [P, KT, 256]) for n in range(4)]
    RAW = [Map(ring_at + 16384 * n)(f"RAW{n}", [P, KT, P]) for n in range(4)]
    WL = [Map(ring_at + 16384 * n)(f"WL{n}", [P, KT, P], F32R) for n in range(4)]
    WH = [Map(ring_at + 16384 * n + 8192)(f"WH{n}", [P, KT, P], F32R) for n in range(4)]
    kv_at = top.at
    kTt = top("kTt", [P, HK, T])
    vTt = top("vTt", [P, HK, T])
    ikT = top("ikT", [P, T])
    iwT = top("iwT", [16, T])
    vN = top("vN", [P, 2, 512])
    tmp_at = top.at
    END = 229368
    assert END - tmp_at >= 17424, END - tmp_at

    m = Map(h_at)
    XTOK = [m("xtok0", [P, D]), m("xtok1", [P, D])]
    m = Map(tmp_at)
    XTOK.append(m("xtok2", [P, D]))
    VA, VB, CT_ = m("VA", [98, P]), m("VB", [48, P]), m("CT_", [P, KT, NC])
    CSIL = m("CSIL", [P, KT, NC])
    CTOK = Map(kv_at)("CTOK", [NC, D])
    MROW = Map(s_at)("MROW", [NC, 6 * D])

    m = Map(tmp_at)
    raw = [m(f"raw{n}", [P, T]) for n in range(2)]
    sq = [m(f"sq{n}", [P, T]) for n in range(2)]
    qks = [m(f"qks{n}", [P, T]) for n in range(2)]
    ra, rb_ = m("ra", [P, T]), m("rb_", [P, T])
    rv, ry, rt = m("rv", [P, T]), m("ry", [P, T]), m("rt", [P, T])
    stage = m("stage", [P, 512])
    iwN = m("iwN", [P, 2, 16])
    m = Map(tmp_at)
    kpg = [m(f"kpg{n}", [P, 2, 512]) for n in range(2)]
    vpg = [m(f"vpg{n}", [P, 2, 512]) for n in range(2)]
    smb = m("smb", [TS, LS])

    m = Map(s3_at)
    MB = m("MB", [P, 2, TP])
    QG = m("QG", [P, GR, T])
    VG = m("VG", [P, 2, P])
    E4 = m("E4", [P, GR, TP])
    PT = m("PT", [P, 2, GR, P])
    st1, st2 = m("st1", [P, GR]), m("st2", [P, GR])
    mx8 = m("mx8", [P, 2, 8])
    rsc = m("rsc", [P, TP])
    IPG = Map(s3_at + 2048 + 4608 + 1024)("IPG", [P, 2 * NB, P])
    m = Map(s2_at)
    IKB = [m(f"IKB{n}", [P, LS]) for n in range(2)]
    IQB = [m(f"IQB{n}", [P, 64]) for n in range(2)]
    RL = [m(f"RL{n}", [64, LS]) for n in range(2)]
    WZ = m("WZ", [64, 288])
    SSC = m("SSC", [TS, LS])
    smx = m("smx", [TS, 8])
    m = Map(s3_at + 2048)
    KTB = m("KTB", [P, HK, LS])
    QSB = [m(f"QSB{n}", [P, HK, 32]) for n in range(2)]
    EN = m("EN", [P, LS])
    PTB = m("PTB", [P, 2, P])
    PTN = m("PTN", [NT, P])
    VNB = m("VNB", [NT, 512])
    sb1, sb2 = m("sb1", [P, 1]), m("sb2", [P, 1])
    assert m.at <= s3_at + 18432

    PA = Map(s2_at)("PA", [P, CT, PADT])
    PB = Map(tmp_at)("PB", [P, CT, PADT])
    PC = Map(s3_at)("PC", [P, CT, PADT])
    POOLED = Map(kv_at)("POOLED", [P, CT, T])
    STT = Map(kv_at)("STT", [NB * NPRE, CT * P])
    PNEW = Map(kv_at + 9216)("PNEW", [P, CT, TS])
    PST = Map(kv_at + 10240)("PST", [P, CT * P])
    m = Map(kv_at)
    INH = m("INH", [P, KT, T], F32R)
    AOL = Map(s_at)("AOL", [P, KT, T], F32R)
    MGH = Map(h_at)("MGH", [P, KT, T], F32R)
    MGL = Map(s3_at)("MGL", [P, KT, T], F32R)
    m.at = max(m.at, tmp_at)
    SG = [m(f"SG{n}", [P, T]) for n in range(2)]
    og = m("og", [P, TS])

    m = Map(s2_at)
    KEYT = m("KEYT", [P, 16, P])
    SS = m("SS", [P, 16, NE])
    m = Map(tmp_at)
    KNAT = m("KNAT", [P, 16, P])
    EQ = Map(s3_at + 18432)("EQ", [P, PH * PK, PK])
    m = Map(kv_at)
    CAND = m("CAND", [P, PH, PK * PK])
    pv = m("pv", [P, 16, PK])
    pi = m("pi", [P, 16, PK], U32)
    pif = m("pif", [P, 16, PK])
    wv = m("wv", [P, PH, PK])
    wi = m("wi", [P, PH, PK], U32)
    wa = m("wa", [P, PH, PK], U32)
    waf = m("waf", [P, PH, PK])
    wbf = m("wbf", [P, PH, PK])
    ei = m("ei", [P, PH * PK])
    ej = m("ej", [P, PH * PK])
    s8 = m("s8", [P, PH])
    slots_at = END - 5 * 576 - 40
    slots_at -= slots_at % 32
    m = Map(slots_at)
    IB, JB = m("IB", [P, T], BF16), m("JB", [P, T], BF16)
    GP = [m(f"GP{n}", [P, T], BF16) for n in range(3)]
    GF = Map(norm_at)("GF", [P, T])
    GRr = Map(norm_at + 1152)("GRr", [P, T])
    assert tmp_at + 8192 <= slots_at

    HL = Map(h_at)("HL", [P, KT, T], F32R)
    HH = Map(s3_at)("HH", [P, KT, T], F32R)
    high_at = s3_at + 18432
    m = Map(high_at)
    GCH = [m(f"GCH{n}", [P, NE, GTOK]) for n in range(2)]
    OA = [m(f"OA{n}", [P, 2, P, 2], BF16) for n in range(2)]
    OQ = [m(f"OQ{n}", [P, 2, NE, 2], BF16) for n in range(2)]
    OBp = [[m(f"OBp{n}_{k}", [P, 2, NE, 2], BF16) for k in range(3)] for n in range(2)]
    iob = m("iob", [P, P, 2], BF16)
    assert m.at <= slots_at
    m = Map(free_at)
    UB = [m(f"UB{n}", [P, D]) for n in range(4)]
    GH = m("GH", [P, 4, T])
    gt = [m(f"gt{n}", [P, T]) for n in range(2)]
    XS = m("XS", [P, KT, TS])
    assert m.at <= s3_at, (m.at, s3_at)
    m = Map(high_at)
    v_at = m.at
    VRAW = [[m(f"VRAW{h}_{n}", [P, D // 2]) for n in range(4)] for h in range(2)]
    m.at = v_at
    VL = [[m(f"VL{h}_{n}", [P, D // 2], F32R) for n in range(4)] for h in range(2)]
    VH = [[m(f"VH{h}_{n}", [P, D // 2], F32R) for n in range(4)] for h in range(2)]
    UTH = [m(f"UTH{n}", [P, 4, P], F32R) for n in range(4)]
    UTL = [m(f"UTL{n}", [P, 4, P], F32R) for n in range(4)]
    AH = [m(f"AH{n}", [P, T], F32R) for n in range(4)]
    AL = [m(f"AL{n}", [P, T], F32R) for n in range(4)]
    af = [m(f"af{n}", [P, T]) for n in range(2)]
    assert m.at <= END, (m.at, END)
    YS = [Map(free_at + 8192 * n)(f"YS{n}", [P, D]) for n in range(2)]

    g_dram = nc.dram_tensor("expert_weights", [P, NE, T], F32, kind="Internal").ap()

    ctx = ExitStack()
    bank = [ctx.enter_context(nc.psum_tensor(f"bank{n}", [P, 512], F32)) for n in range(8)]

    def sem(name):
        return ctx.enter_context(nc.semaphore(name))

    keep_in, mix_in, x_in, c_in, vec_in = (sem(n) for n in ("keep_in", "mix_in", "x_in", "c_in", "vec_in"))
    pages_in = sem("pages_in")
    wload = [sem(f"wload{n}") for n in range(4)]
    gemm_done, gemm_evac = sem("gemm_done"), sem("gemm_evac")
    x_turned, x_copied = sem("x_turned"), sem("x_copied")
    v_turned, v_copied = sem("v_turned"), sem("v_copied")
    c_turned, c_silu = sem("c_turned"), sem("c_silu")
    mod_turned, mod_done = sem("mod_turned"), sem("mod_done")
    sq_done, ssq_done, std_done, norm_done = sem("sq_done"), sem("ssq_done"), sem("std_done"), sem("norm_done")
    rot_done, qk_std, rope_done = sem("rot_done"), sem("qk_std"), sem("rope_done")
    iw_turned, iw_done = sem("iw_turned"), sem("iw_done")
    wz_mm, wz_done = sem("wz_mm"), sem("wz_done")
    ipg_in, ik_turned, ikb_done = sem("ipg_in"), sem("ik_turned"), sem("ikb_done")
    sl_done, sl_relu, ssc_mm = sem("sl_done"), sem("sl_relu"), sem("ssc_mm")
    smb_done, smb_ch = sem("smb_done"), sem("smb_ch")
    qg_ready, il_done, il_used = sem("qg_ready"), sem("il_done"), sem("il_used")
    mb_done = sem("mb_done")
    ag_ready, al_done, al_used, al_shift, al_exp, al_prob = (
        sem(n) for n in ("ag_ready", "al_done", "al_used", "al_shift", "al_exp", "al_prob"))
    pt_turned, pt_copied, ao_done, ao_copied = (sem(n) for n in ("pt_turned", "pt_copied", "ao_done", "ao_copied"))
    kv_turned, kv_staged = sem("kv_turned"), sem("kv_staged")
    kv_out = sem("kv_out")
    kvp_in = [sem(f"kvp_in{n}") for n in range(2)]
    sk_turned, sk_copied, sq_ready = sem("sk_turned"), sem("sk_copied"), sem("sq_ready")
    sal_done, sal_max, sal_exp, sal_prob = (sem(n) for n in ("sal_done", "sal_max", "sal_exp", "sal_prob"))
    sp_turned, sp_copied, so_done, so_copied = (sem(n) for n in ("sp_turned", "sp_copied", "so_done", "so_copied"))
    zero_done = sem("zero_done")
    st_in, st_turned, st_copied = sem("st_in"), sem("st_turned"), sem("st_copied")
    ps_turned, ps_staged, ps_out = sem("ps_turned"), sem("ps_staged"), sem("ps_out")
    pooled_done = sem("pooled_done")
    sig_done, sig_used = sem("sig_done"), sem("sig_used")
    keys_in, keys_turned, keys_copied = sem("keys_in"), sem("keys_turned"), sem("keys_copied")
    psc_done, psc_copied, psel_done, pex_done, pw_done = (
        sem(n) for n in ("psc_done", "psc_copied", "psel_done", "pex_done", "pw_done"))
    sl_turned, slot_copied, slots_done = sem("sl_turned"), sem("slot_copied"), sem("slots_done")
    oh_ready, oh_used, gh_copied = sem("oh_ready"), sem("oh_used"), sem("gh_copied")
    u_in = [sem(f"u_in{n}") for n in range(4)]
    vv_in = [[sem(f"vv_in{h}_{n}") for n in range(4)] for h in range(2)]
    g_out = [sem(f"g_out{n}") for n in range(2)]
    g_in, v_hi, v_lo = sem("g_in"), sem("v_hi"), sem("v_lo")
    in_hi, in_lo = sem("in_hi"), sem("in_lo")
    w_hi, w_lo = sem("w_hi"), sem("w_lo")
    u_turned, ut_hi, ut_lo = sem("u_turned"), sem("ut_hi"), sem("ut_lo")
    s_blk, gelu_done, aj_done = sem("s_blk"), sem("gelu_done"), sem("aj_done")
    o_done, o_added, xs_done = sem("o_done"), sem("o_added"), sem("xs_done")
    y_turned, y_act, y_dve = sem("y_turned"), sem("y_act"), sem("y_dve")
    y_out = [sem(f"y_out{n}") for n in range(2)]
    dve_ch, act_ch, pool_ch = sem("dve_ch"), sem("act_ch"), sem("pool_ch")

    w_in_v = w_in.rearrange("(k p) c -> p k c", p=P)
    w_mod_v = w_mod.rearrange("(k p) c -> p k c", p=P)
    w_proj_v = w_proj.rearrange("(k p) c -> p k c", p=P)
    w_out_v = w_out.rearrange("(k p) c -> p k c", p=P)
    w_pq_v = w_pq.rearrange("(k p) c -> p k c", p=P)
    u_v = peer_u.rearrange("(i j) d -> j i d", j=NE)
    v_v = peer_v.rearrange("(i j) d -> j i d", j=NE)

    GROUPS = NE // 4
    GCHUNKS = T // GTOK
    GITERS = GTOK // 8
    ROPES = 37

    block = ctx.enter_context(nc.Block())

    @block.sync
    def _(sp):
        for u in range(4):
            sp.dma_start(ring[u][:], w_mod_v[:, :, 256 * u:256 * (u + 1)]).then_inc(wload[u], 16)
        with sp.Fori(1, 12) as i:
            for u in range(4):
                sp.wait_ge(gemm_done, 4 * i + u - 3)
                sp.dma_start(ring[u][:], w_mod_v[:, :, bass.ds((4 * i + u) * 256, 256)]).then_inc(wload[u], 16)

        def chunk(n, src):
            sp.wait_ge(gemm_done, units_done(n - 4))
            w = src.shape[2]
            sp.dma_start(ring[n % 4][:, 0:src.shape[1], 0:w], src).then_inc(wload[n % 4], 16)

        def cols(first, col, count, src=w_in_v):
            for c in range(count):
                chunk(first + c, src[:, :, col + 256 * c:col + 256 * (c + 1)])

        chunk(K_IK, w_in_v[:, :, C_IK:C_IK + 144])
        cols(K_K, C_K, 2)
        cols(K_V, C_V, 2)
        cols(K_IQ, C_IQ, 8)
        cols(K_Q, C_Q, 8)
        cols(K_P, C_P, 4)
        sp.wait_ge(gemm_done, units_done(K_POOL - 4))
        slot = ring[K_POOL % 4][:].rearrange("p k c -> p (k c)").rearrange("p (g c) -> p g c", g=8)
        sp.dma_start(slot, w_pool.rearrange("g (k p) c -> p (g k) c", p=P)).then_inc(wload[K_POOL % 4], 16)

        for u in range(4):
            sp.wait_ge(gemm_done, units_done(K_GB + u - 4))
            sp.dma_start(RAW[(K_GB + u) % 4][:], w_in_v[:, :, C_GB + 128 * u:C_GB + 128 * (u + 1)])\
                .then_inc(wload[(K_GB + u) % 4], 16)
        for first, src, col in ((K_GB, w_in_v, C_GB), (K_GA, w_in_v, C_GA), (K_PROJ, w_proj_v, 0), (K_OUT, w_out_v, 0),
                                (K_PQ, w_pq_v, 0)):
            with sp.Fori(1 if first == K_GB else 0, 4) as i:
                for u in range(4):
                    c = first + u
                    if first == K_GB:
                        sp.wait_ge(gemm_done, U_GB + u + 1 - 4 + 4 * i)
                    else:
                        sp.wait_ge(gemm_done, units_done(c - 4) + 4 * i)
                    sp.dma_start(RAW[c % 4][:], src[:, :, bass.ds(4 * 128 * i + col + 128 * u, 128)])\
                        .then_inc(wload[c % 4], 16)
        sp.wait_ge(gemm_evac, U_OUT + 16)
        sp.dma_start(KNAT[:], pkeys.rearrange("h p k c -> k (h p) c")).then_inc(keys_in, 16)
        sp.wait_ge(slots_done, 5)
        sp.wait_ge(gemm_done, U_PQ + 16)

        def values(h, jj, tile):
            sp.dma_start(VRAW[h][jj][:], v_v[bass.ds(tile, 1), :, h * D // 2:(h + 1) * D // 2]
                         .rearrange("a i d -> (a i) d")).then_inc(vv_in[h][jj], 16)

        for jj in range(4):
            sp.dma_start(UB[jj][:], u_v[jj]).then_inc(u_in[jj], 16)
        for c in range(GCHUNKS):
            sp.wait_ge(gh_copied, 2 + 2 * GITERS * (c + 1))
            sp.dma_start(g_dram[:, :, GTOK * c:GTOK * (c + 1)], GCH[c % 2][:]).then_inc(g_out[c % 2], 16)
        for n in range(2):
            sp.wait_ge(g_out[n], 16 * GCHUNKS // 2)
        sp.dma_start(GH[:], g_dram[:, 0:4]).then_inc(g_in, 16)
        for h in range(2):
            for jj in range(4):
                values(h, jj, jj)
        with sp.Fori(1, GROUPS) as i:
            for jj in range(4):
                sp.wait_ge(u_turned, 16 * i + 4 * jj - 12 + 1)
                sp.dma_start(UB[jj][:], u_v[bass.ds(4 * i + jj, 1)].rearrange("a i d -> (a i) d")).then_inc(u_in[jj], 16)
            sp.wait_ge(aj_done, 4 * i + 1)
            sp.dma_start(GH[:], g_dram[:, bass.ds(4 * i, 4)]).then_inc(g_in, 16)
            for h in range(2):
                sp.wait_ge(o_done, 16 * i - 8 + 8 * h + 1)
                for jj in range(4):
                    values(h, jj, 4 * i + jj)

    @block.gpsimd
    def _(pool):
        pool.dma_start(keep[:], keep_d).then_inc(keep_in, 16)
        pool.dma_start(XTOK[0][:], x_p[0, 0:128]).then_inc(x_in, 16)
        pool.dma_start(XTOK[1][:], x_p[0, 128:256]).then_inc(x_in, 16)
        pool.dma_start(XTOK[2][0:TS], x_s.rearrange("b t d -> (b t) d")).then_inc(x_in, 16)
        pool.dma_start(CTOK[0:1], c_p).then_inc(c_in, 16)
        pool.dma_start(CTOK[1:NC], c_s).then_inc(c_in, 16)
        pool.dma_start(VA[0:96], b_mod.rearrange("(a b) -> a b", b=P)).then_inc(vec_in, 16)
        pool.dma_start(VA[96:97], q_g.rearrange("(a b) -> a b", b=P)).then_inc(vec_in, 16)
        pool.dma_start(VA[97:98], k_g.rearrange("(a b) -> a b", b=P)).then_inc(vec_in, 16)
        for n, v in enumerate((norm1_g, norm2_g, pool_scale)):
            pool.dma_start(VB[16 * n:16 * (n + 1)], v.rearrange("(a b) -> a b", b=P)).then_inc(vec_in, 16)
        pool.dma_start(mix[:], mix_d).then_inc(mix_in, 16)
        pool.dma_start(pages[:, 0:PAGES], ptab.rearrange("b n -> (b n)").rearrange("(a n) -> a n", a=1)).then_inc(pages_in, 16)
        pool.wait_ge(pages_in, 16)
        pool.wait_ge(mod_done, 2)
        page = []
        for n in range(PAGES):
            page.append(pool.value_load(pages[0:1, n:n + 1], min_val=0, max_val=NPOOL - 1))
            pool.dma_start(IPG[:, n], cache_ik[bass.ds(page[n], 1)].rearrange("a s d -> (a s) d")).then_inc(ipg_in, 16)
        n = 0
        for tt, (t0, nt) in enumerate(TILES):
            for which in range(3):
                n += 1
                pool.wait_ge(kv_staged, n)
                src = vN[:, tt] if which == 1 and tt < 2 else stage[:]
                if tt < 2:
                    dst = ((k_p, v_p)[which][0, t0:t0 + nt].rearrange("s h d -> s (h d)") if which < 2
                           else ik_p[0, t0:t0 + nt])
                else:
                    dst = ((k_s, v_s)[which].rearrange("b t h d -> (b t) (h d)") if which < 2
                           else ik_s.rearrange("b t d -> (b t) d"))
                pool.dma_start(dst, src[0:nt, 0:dst.shape[1]]).then_inc(kv_out, 16)
        pool.wait_ge(kv_out, 16 * 9)
        pool.wait_ge(rope_done, ROPES)
        for b in range(NB):
            if b >= 2:
                pool.wait_ge(so_done, b - 1)
            for n in range(2):
                at = bass.ds(page[2 * b + n], 1)
                pool.dma_start(kpg[b % 2][:, n], cache_k[at].rearrange("a s h d -> (a s) (h d)")).then_inc(kvp_in[b % 2], 16)
                pool.dma_start(vpg[b % 2][:, n], cache_v[at].rearrange("a s h d -> (a s) (h d)")).then_inc(kvp_in[b % 2], 16)
        pool.wait_ge(so_copied, NB)
        pool.dma_start(STT[0:NB * NPRE], state.rearrange("b s c -> (b s) c")).then_inc(st_in, 16)
        for b in range(NB):
            pool.dma_start(ps_s[b, 0:NPRE - NT], state[b, NT:NPRE]).then_inc(ps_out, 16)
        pool.wait_ge(ps_staged, 1)
        pool.dma_start(ps_p[0], PST[0:NPRE]).then_inc(ps_out, 16)
        pool.wait_ge(ps_out, 16 * (NB + 1))
        pool.wait_ge(ps_staged, 2)
        for b in range(NB):
            pool.dma_start(ps_s[b, NPRE - NT:NPRE], PST[NT * b:NT * (b + 1)]).then_inc(ps_out, 16)
        pool.wait_ge(ps_out, 16 * (2 * NB + 1))
        with pool.Fori(0, 20) as i:
            for u in range(4):
                n = (K_GB + u) % 4
                pool.wait_ge(w_hi, 4 * i + u + 1)
                pool.tensor_tensor(WL[n][:], RAW[n][:], WH[n][:].bitcast(F32), ALU.subtract).then_inc(w_lo, 1)
        with pool.Fori(0, GROUPS) as i:
            for h in range(2):
                for jj in range(4):
                    pool.wait_ge(v_hi, 8 * i + 4 * h + jj + 1)
                    pool.tensor_tensor(VL[h][jj][:], VRAW[h][jj][:], VH[h][jj][:].bitcast(F32), ALU.subtract)\
                        .then_inc(v_lo, 1)
        for tt, (t0, nt) in enumerate(TILES):
            pool.wait_ge(y_act, tt + 1)
            pool.wait_ge(y_dve, tt + 1)
            dst = y_p[0, t0:t0 + nt] if tt < 2 else y_s.rearrange("b t d -> (b t) d")
            pool.dma_start(dst, YS[tt % 2][0:nt]).then_inc(y_out[tt % 2], 16)
        pool.wait_ge(y_out[0], 32)
        pool.wait_ge(y_out[1], 16)

    @block.tensor
    def _(pe):
        mm, turn = nc.tensor.matmul, nc.tensor.transpose
        for s_, n in ((il_done, 1), (al_done, 1), (pt_turned, 1), (ao_done, 1), (oh_used, 2), (u_turned, 1), (s_blk, 1),
                      (o_done, 1)):
            pe.sem_inc(s_, n)

        def product(unit, out, lhs, rhs, steps):
            for k in range(steps):
                last = mm(out, lhs(k), rhs(k), start=(k == 0), stop=(k == steps - 1))
            return last

        def gemm(unit0, chunk0, u, i, rhs):
            if u % 2 == 0:
                c = chunk0 + u // 2
                pe.wait_ge(wload[c % 4], 16 * (c // 4 + 1) + 16 * i)
            pe.wait_ge(gemm_evac, unit0 + u - 3 + 8 * i)
            slot = ring[(chunk0 + u // 2) % 4]
            c0 = 128 * (u % 2)
            product(u, bank[(unit0 + u) % 4][:, 0:T], lambda k: slot[:, k, c0:c0 + 128],
                    lambda k: rhs[:, k], KT).then_inc(gemm_done, 1)

        pe.wait_ge(keep_in, 16)
        pe.wait_ge(x_in, 48)
        n = 0
        for tt, (t0, nt) in enumerate(TILES):
            for q in range(4):
                if n >= 2:
                    pe.wait_ge(x_copied, n - 1)
                for a in range(4):
                    last = turn(bank[4 + n % 2][:].rearrange("p (a t) -> p a t", a=4)[:, a, 0:nt],
                                XTOK[tt][0:nt, 128 * (4 * q + a):128 * (4 * q + a + 1)], ident[0:nt, 0:nt])
                last.then_inc(x_turned, 1)
                n += 1
        pe.wait_ge(vec_in, 96)
        turn(bank[6][:, 0:98], VA[0:98], ident[0:98, 0:98])
        turn(bank[6][:, 98:146], VB[0:48], ident[0:48, 0:48]).then_inc(v_turned, 1)
        pe.wait_ge(c_in, 32)
        for k in range(KT):
            last = turn(bank[7][:, NC * k:NC * (k + 1)], CTOK[0:NC, 128 * k:128 * (k + 1)], ident[0:NC, 0:NC])
        last.then_inc(c_turned, 1)

        pe.wait_ge(c_silu, 2)
        for u in range(4):
            pe.wait_ge(wload[u], 16)
            product(u, bank[u][0:NC, 0:256], lambda k: CSIL[:, k], lambda k: ring[u][:, k], KT).then_inc(gemm_done, 1)
        with pe.Fori(1, 12) as i:
            for u in range(4):
                pe.wait_ge(wload[u], 16 * i + 16)
                pe.wait_ge(gemm_evac, 4 * i + u - 3)
                product(u, bank[u][0:NC, 0:256], lambda k: CSIL[:, k], lambda k: ring[u][:, k], KT).then_inc(gemm_done, 1)
        pe.wait_ge(gemm_evac, 48)
        for half in range(2):
            for f in range(48):
                last = turn(bank[4 + half][:, NC * f:NC * (f + 1)],
                            MROW[0:NC, 128 * (48 * half + f):128 * (48 * half + f + 1)], ident[0:NC, 0:NC])
            last.then_inc(mod_turned, 1)

        def norm_sum(n):
            pe.wait_ge(sq_done, n + 1)
            product(0, bank[6][:, 0:T], lambda k: ones, lambda k: H[:, k], KT).then_inc(ssq_done, 1)

        norm_sum(0)
        pe.wait_ge(norm_done, 1)
        pe.wait_ge(mix_in, 16)

        def rotary(r, unit, normed, off=0):
            pe.wait_ge(gemm_evac, unit + 1)
            mm(bank[4 + r % 2][:, 0:T], mix[:, M_ROT:M_ROT + 128], raw[r % 2][:], start=True, stop=True)\
                .then_inc(rot_done, 1)
            if normed:
                mm(bank[6 + r % 2][:, 0:T], ones, sq[r % 2][:], start=True, stop=True).then_inc(rot_done, 1)

        c = K_IK
        pe.wait_ge(wload[c % 4], 16 * (c // 4 + 1))
        pe.wait_ge(gemm_evac, U_IK - 3)
        product(0, bank[U_IK % 4][:, 0:T], lambda k: ring[c % 4][:, k, 0:128], lambda k: H[:, k], KT).then_inc(gemm_done, 1)
        product(0, bank[(U_IK + 1) % 4][0:16, 0:T], lambda k: ring[c % 4][:, k, 128:144], lambda k: H[:, k], KT)\
            .then_inc(gemm_done, 1)
        rotary(0, U_IK, False)
        for u in range(4):
            gemm(U_K, K_K, u, 0, H)
            rotary(1 + u, U_K + u, True)
        for u in range(4):
            gemm(U_V, K_V, u, 0, H)
        pe.wait_ge(gemm_evac, U_IK + 2)
        pe.wait_ge(rope_done, 5)
        for tt in range(2):
            last = turn(bank[7][:, 16 * tt:16 * (tt + 1)], iwT[0:16, 128 * tt:128 * (tt + 1)], ident[0:16, 0:16])
        last.then_inc(iw_turned, 1)
        pe.wait_ge(iw_done, 1)
        mm(bank[7][0:64, 0:TS], mix[0:16, M_E16:M_E16 + 64], iwT[0:16, TP:T], start=True, stop=True).then_inc(wz_mm, 1)
        n = 0
        for tt, (t0, nt) in enumerate(TILES):
            for which in range(3):
                if n == 0:
                    pe.wait_ge(rope_done, 5)
                    pe.wait_ge(gemm_evac, U_V + 4)
                if n >= 1:
                    pe.wait_ge(kv_staged, n)
                for g in range(1 if which == 2 else 4):
                    src = (kTt[:, g], vTt[:, g], ikT[:])[which]
                    last = turn(bank[6][0:nt, 128 * g:128 * (g + 1)], src[:, t0:t0 + nt], ident)
                last.then_inc(kv_turned, 1)
                n += 1
        pe.wait_ge(wz_done, 2)
        pe.wait_ge(kv_staged, 9)

        with pe.Fori(0, 2) as i:
            for u in range(8):
                gemm(U_IQ, K_IQ, u, i, H)
                pe.wait_ge(gemm_evac, U_IQ + u + 1 + 8 * i)
                pe.wait_ge(rope_done, 4 + u + 8 * i)
                mm(bank[4 + (5 + u) % 2][:, 0:T], mix[:, M_ROT:M_ROT + 128], raw[(5 + u) % 2][:], start=True, stop=True)\
                    .then_inc(rot_done, 1)
        pe.wait_ge(rope_done, 21)

        for b in range(NB):
            if b == 0:
                pe.wait_ge(ipg_in, 16 * PAGES)
            else:
                pe.wait_ge(ikb_done, 3 * b)
            for n in range(2):
                last = turn(bank[4][:, 128 * n:128 * (n + 1)], IPG[:, 2 * b + n], ident)
            last.then_inc(ik_turned, 1)
            pe.wait_ge(ikb_done, 3 * (b + 1))
            if b:
                pe.wait_ge(sl_relu, b)
            mm(bank[5][0:64, 0:LS], IQB[b % 2][:], IKB[b % 2][:], start=True, stop=True)\
                .then_inc(sl_done, 1)
            pe.wait_ge(sl_relu, b + 1)
            mm(bank[6][0:TS, 0:LS], WZ[:, 32 * b:32 * (b + 1)], RL[b % 2][:], start=(b == 0), stop=(b == NB - 1))\
                .then_inc(ssc_mm, 1)
        with pe.Fori(0, 4) as i:
            pe.wait_ge(qg_ready, i + 1)
            for tt in range(2):
                pe.wait_ge(il_used, 2 * i + tt + 1)
                for a in range(4):
                    last = mm(bank[4 + a // 2][:, 256 * (a % 2):256 * (a % 2 + 1)], QG[:, a, 128 * tt:128 * (tt + 1)],
                              ikT[:, 0:TP], start=True, stop=True)
                last.then_inc(il_done, 1)
        pe.wait_ge(il_used, 8 + 1)

        with pe.Fori(0, 2) as i:
            for u in range(8):
                gemm(U_Q, K_Q, u, i, H)
                pe.wait_ge(gemm_evac, U_Q + u + 1 + 8 * i)
                pe.wait_ge(rope_done, 20 + u + 8 * i)
                r = 21 + u
                mm(bank[4 + r % 2][:, 0:T], mix[:, M_ROT:M_ROT + 128], raw[r % 2][:], start=True, stop=True)
                mm(bank[6 + r % 2][:, 0:T], ones, sq[r % 2][:], start=True, stop=True).then_inc(rot_done, 1)
        pe.wait_ge(rope_done, ROPES)

        with pe.Fori(0, 4) as g:
            pe.wait_ge(ag_ready, 2 * g + 2)
            for tt in range(2):
                S = 128 * (tt + 1)
                pe.wait_ge(al_used, 2 * g + tt + 1)
                for a in range(4):
                    last = mm(bank[4 + a // 2][:, 256 * (a % 2):256 * (a % 2) + S], QG[:, a, 128 * tt:128 * (tt + 1)],
                              kTt[:, bass.ds(g, 1), 0:S].rearrange("p a s -> p (a s)"), start=True, stop=True)
                last.then_inc(al_done, 1)
                pe.wait_ge(al_prob, 2 * g + tt + 1)
                for sb in range(tt + 1):
                    pe.wait_ge(pt_copied, 3 * g + tt + sb + 1)
                    for a in range(4):
                        last = turn(bank[6][:, 128 * a:128 * (a + 1)], E4[:, a, 128 * sb:128 * (sb + 1)], ident)
                    last.then_inc(pt_turned, 1)
                pe.wait_ge(pt_copied, 3 * g + 2 * tt + 1 + 1)
                pe.wait_ge(ao_copied, 2 * g + tt + 1)
                for sb in range(tt + 1):
                    last = mm(bank[7][:], VG[:, sb], PT[:, sb].rearrange("p a t -> p (a t)"),
                              start=(sb == 0), stop=(sb == tt))
                last.then_inc(ao_done, 1)
        pe.wait_ge(ao_copied, 8 + 1)

        for b in range(NB):
            pe.wait_ge(kvp_in[b % 2], 64 * (b // 2 + 1))
            if b:
                pe.wait_ge(sp_copied, b)
                pe.wait_ge(so_copied, b)
            for n in range(2):
                for g in range(4):
                    last = turn(bank[4 + n][:, 128 * g:128 * (g + 1)], kpg[b % 2][:, n, 128 * g:128 * (g + 1)], ident)
                last.then_inc(sk_turned, 1)
            pe.wait_ge(sk_copied, 3 * (b + 1))
            pe.wait_ge(sq_ready, b + 1)
            mm(bank[6][:, 0:LS], mix[0:TS, M_REP + 128 * b:M_REP + 128 * (b + 1)], smb[:], start=True, stop=False,
               skip_group_check=True)
            for g in range(4):
                last = mm(bank[6][32 * g:32 * g + 32, 0:LS], QSB[b % 2][:, g], KTB[:, g], start=False, stop=True,
                          skip_group_check=True)
            last.then_inc(sal_done, 1)
            for g in range(4):
                last = turn(bank[5][0:NT, 128 * g:128 * (g + 1)], vTt[:, g, TP + NT * b:TP + NT * (b + 1)], ident)
            pe.wait_ge(sal_prob, b + 1)
            for n in range(2):
                turn(bank[7][:, 128 * n:128 * (n + 1)], EN[:, 128 * n:128 * (n + 1)], ident)
            turn(bank[7][0:NT, 256:384], EN[:, PAST:LS], ident).then_inc(sp_turned, 1)
            pe.wait_ge(sp_copied, b + 1)
            for g in range(4):
                o = bank[4][:, 16 * g:16 * (g + 1)]
                for n in range(2):
                    mm(o, vpg[b % 2][:, n, 128 * g:128 * (g + 1)], PTB[:, n, 32 * g:32 * g + 16], start=(n == 0), stop=False)
                last = mm(o, VNB[0:NT, 128 * g:128 * (g + 1)], PTN[0:NT, 32 * g:32 * g + 16], start=False, stop=True)
            last.then_inc(so_done, 1)

        for u in range(8):
            gemm(U_P, K_P, u, 0, H)
        pe.wait_ge(st_in, 16)
        for n in range(2):
            for a in range(4):
                last = turn(bank[4 + n][:, 120 * a:120 * (a + 1)], STT[0:120, 128 * (4 * n + a):128 * (4 * n + a + 1)], ident[0:120, 0:120])
            last.then_inc(st_turned, 1)
        pe.wait_ge(gemm_evac, U_P + 8)
        pe.wait_ge(st_copied, 2)
        for a in range(8):
            last = turn(bank[6 + a // 4][0:NPRE, 128 * (a % 4):128 * (a % 4 + 1)], PA[:, a, PADP - NPRE:PADP], ident)
        last.then_inc(ps_turned, 1)
        for a in range(8):
            last = turn(bank[4 + a // 4][0:TS, 128 * (a % 4):128 * (a % 4 + 1)], PNEW[:, a], ident)
        last.then_inc(ps_turned, 1)
        pe.wait_ge(pooled_done, 1)
        pe.wait_ge(wload[K_POOL % 4], 16 * (K_POOL // 4 + 1))
        slot = ring[K_POOL % 4][:].rearrange("p k c -> p (k c)").rearrange("p (g k c) -> p g k c", g=4, k=2)
        for u in range(16):
            g = u // 4
            pe.wait_ge(gemm_evac, U_POOL + u - 3)
            product(u, bank[(U_POOL + u) % 4][:, 0:T], lambda k: slot[:, g, k, 128 * (u % 4):128 * (u % 4 + 1)],
                    lambda k: POOLED[:, 2 * g + k], 2).then_inc(gemm_done, 1)

        def split_gemm(unit0, u, i, x_hi, x_lo, quarters=None):
            pe.wait_ge(w_lo, unit0 - U_GB + u + 1 + 8 * i)
            pe.wait_ge(gemm_evac, unit0 + u - 3 + 8 * i)
            n = (K_GB + unit0 - U_GB + u) % 4
            out = bank[(unit0 + u) % 4][:, 0:T]
            for k in range(KT):
                if quarters is not None and k % 4 == 0:
                    pe.wait_ge(in_lo, quarters + k // 4 + 1)
                mm(out, WH[n][:, k], x_hi[:, k], start=(k == 0), stop=False)
                mm(out, WH[n][:, k], x_lo[:, k], start=False, stop=False)
                last = mm(out, WL[n][:, k], x_hi[:, k], start=False, stop=(k == KT - 1))
            last.then_inc(gemm_done, 1)

        def split_pass(unit0, x_hi, x_lo, quarters=None):
            if quarters is not None:
                for u in range(8):
                    split_gemm(unit0, u, 0, x_hi, x_lo, quarters if u == 0 else None)
                for u in range(8, 16):
                    split_gemm(unit0, u, 0, x_hi, x_lo)
            else:
                with pe.Fori(0, 2) as i:
                    for u in range(8):
                        split_gemm(unit0, u, i, x_hi, x_lo)

        split_pass(U_GB, INH, HL, 0)
        split_pass(U_GA, INH, HL)
        split_pass(U_PROJ, INH, AOL, 4)
        pe.wait_ge(gemm_evac, U_OUT)
        split_pass(U_OUT, MGH, MGL)
        norm_sum(1)
        split_pass(U_PQ, HH, HL, 8)

        pe.wait_ge(keys_in, 16)
        for n in range(4):
            for a in range(4):
                last = turn(bank[4 + n][:, 128 * a:128 * (a + 1)], KNAT[:, 4 * n + a], ident)
        last.then_inc(keys_turned, 1)
        pe.wait_ge(gemm_evac, U_PQ + 16)
        pe.wait_ge(keys_copied, 1)
        for tt, (t0, nt) in enumerate(TILES):
            if tt:
                pe.wait_ge(slot_copied, 3 * tt)
            for a in range(16):
                last = mm(bank[4 + a // 4][0:nt, 128 * (a % 4):128 * (a % 4 + 1)], S1[:, a, t0:t0 + nt], KEYT[:, a],
                          start=True, stop=True)
            last.then_inc(psc_done, 1)
            pe.wait_ge(pw_done, tt + 1)
            for n, src in enumerate((ei, ej, wv)):
                flat = src[0:nt].rearrange("t h k -> t (h k)") if n == 2 else src[0:nt]
                last = turn(bank[n][:, 0:nt], flat, ident[0:nt, 0:nt])
            last.then_inc(sl_turned, 1)
        pe.wait_ge(slots_done, 5)
        for c in range(GCHUNKS):
            nb0 = 2 * GITERS * c
            with pe.Fori(0, GITERS) as i:
                for par in range(2):
                    pe.wait_ge(oh_ready, nb0 + 2 * i + par + 1)
                    pe.wait_ge(gh_copied, nb0 + 2 * i + par + 1)
                    out = bank[par][:].rearrange("p (t j) -> p t j", t=4)
                    for t in range(4):
                        for k in range(3):
                            last = mm(out[:, t], OA[par][:, t // 2, :, t % 2], OBp[par][k][:, t // 2, :, t % 2], start=(k == 0), stop=(k == 2))
                    last.then_inc(oh_used, 1)
        pe.wait_ge(gh_copied, 2 * GITERS * GCHUNKS + 2)

        def turn_u(i, b):
            jj, q = b // 4 % 4, b % 4
            if q == 0:
                pe.wait_ge(u_in[jj], 16 * i + 16 + 16 * (b // 16))
            pe.wait_ge(ut_lo, 16 * i + max(b - 3, 0) + 1)
            for k in range(4):
                f = 4 * q + k
                last = turn(bank[b % 4][:, 128 * k:128 * (k + 1)], UB[jj][:, 128 * f:128 * (f + 1)], ident)
            last.then_inc(u_turned, 1)

        def score(i, b):
            jj, q = b // 4, b % 4
            pe.wait_ge(ut_lo, 16 * i + b + 2)
            if q == 0:
                pe.wait_ge(gelu_done, 4 * i + max(jj - 1, 0) + 1)
            out = bank[4 + jj % 2][:, 0:T]
            for k in range(4):
                f = 4 * q + k
                for n, (w, x) in enumerate(((UTH, HH), (UTH, HL), (UTL, HH))):
                    last = mm(out, w[b % 4][:, k], x[:, f], start=(f + n == 0), stop=(f == KT - 1 and n == 2))
            last.then_inc(s_blk, 1)

        def mix_values(i):
            pe.wait_ge(aj_done, 4 * i + 5)
            for m_ in range(KT):
                if m_ % 8 == 0:
                    pe.wait_ge(v_lo, 8 * i + 4 * (m_ // 8) + 4)
                pe.wait_ge(o_added, 16 * i + max(m_ - 1, 0) + 1)
                c0 = 128 * (m_ % 8)
                out = bank[6 + m_ % 2][:, 0:T]
                for jj in range(4):
                    vh, vl = (x[m_ // 8][jj][:, c0:c0 + 128] for x in (VH, VL))
                    mm(out, vh, AH[jj][:], start=(jj == 0), stop=False)
                    mm(out, vh, AL[jj][:], start=False, stop=False)
                    last = mm(out, vl, AH[jj][:], start=False, stop=(jj == 3))
                last.then_inc(o_done, 1)

        turn_u(0, 0)
        turn_u(0, 1)
        with pe.Fori(0, GROUPS - 1) as i:
            for b in range(16):
                turn_u(i, b + 2)
                score(i, b)
            mix_values(i)
        for b in range(16):
            if b < 14:
                turn_u(GROUPS - 1, b + 2)
            score(GROUPS - 1, b)
        mix_values(GROUPS - 1)
        pe.wait_ge(o_added, 16 * GROUPS + 1)
        pe.wait_ge(xs_done, 1)
        for tt, (t0, nt) in enumerate(TILES):
            if tt:
                pe.wait_ge(y_act, tt)
                pe.wait_ge(y_dve, tt)
            for k in range(KT):
                last = turn(bank[k // 4][0:nt, 128 * (k % 4):128 * (k % 4 + 1)], X[:, k, t0:t0 + nt], ident)
            last.then_inc(y_turned, 1)

    @block.scalar
    def _(act):
        for s_, n in ((pt_copied, 1), (gh_copied, 2), (gelu_done, 1)):
            act.sem_inc(s_, n)
        run = nc.scalar.activation

        def evac(unit, out, src, func=ACT.Copy, **kw):
            act.wait_ge(gemm_done, unit + 1)
            run(out, src, func, **kw).then_inc(gemm_evac, 1)

        n = 0
        for tt, (t0, nt) in enumerate(TILES):
            for q in range(4):
                act.wait_ge(x_turned, n + 1)
                run(X[:, 4 * q:4 * q + 4, t0:t0 + nt],
                    bank[4 + n % 2][:].rearrange("p (a t) -> p a t", a=4)[:, :, 0:nt], ACT.Copy).then_inc(x_copied, 1)
                n += 1
        act.wait_ge(v_turned, 1)
        run(VEC[:], bank[6][:, 0:146], ACT.Copy).then_inc(v_copied, 1)
        act.wait_ge(c_turned, 1)
        run(CT_[:], bank[7][:, 0:NC * KT].rearrange("p (k c) -> p k c", c=NC), ACT.Sigmoid).then_inc(c_silu, 1)
        with act.Fori(0, 12) as i:
            for u in range(4):
                act.wait_ge(gemm_done, 4 * i + u + 1)
                run(MROW[0:NC, bass.ds((4 * i + u) * 256, 256)], bank[u][0:NC, 0:256], ACT.Copy).then_inc(gemm_evac, 1)

        def norm_squares(n):
            if n == 0:
                act.wait_ge(x_copied, 12)
            else:
                act.wait_ge(gemm_evac, U_OUT + 16)
                act.wait_ge(gemm_done, U_GA + 16)
            run(H[:], X[:], ACT.Square).then_inc(sq_done, 1)
            act.wait_ge(ssq_done, n + 1)
            run(n_s[:], bank[6][:, 0:T], ACT.Sqrt, bias=eps, scale=1.0 / D).then_inc(std_done, 1)

        norm_squares(0)

        def raw_unit(r, unit, g=None):
            act.wait_ge(gemm_done, unit + 1)
            if g is not None:
                run(sq[r % 2][:], bank[unit % 4][:, 0:T], ACT.Square)
                run(raw[r % 2][:], bank[unit % 4][:, 0:T], ACT.Copy, scale=g).then_inc(gemm_evac, 1)
            else:
                run(raw[r % 2][:], bank[unit % 4][:, 0:T], ACT.Copy).then_inc(gemm_evac, 1)

        raw_unit(0, U_IK)
        evac(U_IK + 1, iwT[:], bank[(U_IK + 1) % 4][0:16, 0:T], scale=IW_SCALE)
        for u in range(4):
            if u >= 1:
                act.wait_ge(rope_done, u)
            raw_unit(1 + u, U_K + u, VEC[:, 97:98])
            act.wait_ge(rot_done, 1 + 2 * (u + 1))
            run(qks[(1 + u) % 2][:], bank[6 + (1 + u) % 2][:, 0:T], ACT.Sqrt, bias=eps, scale=1.0 / 128).then_inc(qk_std, 1)
        for u in range(4):
            evac(U_V + u, vTt[:, u], bank[(U_V + u) % 4][:, 0:T])
        act.wait_ge(iw_turned, 1)
        run(iwN[:], bank[7][:, 0:32].rearrange("p (a b) -> p a b", a=2), ACT.Copy).then_inc(iw_done, 1)
        n = 0
        for tt, (t0, nt) in enumerate(TILES):
            for which in range(3):
                act.wait_ge(kv_turned, n + 1)
                if n:
                    act.wait_ge(kv_out, 16 * n)
                w = 128 if which == 2 else 512
                dst = vN[:, tt] if which == 1 and tt < 2 else stage[:]
                run(dst[0:nt, 0:w], bank[6][0:nt, 0:w], ACT.Copy).then_inc(kv_staged, 1)
                n += 1
        with act.Fori(0, 2) as i:
            for u in range(8):
                r = 5 + u
                act.wait_ge(gemm_done, U_IQ + u + 1 + 8 * i)
                act.wait_ge(rope_done, 4 + u + 8 * i)
                run(raw[r % 2][:], bank[(U_IQ + u) % 4][:, 0:T], ACT.Copy).then_inc(gemm_evac, 1)
        for b in range(NB):
            act.wait_ge(ik_turned, b + 1)
            if b >= 2:
                act.wait_ge(sl_done, b - 1)
            run(IKB[b % 2][:, 0:PAST], bank[4][:, 0:256], ACT.Copy).then_inc(ikb_done, 1)
            if b == 0:
                act.wait_ge(rope_done, 21)
            run(IQB[b % 2][:].rearrange("p (h t) -> p h t", h=HQ), S1[:, :, TP + NT * b:TP + NT * (b + 1)], ACT.Copy)\
                .then_inc(ikb_done, 1)
            run(IKB[b % 2][:, PAST:LS], ikT[:, TP + NT * b:TP + NT * (b + 1)], ACT.Copy).then_inc(ikb_done, 1)
            act.wait_ge(sl_done, b + 1)
            if b >= 2:
                act.wait_ge(ssc_mm, b - 1)
            run(RL[b % 2][:], bank[5][0:64, 0:LS], ACT.Relu).then_inc(sl_relu, 1)
        with act.Fori(0, 2) as i:
            for u in range(8):
                r = 21 + u
                act.wait_ge(gemm_done, U_Q + u + 1 + 8 * i)
                act.wait_ge(rope_done, 20 + u + 8 * i)
                run(sq[r % 2][:], bank[(U_Q + u) % 4][:, 0:T], ACT.Square)
                run(raw[r % 2][:], bank[(U_Q + u) % 4][:, 0:T], ACT.Copy, scale=VEC[:, 96:97]).then_inc(gemm_evac, 1)
                act.wait_ge(rot_done, 25 + u + 1 + 8 * i)
                run(qks[r % 2][:], bank[6 + r % 2][:, 0:T], ACT.Sqrt, bias=eps, scale=1.0 / 128).then_inc(qk_std, 1)
        with act.Fori(0, 4) as g:
            act.wait_ge(ao_done, 2 * g + 1)
            run(VG[:], vN[:, :, bass.ds(128 * g, 128)], ACT.Copy).then_inc(ag_ready, 1)
            for tt in range(2):
                S = 128 * (tt + 1)
                act.wait_ge(al_shift, 2 * g + tt + 1)
                run(E4[:, :, 0:S], E4[:, :, 0:S], ACT.Exp, scale=ATT_SCALE).then_inc(al_exp, 1)
                for sb in range(tt + 1):
                    act.wait_ge(pt_turned, 3 * g + tt + sb + 1 + 1)
                    act.wait_ge(ao_done, 2 * g + tt + 1)
                    run(PT[:, sb], bank[6][:].rearrange("p (a t) -> p a t", a=4), ACT.Copy).then_inc(pt_copied, 1)
        for b in range(NB):
            for n in range(2):
                act.wait_ge(sk_turned, 2 * b + n + 1)
                if b:
                    act.wait_ge(sal_done, b)
                elif n == 0:
                    act.wait_ge(ao_copied, 8 + 1)
                run(KTB[:, :, 128 * n:128 * (n + 1)], bank[4 + n][:].rearrange("p (g s) -> p g s", g=4), ACT.Copy)\
                    .then_inc(sk_copied, 1)
            run(KTB[:, :, PAST:LS], kTt[:, :, TP + NT * b:TP + NT * (b + 1)], ACT.Copy).then_inc(sk_copied, 1)
            act.wait_ge(sal_max, b + 1)
            run(EN[:], bank[6][:, 0:LS], ACT.Exp, bias=sb1[:], scale=ATT_SCALE, accum_out=sb2[:]).then_inc(sal_exp, 1)
            act.wait_ge(sp_turned, b + 1)
            if b:
                act.wait_ge(so_done, b)
            run(VNB[:], bank[5][0:NT, :], ACT.Copy)
            run(PTN[:], bank[7][0:NT, 256:384], ACT.Copy)
            run(PTB[:], bank[7][:, 0:256].rearrange("p (n r) -> p n r", n=2), ACT.Copy).then_inc(sp_copied, 1)
        act.wait_ge(ao_copied, 8 + 1)
        act.wait_ge(so_copied, NB)
        for u in range(8):
            act.wait_ge(gemm_done, U_P + u + 1)
            b_ = bank[(U_P + u) % 4]
            run(PA[:, u, NPRE:PADP], b_[:, 0:TP], ACT.Copy)
            run(PNEW[:, u], b_[:, TP:T], ACT.Copy)
            run(PA[:, u, PADP:PADT].rearrange("p (b s) -> p b s", b=NB)[:, :, NPRE:PADS],
                b_[:, TP:T].rearrange("p (b t) -> p b t", b=NB), ACT.Copy).then_inc(gemm_evac, 1)
        for n in range(2):
            act.wait_ge(st_turned, n + 1)
            for a in range(4):
                last = run(PA[:, 4 * n + a, PADP:PADT].rearrange("p (b s) -> p b s", b=NB)[:, :, 0:NPRE],
                           bank[4 + n][:, 120 * a:120 * (a + 1)].rearrange("p (b s) -> p b s", b=NB), ACT.Copy)
            last.then_inc(st_copied, 1)
        act.wait_ge(ps_turned, 1)
        run(PST[0:NPRE, 0:512], bank[6][0:NPRE, :], ACT.Copy)
        run(PST[0:NPRE, 512:1024], bank[7][0:NPRE, :], ACT.Copy).then_inc(ps_staged, 1)
        act.wait_ge(ps_turned, 2)
        act.wait_ge(ps_out, 16 * (NB + 1))
        run(PST[0:TS, 0:512], bank[4][0:TS, :], ACT.Copy)
        run(PST[0:TS, 512:1024], bank[5][0:TS, :], ACT.Copy).then_inc(ps_staged, 1)

        def weight_hi(n, i=0):
            c = K_GB + n
            act.wait_ge(wload[c % 4], 16 * (c // 4 + 1) + 16 * i)
            run(WH[c % 4][:], RAW[c % 4][:], ACT.Copy).then_inc(w_hi, 1)

        def input_hi(out, src):
            for q in range(4):
                run(out[:, 4 * q:4 * q + 4], src[:, 4 * q:4 * q + 4], ACT.Copy).then_inc(in_hi, 1)

        weight_hi(0)
        weight_hi(1)
        act.wait_ge(pooled_done, 1)
        for u in range(16):
            evac(U_POOL + u, S3[:, u], bank[(U_POOL + u) % 4][:, 0:T], scale=VEC[:, 130 + u:131 + u])
        act.wait_ge(ps_out, 16 * (2 * NB + 1))
        input_hi(INH, H)
        with act.Fori(0, 4) as i:
            for u in range(4):
                weight_hi(u + 2, i)
                act.wait_ge(gemm_done, U_GB + u + 1 + 4 * i)
                act.wait_ge(sig_used, 4 * i + max(u - 1, 0) + 1)
                run(SG[u % 2][:], bank[(U_GB + u) % 4][:, 0:T], ACT.Sigmoid).then_inc(gemm_evac, 1)
        with act.Fori(0, 4) as i:
            for u in range(4):
                weight_hi(16 + u + 2, i)
                act.wait_ge(gemm_done, U_GA + u + 1 + 4 * i)
                run(S2[:, bass.ds(4 * i + u, 1)].rearrange("p a t -> p (a t)"), bank[(U_GA + u) % 4][:, 0:T], ACT.Sigmoid).then_inc(gemm_evac, 1)
        input_hi(INH, S1)
        with act.Fori(0, 8) as i:
            for u in range(4):
                weight_hi(32 + u + 2, i)
        norm_squares(1)
        act.wait_ge(norm_done, 2)
        input_hi(HH, H)

        def peer_query(u, i=0):
            act.wait_ge(gemm_done, U_PQ + u + 1 + 4 * i)
            run(S1[:, bass.ds(4 * i + u, 1)].rearrange("p a t -> p (a t)"), bank[(U_PQ + u) % 4][:, 0:T], ACT.Copy).then_inc(gemm_evac, 1)

        with act.Fori(0, 3) as i:
            for u in range(4):
                weight_hi(64 + u + 2, i)
                peer_query(u, i)
        for u in range(12, 16):
            if u < 14:
                weight_hi(64 + u + 2)
            act.wait_ge(gemm_done, U_PQ + u + 1)
            run(S1[:, u], bank[(U_PQ + u) % 4][:, 0:T], ACT.Copy).then_inc(gemm_evac, 1)
        act.wait_ge(keys_turned, 1)
        for n in range(4):
            last = run(KEYT[:, 4 * n:4 * n + 4], bank[4 + n][:].rearrange("p (a k) -> p a k", a=4), ACT.Copy)
        last.then_inc(keys_copied, 1)
        for tt, (t0, nt) in enumerate(TILES):
            act.wait_ge(psc_done, tt + 1)
            act.wait_ge(psel_done, tt)
            for n in range(4):
                last = run(SS[0:nt, 4 * n:4 * n + 4], bank[4 + n][0:nt].rearrange("p (a k) -> p a k", a=4), ACT.Copy)
            last.then_inc(psc_copied, 1)
            act.wait_ge(pex_done, 2 * tt + 1)
            run(wv[0:nt], wv[0:nt], ACT.Exp).then_inc(pex_done, 1)
            act.wait_ge(sl_turned, tt + 1)
            run(IB[:, t0:t0 + nt], bank[0][:, 0:nt], ACT.Copy).then_inc(slot_copied, 1)
            run(JB[:, t0:t0 + nt], bank[1][:, 0:nt], ACT.Copy).then_inc(slot_copied, 1)
            run(GF[:, t0:t0 + nt], bank[2][:, 0:nt], ACT.Copy).then_inc(slot_copied, 1)
        act.wait_ge(slots_done, 5)
        for c in range(GCHUNKS):
            nb0 = 2 * GITERS * c
            if c >= 2:
                act.wait_ge(g_out[c % 2], 16 * (c // 2))
            with act.Fori(0, GITERS) as i:
                for par in range(2):
                    act.wait_ge(oh_used, nb0 + 2 * i + par + 3)
                    run(GCH[c % 2][:, :, bass.ds(8 * i + 4 * par, 4)].rearrange("p j t -> p t j"),
                        bank[par][:].rearrange("p (t j) -> p t j", t=4), ACT.Copy).then_inc(gh_copied, 1)
        for n in range(2):
            act.wait_ge(g_out[n], 16 * GCHUNKS // 2)

        def expert_hi(i, b):
            act.wait_ge(u_turned, 16 * i + b + 2)
            act.wait_ge(s_blk, 16 * i + max(b - 3, 0) + 1)
            run(UTH[b % 4][:], bank[b % 4][:].rearrange("p (k i) -> p k i", k=4), ACT.Copy).then_inc(ut_hi, 1)

        def gelu(i, jj):
            act.wait_ge(s_blk, 16 * i + 4 * jj + 5)
            act.wait_ge(aj_done, 4 * i + max(jj - 1, 0) + 1)
            run(gt[jj % 2][:], bank[4 + jj % 2][:, 0:T], ACT.Gelu).then_inc(gelu_done, 1)

        def value_hi(i, h, jj):
            act.wait_ge(vv_in[h][jj], 16 * i + 16)
            act.wait_ge(o_done, 16 * i + 1)
            run(VH[h][jj][:], VRAW[h][jj][:], ACT.Copy).then_inc(v_hi, 1)

        def act_group(i, last):
            for b in range(16):
                if b + 2 < 16 or not last:
                    expert_hi(i, b + 2)
                if b % 4 == 0 and b:
                    gelu(i, b // 4 - 1)
                if b >= 4 and b % 2 == 0:
                    n = (b - 4) // 2
                    if n < 4:
                        value_hi(i, 0, n)
            gelu(i, 3)
            for jj in range(4):
                value_hi(i, 1, jj)

        expert_hi(0, 0)
        expert_hi(0, 1)
        with act.Fori(0, GROUPS - 1) as i:
            act_group(i, False)
        act_group(GROUPS - 1, True)
        for tt, (t0, nt) in enumerate(TILES):
            act.wait_ge(y_turned, tt + 1)
            if tt == 2:
                act.wait_ge(y_out[0], 16)
            for n in range(2):
                last = run(YS[tt % 2][0:nt, 512 * n:512 * (n + 1)], bank[n][0:nt, :], ACT.Copy)
            last.then_inc(y_act, 1)

    @block.vector
    def _(dve):
        v = nc.vector
        ch = Chain(dve, dve_ch)
        for s_ in (il_used, al_used, ao_copied, sig_used, ut_lo, aj_done, o_added):
            dve.sem_inc(s_, 1)

        def b3(ap, shape):
            return ap.broadcast_to(shape)

        def inverse_root(s_, var_ps, inv_n, va, y, t):
            ch(v.tensor_scalar(va, var_ps, inv_n, EPS, ALU.mult, ALU.add))
            ch(v.reciprocal(y, s_))
            ch(v.tensor_tensor(t, y, y, ALU.mult))
            ch(v.tensor_tensor(t, t, va, ALU.mult))
            ch(v.tensor_scalar(t, t, -0.5, 1.5, ALU.mult, ALU.add))
            ch(v.tensor_tensor(y, y, t, ALU.mult))

        dve.wait_ge(c_silu, 1)
        v.tensor_tensor(CSIL[:], CT_[:], bank[7][:, 0:NC * KT].rearrange("p (k c) -> p k c", c=NC), ALU.mult).then_inc(c_silu, 1)
        dve.wait_ge(v_copied, 1)
        for half in range(2):
            dve.wait_ge(mod_turned, half + 1)
            v.tensor_tensor(MOD[:, 48 * half:48 * (half + 1)], bank[4 + half][:, 0:48 * NC].rearrange("p (f c) -> p f c", c=NC),
                            b3(VEC[:, 48 * half:48 * (half + 1)].unsqueeze(2), [P, 48, NC]), ALU.add).then_inc(mod_done, 1)
        dve.wait_ge(mod_done, 2)

        def norm(n):
            m0 = 48 * n
            ch(v.tensor_scalar(AM[:], MOD[:, m0 + 16:m0 + 32], 1.0, None, ALU.add))
            ch(v.tensor_tensor(AM[:], AM[:], b3(VEC[:, 98 + 16 * n:114 + 16 * n].unsqueeze(2), [P, KT, NC]), ALU.mult))
            dve.wait_ge(std_done, n + 1)
            inverse_root(n_s[:], bank[6][:, 0:T], 1.0 / D, n_v[:], n_y[:], n_t[:])
            ch(v.tensor_tensor(H[:], X[:], b3(n_y[:].unsqueeze(1), [P, KT, T]), ALU.mult))
            hp = H[:, :, 0:TP]
            hs = H[:, :, TP:T].rearrange("p k (b t) -> p k b t", b=NB)
            for op, w in ((ALU.mult, AM[:]), (ALU.add, MOD[:, m0:m0 + 16])):
                ch(v.tensor_tensor(hp, hp, b3(w[:, :, 0:1], [P, KT, TP]), op))
                last = v.tensor_tensor(hs, hs, b3(w[:, :, 1:NC].unsqueeze(3), [P, KT, NB, NT]), op)
                if op == ALU.mult:
                    ch(last)
            last.then_inc(norm_done, 1)

        norm(0)
        dve.wait_ge(mix_in, 16)
        cos, sin = mix[:, M_COS:M_COS + T], mix[:, M_SIN:M_SIN + T]

        def rotate(par, out, done):
            ch(v.tensor_tensor(ra[:], raw[par][:], cos, ALU.mult))
            ch(v.tensor_tensor(rb_[:], bank[4 + par][:, 0:T], sin, ALU.mult))
            last = v.tensor_tensor(out, ra[:], rb_[:], ALU.add)
            if done:
                last.then_inc(rope_done, 1)
            else:
                ch(last)

        def rotate_normed(par, out):
            inverse_root(qks[par][:], bank[6 + par][:, 0:T], 1.0 / 128, rv[:], ry[:], rt[:])
            rotate(par, ra[:], False)
            v.tensor_tensor(out, ra[:], ry[:], ALU.mult).then_inc(rope_done, 1)

        dve.wait_ge(rot_done, 1)
        rotate(0, ikT[:], True)
        for u in range(4):
            dve.wait_ge(qk_std, u + 1)
            dve.wait_ge(rope_done, u + 1)
            rotate_normed((1 + u) % 2, kTt[:, u])
        ch(v.memset(WZ[:], 0.0))
        dve.wait_ge(wz_mm, 1)
        v.tensor_tensor(WZ[:].rearrange("p (b c) -> p b c", b=NB)[:, :, 0:NT],
                        bank[7][0:64, 0:TS].rearrange("p (b t) -> p b t", b=NB),
                        b3(mix[0:64, M_DT:M_DT + NT].unsqueeze(1), [64, NB, NT]), ALU.mult).then_inc(wz_done, 2)
        with ch.loop(2, 16) as i:
            for u in range(8):
                dve.wait_ge(rot_done, 10 + u + 8 * i)
                dve.wait_ge(rope_done, 5 + u + 8 * i)
                rotate((5 + u) % 2, S1[:, bass.ds(8 * i + u, 1)].rearrange("p a t -> p (a t)"), True)
        dve.wait_ge(rope_done, 21)
        dve.wait_ge(ssc_mm, NB)
        ch(v.tensor_tensor(SSC[:], bank[6][0:TS, 0:LS], mix[0:TS, M_SMASK:M_SMASK + LS], ALU.add))
        for n in range(-(-KSEL_S // 8)):
            left = KSEL_S - 8 * n
            ch(v.max(smx[:], SSC[:]))
            if left < 8:
                ch(v.memset(smx[:, left:8], TAKEN))
            ch(v.match_replace(SSC[:], smx[:], SSC[:], TAKEN))
        ch(v.tensor_scalar(SSC[:], SSC[:], -2e38, NEG, ALU.is_gt, ALU.mult))
        ch(v.tensor_tensor(smb[:], SSC[:], mix[0:TS, M_SMASK:M_SMASK + LS], ALU.add))
        for tt in range(2):
            if tt:
                ch(v.memset(MB[:, 1, 0:128], 0.0))
            ch(v.tensor_copy(MB[:, tt, 128 * tt:128 * (tt + 1)], mix[:, M_TRI:M_TRI + P]))
        ch(v.memset(MB[:, 0, 128:256], NEG))
        with ch.loop(4, 6) as i:
            dve.wait_ge(il_done, 2 * i + 1)
            v.tensor_copy(QG[:], S1[:, bass.ds(4 * i, 4)]).then_inc(qg_ready, 1)
            for tt in range(2):
                dve.wait_ge(il_done, 2 * i + tt + 1 + 1)
                for n in range(2):
                    ch(v.scalar_tensor_tensor(out=E4[:, 2 * n:2 * n + 2], in0=bank[4 + n][:].rearrange("p (a s) -> p a s", a=2),
                                              scalar=0.0, in1=b3(iwN[:, tt, bass.ds(4 * i + 2 * n, 2)].unsqueeze(2), [P, 2, TP]),
                                              op0=ALU.max, op1=ALU.mult))
                ch(v.tensor_reduce(rsc[:], E4[:].rearrange("p a s -> p s a"), AX.X, ALU.add))
                v.tensor_tensor(MB[:, tt], MB[:, tt], rsc[:], ALU.add).then_inc(il_used, 1)
        dve.wait_ge(il_used, 8 + 1)
        for n in range(KSEL_P // 8):
            for tt in range(2):
                ch(v.max(mx8[:, tt], MB[:, tt]))
                ch(v.match_replace(MB[:, tt], mx8[:, tt], MB[:, tt], TAKEN))
        ch(v.tensor_scalar(MB[:], MB[:], -2e38, NEG, ALU.is_gt, ALU.mult))
        for tt in range(2):
            ch(v.tensor_tensor(MB[:, tt, 128 * tt:128 * (tt + 1)], MB[:, tt, 128 * tt:128 * (tt + 1)],
                               mix[:, M_TRI:M_TRI + P], ALU.add))
        with ch.loop(2, 9 * 8) as i:
            for u in range(8):
                par = (21 + u) % 2
                dve.wait_ge(qk_std, 4 + u + 1 + 8 * i)
                dve.wait_ge(rope_done, 21 + u + 8 * i)
                rotate_normed(par, S2[:, bass.ds(8 * i + u, 1)].rearrange("p a t -> p (a t)"))
        dve.wait_ge(rope_done, ROPES)
        with ch.loop(4, 8) as g:
            dve.wait_ge(al_done, 2 * g + 1)
            v.tensor_copy(QG[:], S2[:, bass.ds(4 * g, 4)]).then_inc(ag_ready, 1)
            for tt in range(2):
                S = 128 * (tt + 1)
                dve.wait_ge(al_done, 2 * g + tt + 1 + 1)
                dve.wait_ge(pt_turned, 3 * g + tt + 1)
                for n in range(2):
                    last = v.tensor_tensor(E4[:, 2 * n:2 * n + 2, 0:S],
                                           bank[4 + n][:].rearrange("p (a s) -> p a s", a=2)[:, :, 0:S],
                                           b3(MB[:, tt:tt + 1, 0:S], [P, 2, S]), ALU.add)
                    if n == 0:
                        ch(last)
                last.then_inc(al_used, 1)
                dve.wait_ge(al_used, 2 * g + tt + 1 + 1)
                ch(v.tensor_reduce(st1[:], E4[:, :, 0:S], AX.X, ALU.max))
                v.tensor_tensor(E4[:, :, 0:S], E4[:, :, 0:S], b3(st1[:].unsqueeze(2), [P, GR, S]), ALU.subtract).then_inc(al_shift, 1)
                dve.wait_ge(al_exp, 2 * g + tt + 1)
                ch(v.tensor_reduce(st2[:], E4[:, :, 0:S], AX.X, ALU.add))
                ch(v.reciprocal(st2[:], st2[:]))
                v.tensor_tensor(E4[:, :, 0:S], E4[:, :, 0:S], b3(st2[:].unsqueeze(2), [P, GR, S]), ALU.mult).then_inc(al_prob, 1)
                dve.wait_ge(ao_done, 2 * g + tt + 1 + 1)
                v.tensor_copy(S1[:, bass.ds(4 * g, 4), 128 * tt:128 * (tt + 1)],
                              bank[7][:].rearrange("p (a t) -> p a t", a=4)).then_inc(ao_copied, 1)
        dve.wait_ge(ao_copied, 8 + 1)
        for n in range(2):
            ch(v.memset(QSB[n][:], 0.0))
        for b in range(NB):
            if b >= 2:
                dve.wait_ge(sal_done, b - 1)
            v.tensor_copy(QSB[b % 2][:, :, 0:16].rearrange("p g (h t) -> p g h t", h=4),
                          S2[:, :, TP + NT * b:TP + NT * (b + 1)].rearrange("p (g h) t -> p g h t", g=4)).then_inc(sq_ready, 1)
            dve.wait_ge(sal_done, b + 1)
            ch(v.tensor_reduce(sb2[:], bank[6][:, 0:LS], AX.X, ALU.max))
            v.tensor_scalar(sb1[:], sb2[:], -ATT_SCALE, None, ALU.mult).then_inc(sal_max, 1)
            dve.wait_ge(sal_exp, b + 1)
            ch(v.reciprocal(sb1[:], sb2[:]))
            v.tensor_scalar(EN[:], EN[:], sb1[:], None, ALU.mult).then_inc(sal_prob, 1)
            dve.wait_ge(so_done, b + 1)
            v.tensor_copy(S1[:, :, TP + NT * b:TP + NT * (b + 1)],
                          bank[4][:, 0:64].rearrange("p (h t) -> p h t", h=16)).then_inc(so_copied, 1)
        ch(v.memset(PA[:, :, 0:NPRE], 0.0))
        dve.wait_ge(st_copied, 2)
        dve.wait_ge(gemm_evac, U_P + 8)
        for n, (dst, src) in enumerate(((PB, PA), (PC, PB), (PB, PC), (PC, PB))):
            sh = 1 << n
            c0 = 2 * n
            ch(v.tensor_tensor(dst[:, c0:CT, 2 * sh - 1:PADT], src[:, c0:CT, 2 * sh - 1:PADT],
                               src[:, c0:CT, sh - 1:PADT - sh], ALU.add))
            cs = slice(c0, c0 + 2)
            w = POOL_W[n]
            o_p = POOLED[:, cs, 0:TP]
            ch(v.tensor_scalar(o_p[:, :, 16:TP], dst[:, cs, NPRE + 16:PADP], 1.0 / w, None, ALU.mult))
            ch(v.tensor_tensor(o_p[:, :, 0:16], dst[:, cs, NPRE:NPRE + 16],
                               b3(mix[:, M_CNT + 16 * n:M_CNT + 16 * (n + 1)].unsqueeze(1), [P, 2, 16]), ALU.mult))
            ch(v.tensor_tensor(o_p, o_p, PA[:, cs, NPRE:PADP], ALU.subtract))
            for c in range(c0, c0 + 2):
                d_s = dst[:, c, PADP:PADT].rearrange("p (b s) -> p b s", b=NB)[:, :, NPRE:PADS]
                a_s = PA[:, c, PADP:PADT].rearrange("p (b s) -> p b s", b=NB)[:, :, NPRE:PADS]
                last = v.scalar_tensor_tensor(out=POOLED[:, c, TP:T].rearrange("p (b t) -> p b t", b=NB), in0=d_s,
                                              scalar=1.0 / w, in1=a_s, op0=ALU.mult, op1=ALU.subtract)
                if (n, c) != (3, 7):
                    ch(last)
        last.then_inc(pooled_done, 1)

        def input_lo(n, out, src, hi):
            for q in range(4):
                dve.wait_ge(in_hi, n + q + 1)
                v.tensor_tensor(out[:, 4 * q:4 * q + 4], src[:, 4 * q:4 * q + 4], hi[:, 4 * q:4 * q + 4].bitcast(F32),
                                ALU.subtract).then_inc(in_lo, 1)

        input_lo(0, HL, H, INH)
        with ch.loop(2, 0) as i:
            for u in range(8):
                dve.wait_ge(gemm_evac, U_GB + u + 1 + 8 * i)
                s3u = S3[:, bass.ds(8 * i + u, 1)].rearrange("p a t -> p (a t)")
                v.tensor_tensor(s3u, s3u, SG[u % 2][:], ALU.mult).then_inc(sig_used, 1)
        dve.wait_ge(sig_used, 16 + 1)
        input_lo(4, AOL, S1, INH)
        with ch.loop(2, 24) as i:
            for u in range(8):
                dve.wait_ge(gemm_done, U_PROJ + u + 1 + 8 * i)
                dve.wait_ge(gemm_evac, U_PROJ + u + 8 * i)
                s3u = S3[:, bass.ds(8 * i + u, 1)].rearrange("p a t -> p (a t)")
                ch(v.tensor_tensor(SG[u % 2][:], bank[(U_PROJ + u) % 4][:, 0:T],
                                   S2[:, bass.ds(8 * i + u, 1)].rearrange("p a t -> p (a t)"), ALU.mult))
                ch(v.tensor_tensor(SG[u % 2][:], s3u, SG[u % 2][:], ALU.add))
                hi, lo = (x[:, bass.ds(8 * i + u, 1)].rearrange("p a t -> p (a t)") for x in (MGH, MGL))
                ch(v.tensor_copy(hi, SG[u % 2][:]))
                v.tensor_tensor(lo, SG[u % 2][:], hi.bitcast(F32), ALU.subtract).then_inc(gemm_evac, 1)
        with ch.loop(2, 16) as i:
            for u in range(8):
                f = 32 + u
                dve.wait_ge(gemm_done, U_OUT + u + 1 + 8 * i)
                xu = X[:, bass.ds(8 * i + u, 1)].rearrange("p a t -> p (a t)")
                ch(v.scalar_tensor_tensor(out=xu[:, 0:TP], in0=bank[(U_OUT + u) % 4][:, 0:TP],
                                          scalar=MOD[:, bass.ds(8 * i + f, 1), 0:1].rearrange("p a b -> p (a b)"),
                                          in1=xu[:, 0:TP], op0=ALU.mult, op1=ALU.add))
                ch(v.tensor_tensor(og[:].rearrange("p (b t) -> p b t", b=NB),
                                   bank[(U_OUT + u) % 4][:, TP:T].rearrange("p (b t) -> p b t", b=NB),
                                   b3(MOD[:, bass.ds(8 * i + f, 1), 1:NC].rearrange("p a b -> p (a b)").unsqueeze(2), [P, NB, NT]), ALU.mult))
                v.tensor_tensor(xu[:, TP:T], xu[:, TP:T], og[:], ALU.add).then_inc(gemm_evac, 1)
        norm(1)
        input_lo(8, HL, H, HH)

        for tt, (t0, nt) in enumerate(TILES):
            dve.wait_ge(psc_copied, tt + 1)
            if tt:
                dve.wait_ge(sl_turned, tt)
            s_ = slice(0, nt)

            def best(values, index, rows, count):
                for r in range(2):
                    k8 = slice(8 * r, 8 * r + 8)
                    for a in range(count):
                        last = v.max(values[s_, a, k8], rows[s_, a])
                    ch(last)
                    for a in range(count):
                        last = v.max_index(index[s_, a, k8], values[s_, a, k8], rows[s_, a])
                    ch(last)
                    if r == 0:
                        for a in range(count):
                            last = v.match_replace(rows[s_, a], values[s_, a, k8], rows[s_, a], TAKEN)
                        ch(last)

            best(pv, pi, SS, 16)
            ch(v.tensor_copy(pif[s_], pi[s_]))
            halves = pv[s_].rearrange("t (h q) k -> t h q k", q=2)
            ch(v.tensor_tensor(CAND[s_].rearrange("t h (a b) -> t h a b", a=PK),
                               b3(halves[:, :, 0].unsqueeze(3), [nt, PH, PK, PK]),
                               b3(halves[:, :, 1].unsqueeze(2), [nt, PH, PK, PK]), ALU.add))
            best(wv, wi, CAND, PH)
            ch(v.tensor_copy(s8[s_], wv[s_, :, 0]))
            v.tensor_tensor(wv[s_], wv[s_], b3(s8[s_].unsqueeze(2), [nt, PH, PK]), ALU.subtract).then_inc(pex_done, 1)
            ch(v.tensor_scalar(wa[s_], wi[s_], 4, None, ALU.logical_shift_right))
            ch(v.tensor_copy(waf[s_], wa[s_]))
            ch(v.tensor_scalar(wa[s_], wi[s_], 15, None, ALU.bitwise_and))
            ch(v.tensor_copy(wbf[s_], wa[s_]))
            idx = pif[s_].rearrange("t (h q) k -> t h q k", q=2)
            for q, (wf, out) in enumerate(((waf, ei), (wbf, ej))):
                ch(v.tensor_tensor(EQ[s_], b3(wf[s_].rearrange("t h k -> t (h k)").unsqueeze(2), [nt, PH * PK, PK]),
                                   b3(iota[s_, 0:PK].unsqueeze(1), [nt, PH * PK, PK]), ALU.is_equal))
                e4 = EQ[s_].rearrange("t (h k) a -> t h k a", h=PH)
                ch(v.tensor_tensor(e4, e4, b3(idx[:, :, q].unsqueeze(2), [nt, PH, PK, PK]), ALU.mult))
                last = v.tensor_reduce(out[s_], EQ[s_], AX.X, ALU.add)
                if q == 0:
                    ch(last)
            last.then_inc(psel_done, 1)
            dve.wait_ge(psel_done, tt + 1)
            dve.wait_ge(pex_done, 2 * tt + 2)
            ch(v.tensor_reduce(s8[s_], wv[s_], AX.X, ALU.add))
            ch(v.reciprocal(s8[s_], s8[s_]))
            v.tensor_tensor(wv[s_], wv[s_], b3(s8[s_].unsqueeze(2), [nt, PH, PK]), ALU.mult).then_inc(pw_done, 1)
        dve.wait_ge(slot_copied, 9)
        v.tensor_copy(GP[0][:], GF[:]).then_inc(slots_done, 1)
        dve.wait_ge(slots_done, 1)
        v.tensor_tensor(GRr[:], GF[:], GP[0][:], ALU.subtract).then_inc(slots_done, 1)
        dve.wait_ge(slots_done, 2)
        v.tensor_copy(GP[1][:], GRr[:]).then_inc(slots_done, 1)
        dve.wait_ge(slots_done, 3)
        v.tensor_tensor(GRr[:], GRr[:], GP[1][:], ALU.subtract).then_inc(slots_done, 1)
        dve.wait_ge(slots_done, 4)
        v.tensor_copy(GP[2][:], GRr[:]).then_inc(slots_done, 1)
        dve.wait_ge(slots_done, 5)

        ch(v.tensor_copy(iob[:], b3(iota.unsqueeze(2), [P, P, 2])))
        full = [P, 2, NE, 2]

        def of_keys(ap):
            return b3(ap.unsqueeze(1), full)

        def of_tokens(ap):
            return b3(ap.rearrange("p (a t) -> p a t", a=2).unsqueeze(2), full)

        for c in range(GCHUNKS):
            nb0 = 2 * GITERS * c
            with ch.loop(GITERS, 2) as i:
                for par in range(2):
                    dve.wait_ge(oh_used, nb0 + 2 * i + par + 1)
                    at = bass.ds(GTOK * c + 8 * i + 4 * par, 4)
                    v.tensor_tensor(OA[par][:], of_keys(iob[:]), of_tokens(IB[:, at]), ALU.is_equal)
                    ch(v.tensor_tensor(OQ[par][:], of_keys(iob[:]), of_tokens(JB[:, at]), ALU.is_equal))
                    for k in range(3):
                        last = v.tensor_tensor(OBp[par][k][:], OQ[par][:], of_tokens(GP[k][:, at]), ALU.mult)
                    last.then_inc(oh_ready, 1)
        for n in range(2):
            dve.wait_ge(g_out[n], 16 * GCHUNKS // 2)
        ch(v.memset(XS[:], 0.0))

        def expert_lo(i, b):
            dve.wait_ge(ut_hi, 16 * i + b + 1)
            v.tensor_tensor(UTL[b % 4][:], bank[b % 4][:].rearrange("p (k i) -> p k i", k=4),
                            UTH[b % 4][:].bitcast(F32), ALU.subtract).then_inc(ut_lo, 1)

        def weigh(i, jj):
            dve.wait_ge(gelu_done, 4 * i + jj + 2)
            if jj == 0:
                dve.wait_ge(g_in, 16 * i + 16)
                dve.wait_ge(o_done, 16 * i + 1)
            ch(v.tensor_tensor(af[jj % 2][:], gt[jj % 2][:], GH[:, jj], ALU.mult))
            ch(v.tensor_copy(AH[jj][:], af[jj % 2][:]))
            v.tensor_tensor(AL[jj][:], af[jj % 2][:], AH[jj][:].bitcast(F32), ALU.subtract).then_inc(aj_done, 1)

        def dve_group(i, last):
            for b in range(16):
                if b + 2 < 16 or not last:
                    expert_lo(i, b + 2)
                if b % 4 == 1 and b > 4:
                    weigh(i, b // 4 - 1)
            weigh(i, 3)
            dve.wait_ge(o_added, 16 * i + 1)
            for m_ in range(KT):
                dve.wait_ge(o_done, 16 * i + m_ + 2)
                o = bank[6 + m_ % 2]
                v.scalar_tensor_tensor(out=X[:, m_, 0:TP], in0=o[:, 0:TP], scalar=MOD[:, 80 + m_, 0:1],
                                       in1=X[:, m_, 0:TP], op0=ALU.mult, op1=ALU.add)
                v.tensor_tensor(XS[:, m_], XS[:, m_], o[:, TP:T], ALU.add).then_inc(o_added, 1)

        expert_lo(0, 0)
        expert_lo(0, 1)
        with ch.loop(GROUPS - 1, 8) as i:
            dve_group(i, False)
        dve_group(GROUPS - 1, True)
        dve.wait_ge(o_added, 16 * GROUPS + 1)
        xs4 = XS[:].rearrange("p k (b t) -> p k b t", b=NB)
        ch(v.tensor_tensor(xs4, xs4, b3(MOD[:, 80:96, 1:NC].unsqueeze(3), [P, KT, NB, NT]), ALU.mult))
        v.tensor_tensor(X[:, :, TP:T], X[:, :, TP:T], XS[:], ALU.add).then_inc(xs_done, 1)
        for tt, (t0, nt) in enumerate(TILES):
            dve.wait_ge(y_turned, tt + 1)
            if tt == 2:
                dve.wait_ge(y_out[0], 16)
            for n in range(2, 4):
                last = v.tensor_copy(YS[tt % 2][0:nt, 512 * n:512 * (n + 1)], bank[n][0:nt, :])
            last.then_inc(y_dve, 1)

    ctx.close()


_INS = ['x_prompt', 'x_sample', 'cache_k', 'cache_v', 'cache_idx_k', 'state_pool', 'page_table', 'c_prompt', 'c_sample',
        'norm1_g', 'norm2_g', 'w_mod', 'b_mod', 'w_in', 'q_norm_g', 'k_norm_g', 'w_attn_proj', 'w_pool', 'pool_scale',
        'w_out', 'w_peer_q', 'peer_keys', 'peer_u', 'peer_v']
_OUTS = [(1, 256, 2048), (8, 4, 2048), (1, 256, 4, 128), (1, 256, 4, 128), (1, 256, 128), (1, 15, 1024),
         (8, 4, 4, 128), (8, 4, 4, 128), (8, 4, 128), (8, 15, 1024)]


def kernel(**inputs):
    import concourse.bacc as _bacc
    from concourse.bass_utils import run_bass_kernel_spmd as _run

    nc = _bacc.Bacc("TRN2", target_bir_lowering=False, num_devices=1)
    arrays, args = {}, []
    for name in _INS:
        a = np.ascontiguousarray(inputs[name])
        arrays[f"in_{name}"] = a
        args.append(nc.dram_tensor(f"in_{name}", a.shape, mybir.dt.from_np(a.dtype), kind="ExternalInput").ap())
    for name, a in zip(("keep", "mix"), constants()):
        arrays[f"in_{name}"] = a
        args.append(nc.dram_tensor(f"in_{name}", a.shape, F32, kind="ExternalInput").ap())
    for i, shape in enumerate(_OUTS):
        args.append(nc.dram_tensor(f"out_{i}", shape, F32, kind="ExternalOutput").ap())
    layer_kernel(nc, *args)
    r = _run(nc, [arrays], core_ids=[0])
    return tuple(r.results[0][f"out_{i}"] for i in range(len(_OUTS)))
```

```python
from contextlib import ExitStack, contextmanager

import numpy as np

import concourse.bass as bass
from concourse import mybir

F32 = mybir.dt.float32
BF16 = mybir.dt.bfloat16
F32R = mybir.dt.float32r
I32 = mybir.dt.int32
U32 = mybir.dt.uint32
ALU = mybir.AluOpType
ACT = mybir.ActivationFunctionType
AX = mybir.AxisListType

P = 128
D = 2048
KT = D // P
TP = 256
NB, NT = 8, 4
TS = NB * NT
T = TP + TS
TILES = [(0, 128), (128, 128), (256, 32)]
HQ, HK, GR = 16, 4, 4
PAST = 256
LS = PAST + NT
KSEL_P, KSEL_S = TP // 4, LS // 4
NC = 1 + NB
CPAD = 72
POOL_W = (2, 4, 8, 16)
NPRE = 15
CT = 8
PADP = NPRE + TP
PADS = NPRE + NT
PADT = PADP + NB * PADS
NE = 128
PH, PK = 8, 16
EPS = 1e-6
GTOK = 32
EARLY = 8
NEG = -1e30
TAKEN = -3e38
ATT_SCALE = 128 ** -0.5
IW_SCALE = 16 ** -0.5 * 128 ** -0.5
C_Q, C_K, C_V, C_IQ, C_IK, C_P = 0, 2048, 2560, 3072, 5120, 5264
C_GA, C_GB = 6288, 8336

U_IK, U_K, U_V, U_IQ, U_G1, U_Q, U_G2, U_G3, U_G4, U_P, U_G5, U_POOL, U_PROJ, U_OUT, U_PQ, U_END = (
    48, 50, 54, 58, 74, 82, 98, 100, 108, 116, 124, 130, 146, 162, 178, 194)
G1, G2, G3, G4, G5 = 0, 8, 10, 18, 26
K_POOL = U_POOL


def units_done(chunk):
    return chunk + 1 if chunk < K_POOL else chunk + 16


def chunk_of(n):
    return n + U_IK if n + U_IK < K_POOL else n + U_IK + 1


def split_of(unit):
    return unit - U_IK if unit < K_POOL else unit - U_IK - 16


class Chain:

    def __init__(self, eng, sem):
        self.eng, self.sem, self.n, self.base = eng, sem, 0, 0

    def __call__(self, ins):
        ins.then_inc(self.sem, 1)
        self.n += 1
        self.eng.wait_ge(self.sem, self.n + self.base)

    @contextmanager
    def loop(self, count, per):
        start = self.n
        with self.eng.Fori(0, count) as i:
            self.base = i * per if per else 0
            yield i
            assert self.n - start == per, (self.n - start, per)
            self.base = 0
        self.n = start + per * count


def constants():
    f = np.float32
    keep = np.zeros((P, 388), f)
    keep[:, 0:128] = np.eye(P)
    keep[:, 128:256] = 1.0
    keep[:, 256:384] = np.arange(P)[None]
    keep[:, 384] = EPS
    pos = np.concatenate([np.arange(TP), np.tile(PAST + np.arange(NT), NB)]).astype(f)
    half = 64
    freqs = (f(10000.0) ** (-np.arange(half, dtype=f) / f(half))).astype(f)
    ang = (pos[None, :] * freqs[:, None]).astype(f)
    mix = np.zeros((P, MIX), f)
    for k in range(half):
        mix[k + half, M_ROT + k] = -1.0
        mix[k, M_ROT + k + half] = 1.0
    mix[:, M_COS:M_COS + T] = np.concatenate([np.cos(ang)] * 2)
    mix[:, M_SIN:M_SIN + T] = np.concatenate([np.sin(ang)] * 2)
    for g, w in enumerate(POOL_W):
        mix[:, M_CNT + 16 * g:M_CNT + 16 * (g + 1)] = 1.0 / np.minimum(np.arange(16) + 1, w)
    mix[:, M_TRI:M_TRI + P] = np.where(np.arange(P)[None] > np.arange(P)[:, None], NEG, 0.0)
    q = np.arange(TS)
    s = np.arange(LS)
    mix[0:TS, M_SMASK:M_SMASK + LS] = np.where(s[None] > PAST + (q % NT)[:, None], NEG, 0.0)
    r = np.arange(P)
    for b in range(NB):
        hit = (q[:, None] == NT * b + (r % NT)[None]) & ((r % 32) < 16)[None]
        mix[0:TS, M_REP + P * b:M_REP + P * (b + 1)] = hit
    for h in range(16):
        mix[h, M_E16 + NT * h:M_E16 + NT * (h + 1)] = 1.0
    for k in range(64):
        mix[k, M_DT + k % NT] = 1.0
    return keep, mix


M_ROT, M_COS, M_SIN, M_CNT, M_TRI, M_SMASK, M_REP, M_E16, M_DT = (
    0, 128, 416, 704, 768, 896, 1156, 2180, 2244)
MIX = 2248


def layer_kernel(nc, x_p, x_s, cache_k, cache_v, cache_ik, state, ptab, c_p, c_s, norm1_g, norm2_g,
                 w_mod, b_mod, w_in, q_g, k_g, w_proj, w_pool, pool_scale, w_out, w_pq, pkeys,
                 peer_u, peer_v, keep_d, mix_d,
                 y_p, y_s, k_p, v_p, ik_p, ps_p, k_s, v_s, ik_s, ps_s):
    PAGES = ptab.shape[0] * ptab.shape[1]
    NPOOL = cache_k.shape[0]

    class Map:
        def __init__(self, at):
            self.at = at

        def __call__(self, name, shape, dt=F32):
            n = int(np.prod(shape[1:])) * (2 if dt == BF16 else 4)
            n = -(-n // 32) * 32
            t = nc.alloc_sbuf_tensor_at(name, list(shape), dt, offset=self.at)
            self.at += n
            return t

        def skip(self, n):
            at = self.at
            self.at += n
            return Map(at)

    top = Map(16896)
    keep = top("keep", [P, 388])
    ident, ones, iota = keep[:, 0:128], keep[:, 128:256], keep[:, 256:384]
    eps = keep[:, 384:385]
    x_at = top.at
    X = top("X", [P, KT, T])
    h_at = top.at
    H = top("H", [P, KT, T])
    MOD = top("MOD", [P, 6 * KT, NC])
    AM = top("AM", [P, KT, NC])
    VEC = top("VEC", [P, 146])
    pages = top("pages", [1, 64], I32)
    norm_at = top.at
    n_s, n_v, n_y, n_t = (top(f"n_{c}", [P, T]) for c in "svyt")
    top.at = norm_at + 4 * 1152
    free_at = top.at
    mix = top("mix", [P, MIX])
    s_at = top.at
    S1 = top("S1", [P, KT, T])
    s2_at = top.at
    S2 = top("S2", [P, KT, T])
    s3_at = top.at
    S3 = top("S3", [P, KT, T])
    ring_at = top.at
    ring = [top(f"ring{n}", [P, KT, 256]) for n in range(4)]
    RAW = [Map(ring_at + 16384 * n)(f"RAW{n}", [P, KT, P]) for n in range(4)]
    WL = [Map(ring_at + 16384 * n)(f"WL{n}", [P, KT, P], F32R) for n in range(4)]
    WH = [Map(ring_at + 16384 * n + 8192)(f"WH{n}", [P, KT, P], F32R) for n in range(4)]
    kv_at = top.at
    kTt = top("kTt", [P, HK, T])
    vTt = top("vTt", [P, HK, T])
    ikT = top("ikT", [P, T])
    iwT = top("iwT", [16, T])
    vN = top("vN", [P, 2, 512])
    tmp_at = top.at
    END = 229368
    assert END - tmp_at >= 17424, END - tmp_at

    m = Map(h_at)
    XTOK = [m("xtok0", [P, D]), m("xtok1", [P, D])]
    m = Map(tmp_at)
    XTOK.append(m("xtok2", [P, D]))
    VA, VB, CT_ = m("VA", [98, P]), m("VB", [48, P]), m("CT_", [P, KT, NC])
    CSF = m("CSF", [P, KT, CPAD])
    m = Map(kv_at)
    CTOK = m("CTOK", [NC, D])
    MR = [m(f"MR{n}", [P, 256]) for n in range(2)]
    CSL = m("CSL", [P, KT, CPAD], F32R)
    assert m.at <= tmp_at
    m = Map(s_at)
    MWH = [m(f"MWH{n}", [P, KT, 256], F32R) for n in range(3)]
    CSH = m("CSH", [P, KT, CPAD], F32R)
    assert m.at <= ring_at
    MWL = [Map(ring_at + 16384 * n)(f"MWL{n}", [P, KT, 256], F32R) for n in range(4)]

    m = Map(tmp_at)
    raw = [m(f"raw{n}", [P, T]) for n in range(4)]
    sq = [m(f"sq{n}", [P, T]) for n in range(2)]
    qks = [m(f"qks{n}", [P, T]) for n in range(2)]
    ra, rb_ = m("ra", [P, T]), m("rb_", [P, T])
    rv, ry, rt = m("rv", [P, T]), m("ry", [P, T]), m("rt", [P, T])
    stage = m("stage", [P, 512])
    iwN = m("iwN", [P, 2, 16])
    assert m.at <= END - 1048
    m = Map(tmp_at)
    kpg = [m(f"kpg{n}", [P, 2, 512]) for n in range(2)]
    vpg = [m(f"vpg{n}", [P, 2, 512]) for n in range(2)]
    smb = Map(END - 1048)("smb", [TS, LS])

    m = Map(s3_at)
    MB = m("MB", [P, 2, TP])
    QG = m("QG", [P, GR, T])
    VG = m("VG", [P, 2, P])
    E4 = m("E4", [P, GR, TP])
    PT = m("PT", [P, 2, GR, P])
    st1, st2 = m("st1", [P, GR]), m("st2", [P, GR])
    mx8 = m("mx8", [P, 2, 8])
    rsc = m("rsc", [P, TP])
    IPG = Map(s3_at + 2048 + 4608 + 1024)("IPG", [P, 2 * NB, P])
    m = Map(s2_at)
    IKB = [m(f"IKB{n}", [P, LS]) for n in range(2)]
    IQB = [m(f"IQB{n}", [P, 64]) for n in range(2)]
    RL = [m(f"RL{n}", [64, LS]) for n in range(2)]
    WZ = m("WZ", [64, 288])
    SSC = m("SSC", [TS, LS])
    smx = m("smx", [TS, 8])
    m = Map(s3_at + 2048)
    KTB = m("KTB", [P, HK, LS])
    QSB = [m(f"QSB{n}", [P, HK, 32]) for n in range(2)]
    EN = m("EN", [P, LS])
    PTB = m("PTB", [P, 2, P])
    PTN = m("PTN", [NT, P])
    VNB = m("VNB", [NT, 512])
    sb1, sb2 = m("sb1", [P, 1]), m("sb2", [P, 1])
    assert m.at <= s3_at + 18432

    PA = Map(s2_at)("PA", [P, CT, PADT])
    PB = Map(tmp_at)("PB", [P, CT, PADT])
    PC = Map(s3_at)("PC", [P, CT, PADT])
    POOLED = Map(kv_at)("POOLED", [P, CT, T])
    STT = Map(kv_at)("STT", [NB * NPRE, CT * P])
    PNEW = Map(kv_at + 9216)("PNEW", [P, CT, TS])
    PST = Map(kv_at + 10240)("PST", [P, CT * P])
    XH = Map(x_at)("XH", [P, KT, T], F32R)
    GBS = Map(x_at)("GBS", [P, KT, T])
    AOH = Map(h_at)("AOH", [P, KT, T], F32R)
    AOL = Map(s_at)("AOL", [P, KT, T], F32R)
    m = Map(kv_at)
    MGH = m("MGH", [P, KT, T], F32R)
    MGL = Map(s3_at)("MGL", [P, KT, T], F32R)
    m2 = Map(norm_at)
    SF = [m2(f"SF{n}", [P, T]) for n in range(2)]
    m.at = max(m.at, tmp_at)
    SG = [m(f"SG{n}", [P, T]) for n in range(2)]
    og = m("og", [P, TS])

    m = Map(s2_at)
    KEYT = m("KEYT", [P, 16, P])
    SS = m("SS", [P, 16, NE])
    m = Map(tmp_at)
    KNAT = m("KNAT", [P, 16, P])
    EQ = Map(s3_at + 18432)("EQ", [P, PH * PK, PK])
    m = Map(kv_at)
    CAND = m("CAND", [P, PH, PK * PK])
    pv = m("pv", [P, 16, PK])
    pi = m("pi", [P, 16, PK], U32)
    pif = m("pif", [P, 16, PK])
    wv = m("wv", [P, PH, PK])
    wi = m("wi", [P, PH, PK], U32)
    wa = m("wa", [P, PH, PK], U32)
    waf = m("waf", [P, PH, PK])
    wbf = m("wbf", [P, PH, PK])
    ei = m("ei", [P, PH * PK])
    ej = m("ej", [P, PH * PK])
    s8 = m("s8", [P, PH])
    slots_at = END - 5 * 576 - 40
    slots_at -= slots_at % 32
    m = Map(slots_at)
    IB, JB = m("IB", [P, T], BF16), m("JB", [P, T], BF16)
    GP = [m(f"GP{n}", [P, T], BF16) for n in range(3)]
    GF = Map(norm_at)("GF", [P, T])
    GRr = Map(norm_at + 1152)("GRr", [P, T])
    assert tmp_at + 8192 <= slots_at

    HL = Map(h_at)("HL", [P, KT, T], F32R)
    HH = Map(s3_at)("HH", [P, KT, T], F32R)
    high_at = s3_at + 18432
    m = Map(high_at + 8192)
    EUB = [m(f"EUB{n}", [P, D]) for n in range(2)]
    EUT = [m(f"EUT{n}", [P, 4, P]) for n in range(2)]
    EUTH = [m(f"EUTH{n}", [P, 4, P], F32R) for n in range(4)]
    EUTL = [m(f"EUTL{n}", [P, 4, P], F32R) for n in range(4)]
    EACT = [m(f"EACT{n}", [P, T]) for n in range(2)]
    assert m.at <= kv_at
    GCH = [m(f"GCH{n}", [P, NE, GTOK]) for n in range(2)]
    OA = [m(f"OA{n}", [P, 2, P, 2], BF16) for n in range(2)]
    OQ = [m(f"OQ{n}", [P, 2, NE, 2], BF16) for n in range(2)]
    OBp = [[m(f"OBp{n}_{k}", [P, 2, NE, 2], BF16) for k in range(3)] for n in range(2)]
    iob = m("iob", [P, P, 2], BF16)
    assert m.at <= slots_at
    m = Map(free_at)
    UB = [m(f"UB{n}", [P, D]) for n in range(4)]
    GH = m("GH", [P, T // GTOK, 4, GTOK])
    gt = [m(f"gt{n}", [P, T]) for n in range(2)]
    XS = m("XS", [P, KT, TS])
    EA = Map(norm_at)("EA", [P, 4, T])
    assert m.at <= s3_at, (m.at, s3_at)
    m = Map(high_at)
    v_at = m.at
    VRAW = [[m(f"VRAW{h}_{n}", [P, D // 2]) for n in range(4)] for h in range(2)]
    m.at = v_at
    VL = [[m(f"VL{h}_{n}", [P, D // 2], F32R) for n in range(4)] for h in range(2)]
    VH = [[m(f"VH{h}_{n}", [P, D // 2], F32R) for n in range(4)] for h in range(2)]
    m2 = Map(m.at)
    AH2 = [m2(f"AH2_{n}", [P, T], F32R) for n in range(4)]
    AL2 = [m2(f"AL2_{n}", [P, T], F32R) for n in range(4)]
    UTH = [m(f"UTH{n}", [P, 4, P], F32R) for n in range(4)]
    UTL = [m(f"UTL{n}", [P, 4, P], F32R) for n in range(4)]
    AH = [m(f"AH{n}", [P, T], F32R) for n in range(4)]
    AL = [m(f"AL{n}", [P, T], F32R) for n in range(4)]
    af = [m(f"af{n}", [P, T]) for n in range(2)]
    assert m.at <= END, (m.at, END)
    YS = [Map(free_at + 8192 * n)(f"YS{n}", [P, D]) for n in range(2)]

    g_dram = nc.dram_tensor("expert_weights", [T // GTOK, P, NE, GTOK], F32, kind="Internal").ap()
    x_dram = nc.dram_tensor("residual", [P, KT, T], F32, kind="Internal").ap()
    s_dram = nc.dram_tensor("gates", [2 * KT, P, T], F32, kind="Internal").ap()
    e_dram = nc.dram_tensor("early_activations", [4 * EARLY, P, T], F32, kind="Internal").ap()

    ctx = ExitStack()
    bank = [ctx.enter_context(nc.psum_tensor(f"bank{n}", [P, 512], F32)) for n in range(8)]

    def sem(name):
        return ctx.enter_context(nc.semaphore(name))

    keep_in, mix_in, x_in, c_in, vec_in = (sem(n) for n in ("keep_in", "mix_in", "x_in", "c_in", "vec_in"))
    pages_in = sem("pages_in")
    wload = [sem(f"wload{n}") for n in range(4)]
    gemm_done, gemm_evac = sem("gemm_done"), sem("gemm_evac")
    x_turned, x_copied = sem("x_turned"), sem("x_copied")
    v_turned, v_copied = sem("v_turned"), sem("v_copied")
    c_turned, c_silu = sem("c_turned"), sem("c_silu")
    mod_turned, mod_done = sem("mod_turned"), sem("mod_done")
    sq_done, ssq_done, std_done, norm_done = sem("sq_done"), sem("ssq_done"), sem("std_done"), sem("norm_done")
    rot_done, qk_std, rope_done = sem("rot_done"), sem("qk_std"), sem("rope_done")
    iw_turned, iw_done = sem("iw_turned"), sem("iw_done")
    wz_mm, wz_done = sem("wz_mm"), sem("wz_done")
    ipg_in, ik_turned, ikb_done = sem("ipg_in"), sem("ik_turned"), sem("ikb_done")
    sl_done, sl_relu, ssc_mm = sem("sl_done"), sem("sl_relu"), sem("ssc_mm")
    il_done, il_used = sem("il_done"), sem("il_used")
    ag_ready, al_done, al_used, al_shift, al_exp, al_prob = (
        sem(n) for n in ("ag_ready", "al_done", "al_used", "al_shift", "al_exp", "al_prob"))
    pt_turned, pt_copied, ao_done, ao_copied = (sem(n) for n in ("pt_turned", "pt_copied", "ao_done", "ao_copied"))
    kv_turned, kv_staged = sem("kv_turned"), sem("kv_staged")
    kv_out = sem("kv_out")
    kvp_in = [sem(f"kvp_in{n}") for n in range(2)]
    sk_turned, sk_copied, sq_ready = sem("sk_turned"), sem("sk_copied"), sem("sq_ready")
    sal_done, sal_max, sal_exp, sal_prob = (sem(n) for n in ("sal_done", "sal_max", "sal_exp", "sal_prob"))
    sp_turned, sp_copied, so_done, so_copied = (sem(n) for n in ("sp_turned", "sp_copied", "so_done", "so_copied"))
    st_in, st_turned, st_copied = sem("st_in"), sem("st_turned"), sem("st_copied")
    ps_turned, ps_staged, ps_out = sem("ps_turned"), sem("ps_staged"), sem("ps_out")
    pooled_done = sem("pooled_done")
    keys_in, keys_turned, keys_copied = sem("keys_in"), sem("keys_turned"), sem("keys_copied")
    psc_done, psc_copied, pex_done, pw_done = (
        sem(n) for n in ("psc_done", "psc_copied", "pex_done", "pw_done"))
    sl_turned, slot_copied, slots_done = sem("sl_turned"), sem("slot_copied"), sem("slots_done")
    oh_ready, oh_used, gh_copied = sem("oh_ready"), sem("oh_used"), sem("gh_copied")
    ssc_read = sem("ssc_read")
    ss_free = sem("ss_free")
    eu_in = [sem(f"eu_in{n}") for n in range(2)]
    e_out = [sem(f"e_out{n}") for n in range(2)]
    ea_in, v_lo2 = sem("ea_in"), sem("v_lo2")
    u_in = [sem(f"u_in{n}") for n in range(4)]
    vv_in = [[sem(f"vv_in{h}_{n}") for n in range(4)] for h in range(2)]
    g_out = [sem(f"g_out{n}") for n in range(2)]
    g_in, v_hi, v_lo = sem("g_in"), sem("v_hi"), sem("v_lo")
    x_out, x_back, gb_back, ga_back, gb_used = (
        sem(n) for n in ("x_out", "x_back", "gb_back", "ga_back", "gb_used"))
    sf_out = [sem(f"sf_out{n}") for n in range(2)]
    mw_hi, mw_lo = sem("mw_hi"), sem("mw_lo")
    in_hi, in_lo = sem("in_hi"), sem("in_lo")
    w_hi, w_lo = sem("w_hi"), sem("w_lo")
    u_turned, ut_hi, ut_lo = sem("u_turned"), sem("ut_hi"), sem("ut_lo")
    s_blk, gelu_done, aj_done = sem("s_blk"), sem("gelu_done"), sem("aj_done")
    o_done, o_added, xs_done = sem("o_done"), sem("o_added"), sem("xs_done")
    y_turned, y_act, y_dve = sem("y_turned"), sem("y_act"), sem("y_dve")
    y_out = [sem(f"y_out{n}") for n in range(2)]
    dve_ch = sem("dve_ch")

    w_in_v = w_in.rearrange("(k p) c -> p k c", p=P)
    w_mod_v = w_mod.rearrange("(k p) c -> p k c", p=P)
    w_proj_v = w_proj.rearrange("(k p) c -> p k c", p=P)
    w_out_v = w_out.rearrange("(k p) c -> p k c", p=P)
    w_pq_v = w_pq.rearrange("(k p) c -> p k c", p=P)
    u_v = peer_u.rearrange("(i j) d -> j i d", j=NE)
    v_v = peer_v.rearrange("(i j) d -> j i d", j=NE)

    GROUPS = NE // 4
    FULL = GROUPS - EARLY
    EB = 16 * EARLY
    GCHUNKS = T // GTOK
    GBODIES = T // (2 * GTOK)
    K_UNITS = 11
    assert T == (2 * GBODIES + 1) * GTOK and K_UNITS + GBODIES + 1 == 2 * EARLY
    ROPES = 37

    block = ctx.enter_context(nc.Block())

    @block.sync
    def _(sp):
        sp.dma_start(CTOK[0:1], c_p).then_inc(c_in, 16)
        sp.dma_start(CTOK[1:NC], c_s).then_inc(c_in, 16)
        sp.dma_start(keep[:], keep_d).then_inc(keep_in, 16)
        for u in range(4):
            sp.dma_start(ring[u][:], w_mod_v[:, :, 256 * u:256 * (u + 1)]).then_inc(wload[u], 16)
        with sp.Fori(1, 12) as i:
            for u in range(4):
                sp.wait_ge(gemm_done, 4 * i + u - 3)
                sp.dma_start(ring[u][:], w_mod_v[:, :, bass.ds((4 * i + u) * 256, 256)]).then_inc(wload[u], 16)

        def stream(unit0, src, col, first, last):
            n = chunk_of(split_of(unit0))
            with sp.Fori(first, last) as i:
                for u in range(4):
                    sp.wait_ge(gemm_done, units_done(n + 4 * first + u - 4) - 4 * first + 4 * i)
                    sp.dma_start(RAW[(n + u) % 4][:], src[:, :, bass.ds(512 * i + col + 128 * u, 128)])\
                        .then_inc(wload[(n + u) % 4], 16)

        def one(unit, src, col):
            n = chunk_of(split_of(unit))
            sp.wait_ge(gemm_done, units_done(n - 4))
            sp.dma_start(RAW[n % 4][:], src[:, :, col:col + 128]).then_inc(wload[n % 4], 16)

        def gate(unit, tile):
            one(unit, w_in_v, C_GB + 128 * tile if tile < KT else C_GA + 128 * (tile - KT))

        one(U_IK, w_in_v, C_IK)
        one(U_IK + 1, w_in_v, C_IK + 128)
        stream(U_K, w_in_v, C_K, 0, 1)
        stream(U_V, w_in_v, C_V, 0, 1)
        for u in range(4):
            one(U_IQ + u, w_in_v, C_IQ + 128 * u)
        stream(U_IQ, w_in_v, C_IQ, 1, 4)
        stream(U_G1, w_in_v, C_GB, 0, 2)
        stream(U_Q, w_in_v, C_Q, 0, 4)
        for u in range(2):
            gate(U_G2 + u, G2 + u)
        for u in range(2):
            gate(U_G3 + u, G3 + u)
        sp.wait_ge(kv_out, 16 * 9)
        sp.wait_ge(rope_done, ROPES)
        sp.wait_ge(pages_in, 16)

        def sequence_pages(b):
            if b >= 2:
                sp.wait_ge(so_done, b - 1)
            for n in range(2):
                at = bass.ds(sp.value_load(pages[0:1, 2 * b + n:2 * b + n + 1], min_val=0, max_val=NPOOL - 1), 1)
                sp.dma_start(kpg[b % 2][:, n], cache_k[at].rearrange("a s h d -> (a s) (h d)")).then_inc(kvp_in[b % 2], 16)
                sp.dma_start(vpg[b % 2][:, n], cache_v[at].rearrange("a s h d -> (a s) (h d)")).then_inc(kvp_in[b % 2], 16)

        sequence_pages(0)
        sequence_pages(1)
        for u in range(2, 8):
            gate(U_G3 + u, G3 + u)
        for u in range(4):
            gate(U_G4 + u, G4 + u)
        for b in range(NB):
            if b < 4:
                gate(U_G4 + b + 4, G4 + b + 4)
            else:
                one(U_P + b - 4, w_in_v, C_P + 128 * (b - 4))
            if b + 2 < NB:
                sequence_pages(b + 2)
        sp.wait_ge(so_copied, NB)
        sp.dma_start(STT[0:NB * NPRE], state.rearrange("b s c -> (b s) c")).then_inc(st_in, 16)
        for b in range(NB):
            sp.dma_start(ps_s[b, 0:NPRE - NT], state[b, NT:NPRE]).then_inc(ps_out, 16)
        stream(U_P, w_in_v, C_P, 1, 2)
        for u in range(4):
            gate(U_G5 + u, G5 + u)
        sp.wait_ge(ps_staged, 1)
        sp.dma_start(ps_p[0], PST[0:NPRE]).then_inc(ps_out, 16)
        sp.wait_ge(ps_out, 16 * (NB + 1))
        sp.wait_ge(ps_staged, 2)
        for b in range(NB):
            sp.dma_start(ps_s[b, NPRE - NT:NPRE], PST[NT * b:NT * (b + 1)]).then_inc(ps_out, 16)
        for u in range(4, 6):
            gate(U_G5 + u, G5 + u)
        sp.wait_ge(ps_out, 16 * (2 * NB + 1))
        sp.wait_ge(gemm_done, units_done(K_POOL - 4))
        slot = ring[K_POOL % 4][:].rearrange("p k c -> p (k c)").rearrange("p (g c) -> p g c", g=8)
        sp.dma_start(slot, w_pool.rearrange("g (k p) c -> p (g k) c", p=P)).then_inc(wload[K_POOL % 4], 16)
        one(U_PROJ, w_proj_v, 0)
        one(U_PROJ + 1, w_proj_v, 128)
        one(U_PROJ + 2, w_proj_v, 256)
        sp.wait_ge(gemm_done, U_POOL)
        for n in range(2):
            sp.wait_ge(sf_out[n], 16 * (KT + 1))
        sp.wait_ge(pooled_done, 1)
        sp.dma_start(GBS[:], s_dram[0:KT].rearrange("k p t -> p k t")).then_inc(gb_back, 16)
        sp.dma_start(S2[:], s_dram[KT:2 * KT].rearrange("k p t -> p k t")).then_inc(ga_back, 16)
        one(U_PROJ + 3, w_proj_v, 384)
        stream(U_PROJ, w_proj_v, 0, 1, 2)
        sp.wait_ge(gb_used, 1)
        sp.dma_start(X[:], x_dram).then_inc(x_back, 16)
        stream(U_PROJ, w_proj_v, 0, 2, 4)
        stream(U_OUT, w_out_v, 0, 0, 4)
        stream(U_PQ, w_pq_v, 0, 0, 4)
        sp.wait_ge(gemm_evac, U_OUT + 16)
        sp.dma_start(KNAT[:], pkeys.rearrange("h p k c -> k (h p) c")).then_inc(keys_in, 16)
        sp.wait_ge(gemm_done, U_PQ + 16)
        for n in range(2):
            sp.dma_start(EUB[n][:], u_v[4 * FULL + n]).then_inc(eu_in[n], 16)

        def early_out(i, t):
            sp.wait_ge(gelu_done, 2 * i + t + 2)
            dst = e_dram[bass.ds(2 * i + t, 1)].rearrange("a p t -> (a p) t")
            sp.dma_start(dst, EACT[t % 2][:]).then_inc(e_out[t % 2], 16)

        with sp.Fori(0, 2 * EARLY - 1) as i:
            for n in range(2):
                sp.wait_ge(u_turned, 8 * i + 4 * (n + 1) + 1)
                sp.dma_start(EUB[n][:], u_v[bass.ds(2 * i + 4 * FULL + 2 + n, 1)].rearrange("a i d -> (a i) d")).then_inc(eu_in[n], 16)
                early_out(i, n)

        def values(h, jj, tile):
            sp.dma_start(VRAW[h][jj][:], v_v[bass.ds(tile, 1), :, h * D // 2:(h + 1) * D // 2]
                         .rearrange("a i d -> (a i) d")).then_inc(vv_in[h][jj], 16)

        def weights(i):
            sp.dma_start(GH[:].rearrange("p c j t -> p c (j t)"),
                         g_dram[:, :, bass.ds(4 * i, 4)].rearrange("c p j t -> p c (j t)")).then_inc(g_in, 16)

        sp.wait_ge(slots_done, 5)
        for jj in range(4):
            sp.dma_start(UB[jj][:], u_v[jj]).then_inc(u_in[jj], 16)
        for n in range(2):
            early_out(0, 4 * EARLY - 2 + n)
        sp.wait_ge(s_blk, EB + 1)
        for jj in range(4):
            values(0, jj, jj)
        sp.wait_ge(g_out[0], 16 * (GBODIES + 2))
        sp.wait_ge(g_out[1], 16 * (GBODIES + 1))
        weights(0)
        for jj in range(4):
            values(1, jj, jj)
        with sp.Fori(1, FULL) as i:
            for jj in range(4):
                sp.wait_ge(u_turned, EB + 16 * i + 4 * jj - 12 + 1)
                sp.dma_start(UB[jj][:], u_v[bass.ds(4 * i + jj, 1)].rearrange("a i d -> (a i) d")).then_inc(u_in[jj], 16)
            sp.wait_ge(aj_done, 4 * i + 1)
            weights(i)
            for h in range(2):
                sp.wait_ge(o_done, 16 * i - 8 + 8 * h + 1)
                for jj in range(4):
                    values(h, jj, 4 * i + jj)
        for n in range(2):
            sp.wait_ge(e_out[n], 16 * (2 * EARLY + 1))

        def scored(i):
            sp.wait_ge(aj_done, 4 * i + 1)
            weights(i)
            sp.dma_start(EA[:], e_dram[bass.ds(4 * i - 4 * FULL, 4)].rearrange("j p t -> p j t")).then_inc(ea_in, 16)

        def scored_values(i, h):
            sp.wait_ge(o_done, 16 * i - 8 + 8 * h + 1)
            for jj in range(4):
                values(h, jj, 4 * i + jj)

        scored(FULL)
        with sp.Fori(FULL, GROUPS - 1) as i:
            scored_values(i, 0)
            scored(i + 1)
            scored_values(i, 1)
        scored_values(GROUPS - 1, 0)
        scored_values(GROUPS - 1, 1)

    @block.gpsimd
    def _(pool):
        pool.dma_start(VA[0:96], b_mod.rearrange("(a b) -> a b", b=P)).then_inc(vec_in, 16)
        pool.dma_start(VA[96:97], q_g.rearrange("(a b) -> a b", b=P)).then_inc(vec_in, 16)
        pool.dma_start(VA[97:98], k_g.rearrange("(a b) -> a b", b=P)).then_inc(vec_in, 16)
        for n, v in enumerate((norm1_g, norm2_g, pool_scale)):
            pool.dma_start(VB[16 * n:16 * (n + 1)], v.rearrange("(a b) -> a b", b=P)).then_inc(vec_in, 16)
        pool.dma_start(XTOK[0][:], x_p[0, 0:128]).then_inc(x_in, 16)
        pool.dma_start(XTOK[1][:], x_p[0, 128:256]).then_inc(x_in, 16)
        pool.dma_start(XTOK[2][0:TS], x_s.rearrange("b t d -> (b t) d")).then_inc(x_in, 16)
        pool.dma_start(mix[:], mix_d).then_inc(mix_in, 16)
        pool.dma_start(pages[:, 0:PAGES], ptab.rearrange("b n -> (b n)").rearrange("(a n) -> a n", a=1)).then_inc(pages_in, 16)
        pool.wait_ge(x_copied, 12)
        pool.dma_start(x_dram, X[:]).then_inc(x_out, 16)
        pool.wait_ge(pages_in, 16)
        pool.wait_ge(mod_done, 48)
        page = []
        for n in range(PAGES):
            page.append(pool.value_load(pages[0:1, n:n + 1], min_val=0, max_val=NPOOL - 1))
            pool.dma_start(IPG[:, n], cache_ik[bass.ds(page[n], 1)].rearrange("a s d -> (a s) d")).then_inc(ipg_in, 16)
        def weight_lo(n, i=0):
            slot = chunk_of(n) % 4
            pool.wait_ge(w_hi, 4 * i + n + 1)
            pool.tensor_tensor(WL[slot][:], RAW[slot][:], WH[slot][:].bitcast(F32), ALU.subtract).then_inc(w_lo, 1)

        before = split_of(U_PROJ)
        with pool.Fori(0, before // 4) as i:
            for n in range(4):
                weight_lo(n, i)
        for n in range(before // 4 * 4, before):
            weight_lo(n)
        with pool.Fori(0, 12) as i:
            for n in range(4):
                weight_lo(before + n, i)
        with pool.Fori(0, 2 * EARLY) as i:
            for c in range(8):
                pool.wait_ge(ut_hi, 8 * i + c + 1)
                pool.wait_ge(s_blk, 8 * i + max(c - 3, 0) + 1)
                pool.tensor_tensor(EUTL[c % 4][:], EUT[c % 2][:], EUTH[c % 4][:].bitcast(F32), ALU.subtract)\
                    .then_inc(ut_lo, 1)
        for g0, g1, tiles in ((0, FULL, range(4)), (FULL, GROUPS, (0, 2))):
            with pool.Fori(g0, g1) as i:
                for h in range(2):
                    for jj in tiles:
                        pool.wait_ge(v_hi, 8 * i + 4 * h + jj + 1)
                        pool.tensor_tensor(VL[h][jj][:], VRAW[h][jj][:], VH[h][jj][:].bitcast(F32), ALU.subtract)\
                            .then_inc(v_lo, 1)
        for tt, (t0, nt) in enumerate(TILES):
            pool.wait_ge(y_act, tt + 1)
            pool.wait_ge(y_dve, tt + 1)
            dst = y_p[0, t0:t0 + nt] if tt < 2 else y_s.rearrange("b t d -> (b t) d")
            pool.dma_start(dst, YS[tt % 2][0:nt]).then_inc(y_out[tt % 2], 16)
        pool.wait_ge(y_out[0], 32)
        pool.wait_ge(y_out[1], 16)

    @block.tensor
    def _(pe):
        mm, turn = nc.tensor.matmul, nc.tensor.transpose
        for s_, n in ((al_done, 1), (pt_turned, 1), (ao_done, 1), (oh_used, 2), (u_turned, 1), (s_blk, 1),
                      (o_done, 1)):
            pe.sem_inc(s_, n)

        def split_gemm(unit, i, x_hi, x_lo, rows=P, quarters=None):
            pe.wait_ge(w_lo, split_of(unit) + 1 + i)
            pe.wait_ge(gemm_evac, unit - 3 + i)
            n = chunk_of(split_of(unit)) % 4
            out = bank[unit % 4][:, 0:T]
            for k in range(KT):
                if quarters is not None and k % 4 == 0:
                    pe.wait_ge(in_lo, quarters + k // 4 + 1)
                mm(out, WH[n][:, k], x_hi[:, k], start=(k == 0), stop=False)
                mm(out, WH[n][:, k], x_lo[:, k], start=False, stop=False)
                last = mm(out, WL[n][:, k], x_hi[:, k], start=False, stop=(k == KT - 1))
            last.then_inc(gemm_done, 1)

        def from_h(unit, i=0, quarters=None):
            split_gemm(unit, i, XH, HL, quarters=quarters)

        pe.wait_ge(keep_in, 16)
        pe.wait_ge(c_in, 32)
        for k in range(KT):
            last = turn(bank[7][:, NC * k:NC * (k + 1)], CTOK[0:NC, 128 * k:128 * (k + 1)], ident[0:NC, 0:NC])
        last.then_inc(c_turned, 1)

        pe.wait_ge(vec_in, 96)
        turn(bank[6][:, 0:98], VA[0:98], ident[0:98, 0:98])
        turn(bank[6][:, 98:146], VB[0:48], ident[0:48, 0:48]).then_inc(v_turned, 1)
        pe.wait_ge(c_silu, 3)
        pe.wait_ge(v_copied, 1)

        def turn_rows(u, i):
            pe.wait_ge(gemm_evac, u + 1 + 12 * i)
            if u > 1 or not isinstance(i, int):
                pe.wait_ge(mod_done, u - 1 + 12 * i)
            for a in range(2):
                last = turn(bank[4 + u % 2][:, 128 * a:128 * (a + 1)], MR[u % 2][:, 128 * a:128 * (a + 1)], ident)
            last.then_inc(mod_turned, 1)

        def mod_units(i):
            for c in range(12):
                pe.wait_ge(mw_lo, c + 1 + 12 * i)
                if c > 3 or not isinstance(i, int):
                    pe.wait_ge(gemm_evac, c - 3 + 12 * i)
                out = bank[c % 4][0:CPAD, 0:256]
                for k in range(KT):
                    mm(out, CSH[:, k], MWH[c % 3][:, k], start=(k == 0), stop=False)
                    mm(out, CSL[:, k], MWH[c % 3][:, k], start=False, stop=False)
                    last = mm(out, CSH[:, k], MWL[c % 4][:, k], start=False, stop=(k == KT - 1))
                last.then_inc(gemm_done, 1)
                if c > 1 or not isinstance(i, int):
                    turn_rows(c - 2, i)

        mod_units(0)
        pe.wait_ge(x_in, 48)
        n = 0
        for tt, (t0, nt) in enumerate(TILES):
            for q in range(4):
                if n >= 2:
                    pe.wait_ge(x_copied, n - 1)
                for a in range(4):
                    last = turn(bank[6 + n % 2][:].rearrange("p (a t) -> p a t", a=4)[:, a, 0:nt],
                                XTOK[tt][0:nt, 128 * (4 * q + a):128 * (4 * q + a + 1)], ident[0:nt, 0:nt])
                last.then_inc(x_turned, 1)
                n += 1
        with pe.Fori(1, 4) as i:
            mod_units(i)
        turn_rows(46, 0)
        turn_rows(47, 0)

        for k in range(KT):
            if k % 4 == 0:
                pe.wait_ge(sq_done, k // 4 + 1)
            last = mm(bank[6][:, 0:T], ones, H[:, k], start=(k == 0), stop=(k == KT - 1))
        last.then_inc(ssq_done, 1)
        pe.wait_ge(mix_in, 16)

        def rotary(r, unit, normed, i=0):
            pe.wait_ge(gemm_evac, unit + 1 + i)
            if r:
                pe.wait_ge(rope_done, r - 1 + i)
            last = mm(bank[4 + r % 2][:, 0:T], mix[:, M_ROT:M_ROT + 128], raw[r % 4][:], start=True, stop=True)
            if normed:
                last = mm(bank[6 + r % 2][:, 0:T], ones, sq[r % 2][:], start=True, stop=True)
            last.then_inc(rot_done, 1)

        from_h(U_IK, quarters=0)
        from_h(U_IK + 1)
        rotary(0, U_IK, False)
        for u in range(4):
            from_h(U_K + u)
            if u:
                rotary(u, U_K + u - 1, True)
        for u in range(4):
            from_h(U_V + u)
            if u == 0:
                rotary(4, U_K + 3, True)
        def rotated_units(unit0, r0, normed):
            for u in range(4):
                from_h(unit0 + u)
                if u:
                    rotary(r0 + u - 1, unit0 + u - 1, normed)
            with pe.Fori(1, 4) as i:
                for u in range(4):
                    from_h(unit0 + u, 4 * i)
                    rotary(r0 + u - 1, unit0 + u - 1, normed, 4 * i)

        rotated_units(U_IQ, 5, False)
        from_h(U_G1)
        rotary(20, U_IQ + 15, False)
        pe.wait_ge(rope_done, 21)
        for tt in range(2):
            last = turn(bank[7][:, 16 * tt:16 * (tt + 1)], iwT[0:16, 128 * tt:128 * (tt + 1)], ident[0:16, 0:16])
        last.then_inc(iw_turned, 1)
        pe.wait_ge(iw_done, 1)
        mm(bank[7][0:64, 0:TS], mix[0:16, M_E16:M_E16 + 64], iwT[0:16, TP:T], start=True, stop=True).then_inc(wz_mm, 1)

        def turn_out(n):
            t0, nt = TILES[n // 3]
            which = n % 3
            if n:
                pe.wait_ge(kv_staged, n)
            for g in range(1 if which == 2 else 4):
                src = (kTt[:, g], vTt[:, g], ikT[:])[which]
                last = turn(bank[7][0:nt, 128 * g:128 * (g + 1)], src[:, t0:t0 + nt], ident)
            last.then_inc(kv_turned, 1)

        def sum_heads(b):
            pe.wait_ge(sl_relu, b + 1)
            mm(bank[6][0:TS, 0:LS], WZ[:, 32 * b:32 * (b + 1)], RL[b % 2][:], start=(b == 0), stop=(b == NB - 1))\
                .then_inc(ssc_mm, 1)

        for b in range(NB):
            if b == 0:
                pe.wait_ge(ipg_in, 16 * PAGES)
            else:
                pe.wait_ge(ikb_done, 3 * b)
            for n in range(2):
                last = turn(bank[4][:, 128 * n:128 * (n + 1)], IPG[:, 2 * b + n], ident)
            last.then_inc(ik_turned, 1)
            if b:
                from_h(U_G1 + b)
            if b == 1:
                pe.wait_ge(wz_done, 2)
            if b:
                turn_out(b - 1)
                sum_heads(b - 1)
            pe.wait_ge(ikb_done, 3 * (b + 1))
            mm(bank[5][0:64, 0:LS], IQB[b % 2][:], IKB[b % 2][:], start=True, stop=True)\
                .then_inc(sl_done, 1)
        turn_out(NB - 1)
        sum_heads(NB - 1)
        turn_out(NB)
        for n in range(8):
            h, tt = n // 2, n % 2
            if n == 1:
                pe.wait_ge(ssc_read, 1)
                pe.wait_ge(kv_staged, NB + 1)
            pe.wait_ge(il_used, n if n > 1 else 1)
            for a in range(4):
                last = mm(bank[4 + 2 * tt + a // 2][:, 256 * (a % 2):256 * (a % 2 + 1)],
                          S1[:, 4 * h + a, 128 * tt:128 * (tt + 1)], ikT[:, 0:TP], start=True, stop=True)
            last.then_inc(il_done, 1)
        pe.wait_ge(il_used, 8 + 1)

        rotated_units(U_Q, 21, True)
        from_h(U_G2)
        rotary(36, U_Q + 15, True)
        from_h(U_G2 + 1)
        pe.wait_ge(rope_done, ROPES)

        with pe.Fori(0, 2) as i:
            for k in range(2):
                pe.wait_ge(ag_ready, 4 * i + 2 * k + 2)
                for tt in range(2):
                    S = 128 * (tt + 1)
                    step = 4 * i + 2 * k + tt
                    pe.wait_ge(al_used, step + 1)
                    for a in range(4):
                        last = mm(bank[4 + a // 2][:, 256 * (a % 2):256 * (a % 2) + S], QG[:, a, 128 * tt:128 * (tt + 1)],
                                  kTt[:, bass.ds(2 * i + k, 1), 0:S].rearrange("p a s -> p (a s)"), start=True, stop=True)
                    last.then_inc(al_done, 1)
                    from_h(U_G3 + 2 * k + tt, 4 * i)
                    pe.wait_ge(al_prob, step + 1)
                    for sb in range(tt + 1):
                        pe.wait_ge(pt_copied, 6 * i + 3 * k + tt + 1)
                        for a in range(4):
                            last = turn(bank[6 - sb][:, 128 * a:128 * (a + 1)], E4[:, a, 128 * sb:128 * (sb + 1)], ident)
                        last.then_inc(pt_turned, 1)
                    pe.wait_ge(pt_copied, 6 * i + 3 * k + 2 * tt + 1 + 1)
                    pe.wait_ge(ao_copied, step + 1)
                    for sb in range(tt + 1):
                        last = mm(bank[7][:], VG[:, sb], PT[:, sb].rearrange("p a t -> p (a t)"),
                                  start=(sb == 0), stop=(sb == tt))
                    last.then_inc(ao_done, 1)
        pe.wait_ge(ao_copied, 8 + 1)

        for b in range(NB):
            pe.wait_ge(kvp_in[b % 2], 64 * (b // 2 + 1))
            if b:
                pe.wait_ge(sp_copied, b)
                pe.wait_ge(so_copied, b)
            for n in range(2):
                for g in range(4):
                    last = turn(bank[4 + n][:, 128 * g:128 * (g + 1)], kpg[b % 2][:, n, 128 * g:128 * (g + 1)], ident)
                last.then_inc(sk_turned, 1)
            pe.wait_ge(sk_copied, 3 * (b + 1))
            pe.wait_ge(sq_ready, b + 1)
            mm(bank[6][:, 0:LS], mix[0:TS, M_REP + 128 * b:M_REP + 128 * (b + 1)], smb[:], start=True, stop=False,
               skip_group_check=True)
            for g in range(4):
                last = mm(bank[6][32 * g:32 * g + 32, 0:LS], QSB[b % 2][:, g], KTB[:, g], start=False, stop=True,
                          skip_group_check=True)
            last.then_inc(sal_done, 1)
            for g in range(4):
                last = turn(bank[5][0:NT, 128 * g:128 * (g + 1)], vTt[:, g, TP + NT * b:TP + NT * (b + 1)], ident)
            from_h(U_G4 + b)
            pe.wait_ge(sal_prob, b + 1)
            for n in range(2):
                turn(bank[7][:, 128 * n:128 * (n + 1)], EN[:, 128 * n:128 * (n + 1)], ident)
            turn(bank[7][0:NT, 256:384], EN[:, PAST:LS], ident).then_inc(sp_turned, 1)
            pe.wait_ge(sp_copied, b + 1)
            for g in range(4):
                o = bank[4][:, 16 * g:16 * (g + 1)]
                for n in range(2):
                    mm(o, vpg[b % 2][:, n, 128 * g:128 * (g + 1)], PTB[:, n, 32 * g:32 * g + 16], start=(n == 0), stop=False)
                last = mm(o, VNB[0:NT, 128 * g:128 * (g + 1)], PTN[0:NT, 32 * g:32 * g + 16], start=False, stop=True)
            last.then_inc(so_done, 1)

        for u in range(8):
            from_h(U_P + u)
        pe.wait_ge(st_in, 16)
        for n in range(2):
            for a in range(4):
                last = turn(bank[4 + n][:, 120 * a:120 * (a + 1)], STT[0:120, 128 * (4 * n + a):128 * (4 * n + a + 1)], ident[0:120, 0:120])
            last.then_inc(st_turned, 1)
        pe.wait_ge(gemm_evac, U_P + 8)
        pe.wait_ge(st_copied, 2)
        for a in range(8):
            last = turn(bank[6 + a // 4][0:NPRE, 128 * (a % 4):128 * (a % 4 + 1)], PA[:, a, PADP - NPRE:PADP], ident)
        last.then_inc(ps_turned, 1)
        for a in range(8):
            last = turn(bank[4 + a // 4][0:TS, 128 * (a % 4):128 * (a % 4 + 1)], PNEW[:, a], ident)
        last.then_inc(ps_turned, 1)
        for u in range(6):
            from_h(U_G5 + u)
        pe.wait_ge(pooled_done, 1)
        pe.wait_ge(wload[K_POOL % 4], 16 * (K_POOL // 4 + 1))
        slot = ring[K_POOL % 4][:].rearrange("p k c -> p (k c)").rearrange("p (g k c) -> p g k c", g=4, k=2)
        for u in range(16):
            g = u // 4
            pe.wait_ge(gemm_evac, U_POOL + u - 3)
            for k in range(2):
                last = mm(bank[(U_POOL + u) % 4][:, 0:T], slot[:, g, k, 128 * (u % 4):128 * (u % 4 + 1)],
                          POOLED[:, 2 * g + k], start=(k == 0), stop=(k == 1))
            last.then_inc(gemm_done, 1)

        def split_pass(unit0, x_hi, x_lo, quarters=None):
            split_gemm(unit0, 0, x_hi, x_lo, quarters=quarters)
            for u in range(1, 4):
                split_gemm(unit0 + u, 0, x_hi, x_lo)
            with pe.Fori(1, 4) as i:
                for u in range(4):
                    split_gemm(unit0 + u, 4 * i, x_hi, x_lo)

        split_pass(U_PROJ, AOH, AOL, 4)
        pe.wait_ge(gemm_evac, U_OUT)
        def add_square(u, i=0, **kw):
            pe.wait_ge(sq_done, 4 + u + 1 + i)
            return mm(bank[6][:, 0:T], ones, H[:, bass.ds(i + u, 1)].rearrange("p a t -> p (a t)"), **kw)

        for u in range(4):
            split_gemm(U_OUT + u, 0, MGH, MGL)
            if u:
                add_square(u - 1, start=(u == 1), stop=False)
        with pe.Fori(1, 4) as i:
            for u in range(4):
                split_gemm(U_OUT + u, 4 * i, MGH, MGL)
                add_square(u - 1, 4 * i, start=False, stop=False)
        add_square(KT - 1, start=False, stop=True).then_inc(ssq_done, 1)
        split_pass(U_PQ, HH, HL, 8)

        pe.wait_ge(keys_in, 16)
        for n in range(4):
            for a in range(4):
                last = turn(bank[4 + n][:, 128 * a:128 * (a + 1)], KNAT[:, 4 * n + a], ident)
        last.then_inc(keys_turned, 1)
        pe.wait_ge(gemm_evac, U_PQ + 16)
        pe.wait_ge(keys_copied, 1)

        def early_turn(i, c):
            if c % 4 == 0:
                pe.wait_ge(eu_in[c // 4 % 2], 16 * i + 16 * (c // 8 + 1))
            pe.wait_ge(ut_lo, 8 * i + max(c - 3, 0) + 1)
            for k in range(4):
                f = 4 * (c % 4) + k
                last = turn(bank[c % 4][:, 128 * k:128 * (k + 1)], EUB[c // 4 % 2][:, 128 * f:128 * (f + 1)], ident)
            last.then_inc(u_turned, 1)

        def early_score(i, c):
            pe.wait_ge(ut_lo, 8 * i + c + 2)
            if c % 4 == 0:
                pe.wait_ge(gelu_done, 2 * i + max(c // 4 - 1, 0) + 1)
            out = bank[4 + c // 4 % 2][:, 0:T]
            for k in range(4):
                f = 4 * (c % 4) + k
                for n, (w, x) in enumerate(((EUTH, HH), (EUTH, HL), (EUTL, HH))):
                    last = mm(out, w[c % 4][:, k], x[:, f], start=(f + n == 0), stop=(f == KT - 1 and n == 2))
            last.then_inc(s_blk, 1)

        def early_step(i, c):
            if not isinstance(i, int) or c + 2 < EB:
                early_turn(i, c + 2)
            early_score(i, c)

        def early_units(first, count):
            with pe.Fori(0, count) as i:
                for c in range(8):
                    early_step(i, 8 * first + c)

        def key_scores(tt):
            t0, nt = TILES[tt]
            for half in range(2):
                if tt or half:
                    pe.wait_ge(psc_copied, 2 * tt + half)
                for a in range(8):
                    last = mm(bank[6 + a // 4][0:nt, 128 * (a % 4):128 * (a % 4 + 1)], S1[:, 8 * half + a, t0:t0 + nt],
                              KEYT[:, 8 * half + a], start=True, stop=True)
                last.then_inc(psc_done, 1)

        def slots(tt):
            nt = TILES[tt][1]
            pe.wait_ge(pw_done, tt + 1)
            pe.wait_ge(psc_copied, 2 * min(tt + 2, len(TILES)))
            for n, src in enumerate((ei, ej, wv)):
                flat = src[0:nt].rearrange("t h k -> t (h k)") if n == 2 else src[0:nt]
                last = turn(bank[6][:, 128 * n:128 * n + nt], flat, ident[0:nt, 0:nt])
            last.then_inc(sl_turned, 1)

        key_scores(0)
        early_turn(0, 0)
        early_turn(0, 1)
        early_units(0, 2)
        key_scores(1)
        early_units(2, 2)
        slots(0)
        early_units(4, 1)
        pe.wait_ge(slot_copied, 3)
        key_scores(2)
        early_units(5, 3)
        slots(1)
        early_units(8, K_UNITS - 8)
        pe.wait_ge(slot_copied, 6)
        slots(2)
        pe.wait_ge(slots_done, 5)

        def lay_out(i, n):
            pe.wait_ge(oh_ready, 16 * i + n + 1)
            pe.wait_ge(gh_copied, 16 * i + n + 1)
            par = n % 2
            out = bank[6 + par][:].rearrange("p (t j) -> p t j", t=4)
            for t in range(4):
                for k in range(3):
                    last = mm(out[:, t], OA[par][:, t // 2, :, t % 2], OBp[par][k][:, t // 2, :, t % 2],
                              start=(k == 0), stop=(k == 2))
            last.then_inc(oh_used, 1)

        with pe.Fori(0, GBODIES) as i:
            for c in range(8):
                lay_out(i, 2 * c)
                lay_out(i, 2 * c + 1)
                early_step(i, 8 * K_UNITS + c)
        for c in range(4):
            lay_out(0, 16 * GBODIES + 2 * c)
            lay_out(0, 16 * GBODIES + 2 * c + 1)
            for n in range(2):
                early_step(0, EB - 8 + 2 * c + n)
        pe.wait_ge(gh_copied, T // 4 + 2)

        def turn_u(i, b):
            jj, q = b // 4 % 4, b % 4
            if q == 0:
                pe.wait_ge(u_in[jj], 16 * i + 16 + 16 * (b // 16))
            pe.wait_ge(ut_lo, EB + 16 * i + max(b - 3, 0) + 1)
            for k in range(4):
                f = 4 * q + k
                last = turn(bank[b % 4][:, 128 * k:128 * (k + 1)], UB[jj][:, 128 * f:128 * (f + 1)], ident)
            last.then_inc(u_turned, 1)

        def score(i, b):
            jj, q = b // 4, b % 4
            pe.wait_ge(ut_lo, EB + 16 * i + b + 2)
            if q == 0:
                pe.wait_ge(gelu_done, 4 * EARLY + 4 * i + max(jj - 1, 0) + 1)
            out = bank[4 + jj % 2][:, 0:T]
            for k in range(4):
                f = 4 * q + k
                for n, (w, x) in enumerate(((UTH, HH), (UTH, HL), (UTL, HH))):
                    last = mm(out, w[b % 4][:, k], x[:, f], start=(f + n == 0), stop=(f == KT - 1 and n == 2))
            last.then_inc(s_blk, 1)

        def mix_values(i, scored=False, a_hi=AH, a_lo=AL):
            def products(m_, tiles):
                c0 = 128 * (m_ % 8)
                out = bank[6 + m_ % 2][:, 0:T]
                for jj in tiles:
                    vh, vl = (x[m_ // 8][jj][:, c0:c0 + 128] for x in (VH, VL))
                    mm(out, vh, a_hi[jj][:], start=(jj == 0), stop=False)
                    mm(out, vh, a_lo[jj][:], start=False, stop=False)
                    last = mm(out, vl, a_hi[jj][:], start=False, stop=(jj == 3))
                return last

            def half_ready(h):
                if scored:
                    pe.wait_ge(v_lo, 4 * FULL + 4 * i + 2 * h + 2)
                    pe.wait_ge(v_lo2, 4 * i + 2 * h + 2 - 4 * FULL)
                else:
                    pe.wait_ge(v_lo, 8 * i + 4 * h + 4)

            half_ready(0)
            early = 0 if scored else 2
            if not scored:
                pe.wait_ge(aj_done, 4 * i + 4)
                for m_ in range(2):
                    pe.wait_ge(o_added, 16 * i + 1)
                    products(m_, range(3))
            pe.wait_ge(aj_done, 4 * i + 5)
            for m_ in range(early):
                products(m_, (3,)).then_inc(o_done, 1)
            for m_ in range(early, KT):
                if m_ == 8:
                    half_ready(1)
                pe.wait_ge(o_added, 16 * i + max(m_ - 1, 0) + 1)
                products(m_, range(4)).then_inc(o_done, 1)

        turn_u(0, 0)
        turn_u(0, 1)
        with pe.Fori(0, FULL - 1) as i:
            for b in range(14):
                turn_u(i, b + 2)
                score(i, b)
            for b in (14, 15):
                score(i, b)
            for b in (16, 17):
                turn_u(i, b)
            mix_values(i)
        for b in range(16):
            if b < 14:
                turn_u(FULL - 1, b + 2)
            score(FULL - 1, b)
        mix_values(FULL - 1)
        with pe.Fori(0, EARLY // 2) as i:
            mix_values(2 * i + FULL, True, AH2, AL2)
            mix_values(2 * i + FULL + 1, True)
        pe.wait_ge(o_added, 16 * GROUPS + 1)
        pe.wait_ge(xs_done, 1)
        for tt, (t0, nt) in enumerate(TILES):
            if tt:
                pe.wait_ge(y_act, tt)
                pe.wait_ge(y_dve, tt)
            for k in range(KT):
                last = turn(bank[k // 4][0:nt, 128 * (k % 4):128 * (k % 4 + 1)], X[:, k, t0:t0 + nt], ident)
            last.then_inc(y_turned, 1)

    @block.scalar
    def _(act):
        for s_, n in ((pt_copied, 1), (gh_copied, 2), (gelu_done, 1), (g_out[0], 16), (g_out[1], 16),
                      (e_out[0], 16), (e_out[1], 16), (sf_out[0], 16), (sf_out[1], 16)):
            act.sem_inc(s_, n)
        run = nc.scalar.activation

        def evac(unit, out, src, func=ACT.Copy, **kw):
            act.wait_ge(gemm_done, unit + 1)
            run(out, src, func, **kw).then_inc(gemm_evac, 1)

        act.wait_ge(c_turned, 1)
        run(CT_[:], bank[7][:, 0:NC * KT].rearrange("p (k c) -> p k c", c=NC), ACT.Sigmoid).then_inc(c_silu, 1)
        act.wait_ge(v_turned, 1)
        run(VEC[:], bank[6][:, 0:146], ACT.Copy).then_inc(v_copied, 1)

        def mod_hi(c, i):
            act.wait_ge(wload[c % 4], 16 * (c // 4 + 1) + 48 * i)
            if c > 2 or not isinstance(i, int):
                act.wait_ge(gemm_done, c - 2 + 12 * i)
            for h in (slice(0, 8), slice(8, 16)):
                run(MWH[c % 3][:, h], ring[c % 4][:, h], ACT.Copy).then_inc(mw_hi, 1)

        def mod_rows(u, i):
            act.wait_ge(gemm_done, u + 1 + 12 * i)
            if u > 1 or not isinstance(i, int):
                act.wait_ge(mod_turned, u - 1 + 12 * i)
            run(MR[u % 2][0:NC], bank[u % 4][0:NC, 0:256], ACT.Copy).then_inc(gemm_evac, 1)

        def mod_units(i):
            for c in range(12):
                mod_hi(c, i)
                if c > 1 or not isinstance(i, int):
                    mod_rows(c - 2, i)

        mod_units(0)
        n = 0
        for tt, (t0, nt) in enumerate(TILES):
            for q in range(4):
                act.wait_ge(x_turned, n + 1)
                run(X[:, 4 * q:4 * q + 4, t0:t0 + nt],
                    bank[6 + n % 2][:].rearrange("p (a t) -> p a t", a=4)[:, :, 0:nt], ACT.Copy).then_inc(x_copied, 1)
                n += 1
        with act.Fori(1, 4) as i:
            mod_units(i)
        mod_rows(46, 0)
        mod_rows(47, 0)

        def root_mean_square(n):
            act.wait_ge(ssq_done, n + 1)
            run(n_s[:], bank[6][:, 0:T], ACT.Sqrt, bias=eps, scale=1.0 / D).then_inc(std_done, 1)

        def weight_hi(n, i=0):
            c = chunk_of(n)
            act.wait_ge(wload[c % 4], 16 * (c // 4 + 1) + 4 * i)
            run(WH[c % 4][:], RAW[c % 4][:], ACT.Copy).then_inc(w_hi, 1)

        def ahead(unit, i=0):
            if split_of(unit) + 2 < split_of(U_END):
                weight_hi(split_of(unit) + 2, i)

        def input_hi(out, src, normed=None):
            for q in range(4):
                if normed is not None:
                    act.wait_ge(norm_done, 4 * normed + q + 1)
                run(out[:, 4 * q:4 * q + 4], src[:, 4 * q:4 * q + 4], ACT.Copy).then_inc(in_hi, 1)

        def gate(unit, tile, i=0):
            act.wait_ge(gemm_done, unit + 1 + i)
            act.wait_ge(sf_out[tile % 2], 8 * (tile - tile % 2) + 16 + 8 * i)
            run(SF[tile % 2][:], bank[unit % 4][:, 0:T], ACT.Sigmoid).then_inc(gemm_evac, 1)
            act.wait_ge(gemm_evac, unit + 1 + i)
            act.dma_start(s_dram[bass.ds(tile + i, 1)].rearrange("a p t -> (a p) t"), SF[tile % 2][:])\
                .then_inc(sf_out[tile % 2], 16)

        act.wait_ge(x_copied, 12)
        for q in range(4):
            run(H[:, 4 * q:4 * q + 4], X[:, 4 * q:4 * q + 4], ACT.Square).then_inc(sq_done, 1)
        root_mean_square(0)
        weight_hi(0)
        weight_hi(1)
        act.wait_ge(x_out, 16)
        input_hi(XH, H, 0)

        def raw_unit(r, unit, g=None, i=0):
            ahead(unit, i)
            act.wait_ge(gemm_done, unit + 1 + i)
            if r > 3:
                act.wait_ge(rope_done, r - 3 + i)
            if g is not None:
                if r > 1:
                    act.wait_ge(rot_done, r - 1 + i)
                run(sq[r % 2][:], bank[unit % 4][:, 0:T], ACT.Square)
                run(raw[r % 4][:], bank[unit % 4][:, 0:T], ACT.Copy, scale=g).then_inc(gemm_evac, 1)
            else:
                run(raw[r % 4][:], bank[unit % 4][:, 0:T], ACT.Copy).then_inc(gemm_evac, 1)

        def root_mean(r, i=0):
            act.wait_ge(rot_done, r + 1 + i)
            if r > 1:
                act.wait_ge(rope_done, r - 1 + i)
            run(qks[r % 2][:], bank[6 + r % 2][:, 0:T], ACT.Sqrt, bias=eps, scale=1.0 / 128).then_inc(qk_std, 1)

        raw_unit(0, U_IK)
        ahead(U_IK + 1)
        evac(U_IK + 1, iwT[:], bank[(U_IK + 1) % 4][0:16, 0:T], scale=IW_SCALE)
        for u in range(4):
            raw_unit(1 + u, U_K + u, VEC[:, 97:98])
            if u:
                root_mean(u)
        for u in range(4):
            ahead(U_V + u)
            evac(U_V + u, vTt[:, u], bank[(U_V + u) % 4][:, 0:T])
            if u == 0:
                root_mean(4)
        with act.Fori(0, 2) as i:
            for u in range(8):
                raw_unit(5 + u, U_IQ + u, None, 8 * i)

        def stage_out(n):
            t0, nt = TILES[n // 3]
            which = n % 3
            act.wait_ge(kv_turned, n + 1)
            if n:
                act.wait_ge(kv_out, 16 * n)
            src = vN[:, n // 3] if which == 1 and n < 6 else stage[:]
            if n < 6:
                dst = ((k_p, v_p)[which][0, t0:t0 + nt].rearrange("s h d -> s (h d)") if which < 2
                       else ik_p[0, t0:t0 + nt])
            else:
                dst = ((k_s, v_s)[which].rearrange("b t h d -> (b t) (h d)") if which < 2
                       else ik_s.rearrange("b t d -> (b t) d"))
            w = dst.shape[1]
            run(src[0:nt, 0:w], bank[7][0:nt, 0:w], ACT.Copy).then_inc(kv_staged, 1)
            act.wait_ge(kv_staged, n + 1)
            act.dma_start(dst, src[0:nt, 0:w]).then_inc(kv_out, 16)

        ahead(U_G1)
        act.wait_ge(iw_turned, 1)
        run(iwN[:], bank[7][:, 0:32].rearrange("p (a b) -> p a b", a=2), ACT.Copy).then_inc(iw_done, 1)
        gate(U_G1, G1)
        for b in range(NB):
            act.wait_ge(ik_turned, b + 1)
            if b >= 2:
                act.wait_ge(sl_done, b - 1)
            run(IKB[b % 2][:, 0:PAST], bank[4][:, 0:256], ACT.Copy).then_inc(ikb_done, 1)
            if b == 0:
                act.wait_ge(rope_done, 21)
            run(IQB[b % 2][:].rearrange("p (h t) -> p h t", h=HQ), S1[:, :, TP + NT * b:TP + NT * (b + 1)], ACT.Copy)\
                .then_inc(ikb_done, 1)
            run(IKB[b % 2][:, PAST:LS], ikT[:, TP + NT * b:TP + NT * (b + 1)], ACT.Copy).then_inc(ikb_done, 1)
            if b:
                ahead(U_G1 + b)
                gate(U_G1 + b, G1 + b)
                stage_out(b - 1)
            act.wait_ge(sl_done, b + 1)
            if b >= 2:
                act.wait_ge(ssc_mm, b - 1)
            run(RL[b % 2][:], bank[5][0:64, 0:LS], ACT.Relu).then_inc(sl_relu, 1)
        stage_out(NB - 1)
        stage_out(NB)
        for u in range(4):
            raw_unit(21 + u, U_Q + u, VEC[:, 96:97])
            if u:
                root_mean(20 + u)
        with act.Fori(1, 4) as i:
            for u in range(4):
                raw_unit(21 + u, U_Q + u, VEC[:, 96:97], 4 * i)
                root_mean(20 + u, 4 * i)
        for u in range(2):
            ahead(U_G2 + u)
            gate(U_G2 + u, G2 + u)
            if u == 0:
                root_mean(36)
        with act.Fori(0, 2) as i:
            for k in range(2):
                act.wait_ge(ao_done, 4 * i + 2 * k + 1)
                run(VG[:], vN[:, :, bass.ds(256 * i + 128 * k, 128)], ACT.Copy).then_inc(ag_ready, 1)
                for tt in range(2):
                    S = 128 * (tt + 1)
                    step = 4 * i + 2 * k + tt
                    act.wait_ge(al_shift, step + 1)
                    for a in range(4):
                        last = run(E4[:, a, 0:S], E4[:, a, 0:S], ACT.Exp, bias=st1[:, a:a + 1], scale=ATT_SCALE,
                                   accum_out=st2[:, a:a + 1])
                    last.then_inc(al_exp, 1)
                    ahead(U_G3 + 2 * k + tt, 4 * i)
                    for sb in range(tt + 1):
                        act.wait_ge(pt_turned, 6 * i + 3 * k + tt + sb + 1 + 1)
                        act.wait_ge(ao_done, step + 1)
                        run(PT[:, sb], bank[6 - sb][:].rearrange("p (a t) -> p a t", a=4), ACT.Copy).then_inc(pt_copied, 1)
                    gate(U_G3 + 2 * k + tt, G3 + 2 * k + tt, 4 * i)
        for b in range(NB):
            for n in range(2):
                act.wait_ge(sk_turned, 2 * b + n + 1)
                if b:
                    act.wait_ge(sal_done, b)
                elif n == 0:
                    act.wait_ge(ao_copied, 8 + 1)
                run(KTB[:, :, 128 * n:128 * (n + 1)], bank[4 + n][:].rearrange("p (g s) -> p g s", g=4), ACT.Copy)\
                    .then_inc(sk_copied, 1)
            run(KTB[:, :, PAST:LS], kTt[:, :, TP + NT * b:TP + NT * (b + 1)], ACT.Copy).then_inc(sk_copied, 1)
            act.wait_ge(sal_max, b + 1)
            run(EN[:], bank[6][:, 0:LS], ACT.Exp, bias=sb1[:], scale=ATT_SCALE, accum_out=sb2[:]).then_inc(sal_exp, 1)
            ahead(U_G4 + b)
            act.wait_ge(sp_turned, b + 1)
            if b:
                act.wait_ge(so_done, b)
            run(VNB[:], bank[5][0:NT, :], ACT.Copy)
            run(PTN[:], bank[7][0:NT, 256:384], ACT.Copy)
            run(PTB[:], bank[7][:, 0:256].rearrange("p (n r) -> p n r", n=2), ACT.Copy).then_inc(sp_copied, 1)
            gate(U_G4 + b, G4 + b)
        act.wait_ge(ao_copied, 8 + 1)
        act.wait_ge(so_copied, NB)
        for u in range(8):
            ahead(U_P + u)
            act.wait_ge(gemm_done, U_P + u + 1)
            b_ = bank[(U_P + u) % 4]
            run(PA[:, u, NPRE:PADP], b_[:, 0:TP], ACT.Copy)
            run(PNEW[:, u], b_[:, TP:T], ACT.Copy)
            run(PA[:, u, PADP:PADT].rearrange("p (b s) -> p b s", b=NB)[:, :, NPRE:PADS],
                b_[:, TP:T].rearrange("p (b t) -> p b t", b=NB), ACT.Copy).then_inc(gemm_evac, 1)
        for n in range(2):
            act.wait_ge(st_turned, n + 1)
            for a in range(4):
                last = run(PA[:, 4 * n + a, PADP:PADT].rearrange("p (b s) -> p b s", b=NB)[:, :, 0:NPRE],
                           bank[4 + n][:, 120 * a:120 * (a + 1)].rearrange("p (b s) -> p b s", b=NB), ACT.Copy)
            last.then_inc(st_copied, 1)
        act.wait_ge(ps_turned, 1)
        run(PST[0:NPRE, 0:512], bank[6][0:NPRE, :], ACT.Copy)
        run(PST[0:NPRE, 512:1024], bank[7][0:NPRE, :], ACT.Copy).then_inc(ps_staged, 1)
        act.wait_ge(ps_turned, 2)
        act.wait_ge(ps_out, 16 * (NB + 1))
        run(PST[0:TS, 0:512], bank[4][0:TS, :], ACT.Copy)
        run(PST[0:TS, 512:1024], bank[5][0:TS, :], ACT.Copy).then_inc(ps_staged, 1)
        for u in range(6):
            ahead(U_G5 + u)
            gate(U_G5 + u, G5 + u)
        act.wait_ge(pooled_done, 1)
        for u in range(16):
            evac(U_POOL + u, S3[:, u], bank[(U_POOL + u) % 4][:, 0:T], scale=VEC[:, 130 + u:131 + u])
        act.wait_ge(gemm_done, U_POOL)
        input_hi(AOH, S1)
        with act.Fori(0, 4) as i:
            for u in range(4):
                ahead(U_PROJ + u, 4 * i)
        with act.Fori(0, 4) as i:
            for u in range(4):
                ahead(U_OUT + u, 4 * i)
                act.wait_ge(gemm_evac, U_OUT + u + 1 + 4 * i)
                at = bass.ds(4 * i + u, 1)
                run(H[:, at], X[:, at], ACT.Square).then_inc(sq_done, 1)
        root_mean_square(1)
        input_hi(HH, H, 1)

        def peer_query(u, i=0):
            act.wait_ge(gemm_done, U_PQ + u + 1 + 4 * i)
            run(S1[:, bass.ds(4 * i + u, 1)].rearrange("p a t -> p (a t)"), bank[(U_PQ + u) % 4][:, 0:T], ACT.Copy).then_inc(gemm_evac, 1)

        with act.Fori(0, 3) as i:
            for u in range(4):
                ahead(U_PQ + u, 4 * i)
                peer_query(u, i)
        for u in range(12, 16):
            ahead(U_PQ + u)
            act.wait_ge(gemm_done, U_PQ + u + 1)
            run(S1[:, u], bank[(U_PQ + u) % 4][:, 0:T], ACT.Copy).then_inc(gemm_evac, 1)
        act.wait_ge(keys_turned, 1)
        for n in range(4):
            last = run(KEYT[:, 4 * n:4 * n + 4], bank[4 + n][:].rearrange("p (a k) -> p a k", a=4), ACT.Copy)
        last.then_inc(keys_copied, 1)

        def early_hi(i, c):
            act.wait_ge(u_turned, 8 * i + c + 2)
            act.wait_ge(ut_lo, 8 * i + max(c - 1, 0) + 1)
            act.wait_ge(s_blk, 8 * i + max(c - 3, 0) + 1)
            src = bank[c % 4][:].rearrange("p (k i) -> p k i", k=4)
            run(EUT[c % 2][:], src, ACT.Copy)
            run(EUTH[c % 4][:], src, ACT.Copy).then_inc(ut_hi, 1)

        def early_gelu(i, t):
            act.wait_ge(s_blk, 8 * i + 4 * t + 5)
            act.wait_ge(e_out[t % 2], 16 * i + 16 * (t // 2) + 16)
            run(EACT[t % 2][:], bank[4 + t % 2][:, 0:T], ACT.Gelu).then_inc(gelu_done, 1)

        def early_step(i, c):
            if not isinstance(i, int) or c + 2 < EB:
                early_hi(i, c + 2)
            if c % 8 == 4:
                early_gelu(i, c // 4 - 1)
            if c % 8 == 7:
                early_gelu(i, c // 4)

        def early_units(first, count):
            with act.Fori(0, count) as i:
                for c in range(8):
                    early_step(i, 8 * first + c)

        def key_scores(tt):
            nt = TILES[tt][1]
            for half in range(2):
                act.wait_ge(psc_done, 2 * tt + half + 1)
                if tt:
                    act.wait_ge(ss_free, tt)
                for n in range(2):
                    a = 8 * half + 4 * n
                    last = run(SS[0:nt, a:a + 4], bank[6 + n][0:nt].rearrange("p (a k) -> p a k", a=4), ACT.Copy)
                last.then_inc(psc_copied, 1)

        def exponentials(tt):
            nt = TILES[tt][1]
            act.wait_ge(pex_done, 2 * tt + 1)
            run(wv[0:nt], wv[0:nt], ACT.Exp).then_inc(pex_done, 1)

        def slots(tt):
            t0, nt = TILES[tt]
            act.wait_ge(sl_turned, tt + 1)
            for n, out in enumerate((IB, JB, GF)):
                run(out[:, t0:t0 + nt], bank[6][:, 128 * n:128 * n + nt], ACT.Copy).then_inc(slot_copied, 1)

        key_scores(0)
        early_hi(0, 0)
        early_hi(0, 1)
        early_units(0, 2)
        key_scores(1)
        early_units(2, 2)
        exponentials(0)
        slots(0)
        early_units(4, 1)
        key_scores(2)
        early_units(5, 3)
        exponentials(1)
        slots(1)
        early_units(8, K_UNITS - 8)
        exponentials(2)
        slots(2)
        act.wait_ge(slots_done, 5)

        def lay_out(i, n):
            act.wait_ge(oh_used, 16 * i + n + 3)
            t0 = 4 * n % GTOK
            run(GCH[n // 8 % 2][:, :, t0:t0 + 4].rearrange("p j t -> p t j"),
                bank[6 + n % 2][:].rearrange("p (t j) -> p t j", t=4), ACT.Copy).then_inc(gh_copied, 1)

        def chunk_out(i, n, chunk):
            act.wait_ge(gh_copied, 16 * i + n + 3)
            act.dma_start(g_dram[bass.ds(chunk, 1)].rearrange("a p j t -> p (a j) t"), GCH[n // 8 % 2][:])\
                .then_inc(g_out[n // 8 % 2], 16)

        with act.Fori(0, GBODIES) as i:
            for c in range(8):
                if c % 4 == 0:
                    act.wait_ge(g_out[c // 4], 16 * i + 16)
                lay_out(i, 2 * c)
                lay_out(i, 2 * c + 1)
                if c % 4 == 3:
                    chunk_out(i, 2 * c + 1, 2 * i + c // 4)
                early_step(i, 8 * K_UNITS + c)
        act.wait_ge(g_out[0], 16 * (GBODIES + 1))
        for c in range(4):
            lay_out(0, 16 * GBODIES + 2 * c)
            lay_out(0, 16 * GBODIES + 2 * c + 1)
            if c == 3:
                chunk_out(0, 16 * GBODIES + 7, GCHUNKS - 1)
            for n in range(2):
                early_step(0, EB - 8 + 2 * c + n)
        act.wait_ge(g_out[1], 16 * (GBODIES + 1))

        def expert_hi(i, b):
            act.wait_ge(u_turned, EB + 16 * i + b + 2)
            act.wait_ge(s_blk, EB + 16 * i + max(b - 3, 0) + 1)
            run(UTH[b % 4][:], bank[b % 4][:].rearrange("p (k i) -> p k i", k=4), ACT.Copy).then_inc(ut_hi, 1)

        def gelu(i, jj):
            act.wait_ge(s_blk, EB + 16 * i + 4 * jj + 5)
            act.wait_ge(aj_done, 4 * i + max(jj - 1, 0) + 1)
            run(gt[jj % 2][:], bank[4 + jj % 2][:, 0:T], ACT.Gelu).then_inc(gelu_done, 1)

        def value_hi(i, h, jj):
            act.wait_ge(vv_in[h][jj], 16 * i + 16)
            act.wait_ge(o_done, 16 * i + 1)
            act.wait_ge(g_out[0], 16 * (GBODIES + 2))
            act.wait_ge(e_out[jj % 2], 16 * (2 * EARLY + 1))
            run(VH[h][jj][:], VRAW[h][jj][:], ACT.Copy).then_inc(v_hi, 1)

        def act_group(i, last):
            for b in range(14):
                expert_hi(i, b + 2)
                if b % 4 == 0 and b:
                    gelu(i, b // 4 - 1)
                if b >= 4 and b % 2 == 0:
                    n = (b - 4) // 2
                    if n < 4:
                        value_hi(i, 0, n)
            gelu(i, 3)
            if not last:
                expert_hi(i, 16)
                expert_hi(i, 17)
            for jj in range(4):
                value_hi(i, 1, jj)

        expert_hi(0, 0)
        expert_hi(0, 1)
        with act.Fori(0, FULL - 1) as i:
            act_group(i, False)
        act_group(FULL - 1, True)

        def scored_hi(i, h):
            for jj in range(4):
                act.wait_ge(vv_in[h][jj], 16 * i + 16)
                act.wait_ge(o_done, 16 * i - 8 + 8 * h + 1)
                run(VH[h][jj][:], VRAW[h][jj][:], ACT.Copy).then_inc(v_hi, 1)

        scored_hi(FULL, 0)
        with act.Fori(FULL, GROUPS - 1) as i:
            scored_hi(i, 1)
            scored_hi(i + 1, 0)
        scored_hi(GROUPS - 1, 1)
        for tt, (t0, nt) in enumerate(TILES):
            act.wait_ge(y_turned, tt + 1)
            if tt == 2:
                act.wait_ge(y_out[0], 16)
            for n in range(2):
                last = run(YS[tt % 2][0:nt, 512 * n:512 * (n + 1)], bank[n][0:nt, :], ACT.Copy)
            last.then_inc(y_act, 1)

    @block.vector
    def _(dve):
        v = nc.vector
        ch = Chain(dve, dve_ch)
        for s_ in (il_used, al_used, ao_copied, ut_lo, aj_done, o_added):
            dve.sem_inc(s_, 1)

        def b3(ap, shape):
            return ap.broadcast_to(shape)

        def inverse_root(s_, var_ps, inv_n, va, y, t):
            ch(v.tensor_scalar(va, var_ps, inv_n, EPS, ALU.mult, ALU.add))
            ch(v.reciprocal(y, s_))
            ch(v.tensor_tensor(t, y, y, ALU.mult))
            ch(v.tensor_tensor(t, t, va, ALU.mult))
            ch(v.tensor_scalar(t, t, -0.5, 1.5, ALU.mult, ALU.add))
            ch(v.tensor_tensor(y, y, t, ALU.mult))

        for n in range(2):
            ch(v.memset(MR[n][:], 0.0))
        ch(v.memset(CSF[:], 0.0))
        dve.wait_ge(c_silu, 1)
        v.tensor_tensor(CSF[:, :, 0:NC], CT_[:], bank[7][:, 0:NC * KT].rearrange("p (k c) -> p k c", c=NC), ALU.mult).then_inc(c_silu, 1)
        dve.wait_ge(c_silu, 2)
        ch(v.tensor_copy(CSH[:], CSF[:]))
        v.tensor_tensor(CSL[:], CSF[:], CSH[:].bitcast(F32), ALU.subtract).then_inc(c_silu, 1)
        dve.wait_ge(v_copied, 1)

        def mod_add(u, i):
            dve.wait_ge(mod_turned, u + 1 + 12 * i)
            at = bass.ds(24 * i + 2 * u, 2)
            v.tensor_tensor(MOD[:, at], bank[4 + u % 2][:, 0:256].rearrange("p (f c) -> p f c", f=2)[:, :, 0:NC],
                            b3(VEC[:, at].unsqueeze(2), [P, 2, NC]), ALU.add).then_inc(mod_done, 1)

        def mod_units(i):
            for c in range(12):
                for n, h in enumerate((slice(0, 8), slice(8, 16))):
                    dve.wait_ge(mw_hi, 2 * c + n + 1 + 24 * i)
                    last = v.tensor_tensor(MWL[c % 4][:, h], ring[c % 4][:, h], MWH[c % 3][:, h].bitcast(F32), ALU.subtract)
                last.then_inc(mw_lo, 1)
                if c > 3 or not isinstance(i, int):
                    mod_add(c - 4, i)

        mod_units(0)
        with dve.Fori(1, 4) as i:
            mod_units(i)
        for u in range(44, 48):
            mod_add(u, 0)
        dve.wait_ge(mod_done, 48)

        def input_lo(n, out, src, hi, q):
            dve.wait_ge(in_hi, n + 1)
            v.tensor_tensor(out[:, 4 * q:4 * q + 4], src[:, 4 * q:4 * q + 4], hi[:, 4 * q:4 * q + 4].bitcast(F32),
                            ALU.subtract).then_inc(in_lo, 1)

        def norm(n, hi, quarter):
            m0 = 48 * n
            ch(v.tensor_scalar(AM[:], MOD[:, m0 + 16:m0 + 32], 1.0, None, ALU.add))
            ch(v.tensor_tensor(AM[:], AM[:], b3(VEC[:, 98 + 16 * n:114 + 16 * n].unsqueeze(2), [P, KT, NC]), ALU.mult))
            dve.wait_ge(std_done, n + 1)
            inverse_root(n_s[:], bank[6][:, 0:T], 1.0 / D, n_v[:], n_y[:], n_t[:])
            for q in range(4):
                k4 = slice(4 * q, 4 * q + 4)
                ch(v.tensor_tensor(H[:, k4], X[:, k4], b3(n_y[:].unsqueeze(1), [P, 4, T]), ALU.mult))
                for k in range(4 * q, 4 * q + 4):
                    v.tensor_scalar(H[:, k, 0:TP], H[:, k, 0:TP], AM[:, k, 0:1], MOD[:, m0 + k, 0:1], ALU.mult, ALU.add)
                hs = H[:, k4, TP:T].rearrange("p k (b t) -> p k b t", b=NB)
                ch(v.tensor_tensor(hs, hs, b3(AM[:, k4, 1:NC].unsqueeze(3), [P, 4, NB, NT]), ALU.mult))
                v.tensor_tensor(hs, hs, b3(MOD[:, m0 + 4 * q:m0 + 4 * q + 4, 1:NC].unsqueeze(3), [P, 4, NB, NT]), ALU.add)\
                    .then_inc(norm_done, 1)
                if q:
                    input_lo(quarter + q - 1, HL, H, hi, q - 1)
            input_lo(quarter + 3, HL, H, hi, 3)

        norm(0, XH, 0)
        dve.wait_ge(mix_in, 16)
        cos, sin = mix[:, M_COS:M_COS + T], mix[:, M_SIN:M_SIN + T]

        def rotate(r, out, done):
            par = r % 2
            ch(v.tensor_tensor(ra[:], raw[r % 4][:], cos, ALU.mult))
            ch(v.tensor_tensor(rb_[:], bank[4 + par][:, 0:T], sin, ALU.mult))
            last = v.tensor_tensor(out, ra[:], rb_[:], ALU.add)
            if done:
                last.then_inc(rope_done, 1)
            else:
                ch(last)

        def rotate_normed(r, out):
            par = r % 2
            inverse_root(qks[par][:], bank[6 + par][:, 0:T], 1.0 / 128, rv[:], ry[:], rt[:])
            rotate(r, ra[:], False)
            v.tensor_tensor(out, ra[:], ry[:], ALU.mult).then_inc(rope_done, 1)

        dve.wait_ge(rot_done, 1)
        rotate(0, ikT[:], True)
        for u in range(4):
            dve.wait_ge(qk_std, u + 1)
            dve.wait_ge(rope_done, u + 1)
            rotate_normed(1 + u, kTt[:, u])
        with ch.loop(2, 16) as i:
            for u in range(8):
                dve.wait_ge(rot_done, 6 + u + 8 * i)
                dve.wait_ge(rope_done, 5 + u + 8 * i)
                rotate(5 + u, S1[:, bass.ds(8 * i + u, 1)].rearrange("p a t -> p (a t)"), True)
        dve.wait_ge(rope_done, 21)
        ch(v.memset(WZ[:], 0.0))
        dve.wait_ge(wz_mm, 1)
        v.tensor_tensor(WZ[:].rearrange("p (b c) -> p b c", b=NB)[:, :, 0:NT],
                        bank[7][0:64, 0:TS].rearrange("p (b t) -> p b t", b=NB),
                        b3(mix[0:64, M_DT:M_DT + NT].unsqueeze(1), [64, NB, NT]), ALU.mult).then_inc(wz_done, 2)
        dve.wait_ge(ssc_mm, NB)
        v.tensor_tensor(SSC[:], bank[6][0:TS, 0:LS], mix[0:TS, M_SMASK:M_SMASK + LS], ALU.add).then_inc(ssc_read, 1)
        dve.wait_ge(ssc_read, 1)
        for n in range(-(-KSEL_S // 8)):
            left = KSEL_S - 8 * n
            ch(v.max(smx[:], SSC[:]))
            if left < 8:
                ch(v.memset(smx[:, left:8], TAKEN))
            ch(v.match_replace(SSC[:], smx[:], SSC[:], TAKEN))
        ch(v.tensor_scalar(SSC[:], SSC[:], -2e38, NEG, ALU.is_gt, ALU.mult))
        ch(v.tensor_tensor(smb[:], SSC[:], mix[0:TS, M_SMASK:M_SMASK + LS], ALU.add))
        for tt in range(2):
            if tt:
                ch(v.memset(MB[:, 1, 0:128], 0.0))
            ch(v.tensor_copy(MB[:, tt, 128 * tt:128 * (tt + 1)], mix[:, M_TRI:M_TRI + P]))
        ch(v.memset(MB[:, 0, 128:256], NEG))
        for n in range(8):
            h, tt = n // 2, n % 2
            dve.wait_ge(il_done, n + 1)
            for q in range(2):
                last = v.scalar_tensor_tensor(out=E4[:, 2 * q:2 * q + 2],
                                              in0=bank[4 + 2 * tt + q][:].rearrange("p (a s) -> p a s", a=2),
                                              scalar=0.0, in1=b3(iwN[:, tt, 4 * h + 2 * q:4 * h + 2 * q + 2].unsqueeze(2), [P, 2, TP]),
                                              op0=ALU.max, op1=ALU.mult)
            last.then_inc(il_used, 1)
            dve.wait_ge(il_used, n + 2)
            ch(v.tensor_reduce(rsc[:], E4[:].rearrange("p a s -> p s a"), AX.X, ALU.add))
            ch(v.tensor_tensor(MB[:, tt], MB[:, tt], rsc[:], ALU.add))
        dve.wait_ge(il_used, 8 + 1)
        for n in range(KSEL_P // 8):
            for tt in range(2):
                ch(v.max(mx8[:, tt], MB[:, tt]))
                ch(v.match_replace(MB[:, tt], mx8[:, tt], MB[:, tt], TAKEN))
        ch(v.tensor_scalar(MB[:], MB[:], -2e38, NEG, ALU.is_gt, ALU.mult))
        for tt in range(2):
            ch(v.tensor_tensor(MB[:, tt, 128 * tt:128 * (tt + 1)], MB[:, tt, 128 * tt:128 * (tt + 1)],
                               mix[:, M_TRI:M_TRI + P], ALU.add))
        with ch.loop(2, 9 * 8) as i:
            for u in range(8):
                dve.wait_ge(qk_std, 4 + u + 1 + 8 * i)
                dve.wait_ge(rope_done, 21 + u + 8 * i)
                rotate_normed(21 + u, S2[:, bass.ds(8 * i + u, 1)].rearrange("p a t -> p (a t)"))
        dve.wait_ge(rope_done, ROPES)
        with ch.loop(2, 12) as i:
            for k in range(2):
                dve.wait_ge(al_done, 4 * i + 2 * k + 1)
                v.tensor_copy(QG[:], S2[:, bass.ds(8 * i + 4 * k, 4)]).then_inc(ag_ready, 1)
                for tt in range(2):
                    S = 128 * (tt + 1)
                    step = 4 * i + 2 * k + tt
                    dve.wait_ge(al_done, step + 1 + 1)
                    dve.wait_ge(pt_turned, 6 * i + 3 * k + tt + 1)
                    for n in range(2):
                        last = v.tensor_tensor(E4[:, 2 * n:2 * n + 2, 0:S],
                                               bank[4 + n][:].rearrange("p (a s) -> p a s", a=2)[:, :, 0:S],
                                               b3(MB[:, tt:tt + 1, 0:S], [P, 2, S]), ALU.add)
                        if n == 0:
                            ch(last)
                    last.then_inc(al_used, 1)
                    dve.wait_ge(al_used, step + 1 + 1)
                    ch(v.tensor_reduce(st1[:], E4[:, :, 0:S], AX.X, ALU.max))
                    v.tensor_scalar(st1[:], st1[:], -ATT_SCALE, None, ALU.mult).then_inc(al_shift, 1)
                    dve.wait_ge(al_exp, step + 1)
                    ch(v.reciprocal(st2[:], st2[:]))
                    v.tensor_tensor(E4[:, :, 0:S], E4[:, :, 0:S], b3(st2[:].unsqueeze(2), [P, GR, S]), ALU.mult).then_inc(al_prob, 1)
                    dve.wait_ge(ao_done, step + 1 + 1)
                    v.tensor_copy(S1[:, bass.ds(8 * i + 4 * k, 4), 128 * tt:128 * (tt + 1)],
                                  bank[7][:].rearrange("p (a t) -> p a t", a=4)).then_inc(ao_copied, 1)
        dve.wait_ge(ao_copied, 8 + 1)
        for n in range(2):
            ch(v.memset(QSB[n][:], 0.0))
        for b in range(NB):
            if b >= 2:
                dve.wait_ge(sal_done, b - 1)
            v.tensor_copy(QSB[b % 2][:, :, 0:16].rearrange("p g (h t) -> p g h t", h=4),
                          S2[:, :, TP + NT * b:TP + NT * (b + 1)].rearrange("p (g h) t -> p g h t", g=4)).then_inc(sq_ready, 1)
            dve.wait_ge(sal_done, b + 1)
            ch(v.tensor_reduce(sb2[:], bank[6][:, 0:LS], AX.X, ALU.max))
            v.tensor_scalar(sb1[:], sb2[:], -ATT_SCALE, None, ALU.mult).then_inc(sal_max, 1)
            dve.wait_ge(sal_exp, b + 1)
            ch(v.reciprocal(sb1[:], sb2[:]))
            v.tensor_scalar(EN[:], EN[:], sb1[:], None, ALU.mult).then_inc(sal_prob, 1)
            dve.wait_ge(so_done, b + 1)
            v.tensor_copy(S1[:, :, TP + NT * b:TP + NT * (b + 1)],
                          bank[4][:, 0:64].rearrange("p (h t) -> p h t", h=16)).then_inc(so_copied, 1)
        ch(v.memset(PA[:, :, 0:NPRE], 0.0))
        dve.wait_ge(st_copied, 2)
        dve.wait_ge(gemm_evac, U_P + 8)
        for n, (dst, src) in enumerate(((PB, PA), (PC, PB), (PB, PC), (PC, PB))):
            sh = 1 << n
            c0 = 2 * n
            ch(v.tensor_tensor(dst[:, c0:CT, 2 * sh - 1:PADT], src[:, c0:CT, 2 * sh - 1:PADT],
                               src[:, c0:CT, sh - 1:PADT - sh], ALU.add))
            cs = slice(c0, c0 + 2)
            w = POOL_W[n]
            o_p = POOLED[:, cs, 0:TP]
            ch(v.tensor_scalar(o_p[:, :, 16:TP], dst[:, cs, NPRE + 16:PADP], 1.0 / w, None, ALU.mult))
            ch(v.tensor_tensor(o_p[:, :, 0:16], dst[:, cs, NPRE:NPRE + 16],
                               b3(mix[:, M_CNT + 16 * n:M_CNT + 16 * (n + 1)].unsqueeze(1), [P, 2, 16]), ALU.mult))
            ch(v.tensor_tensor(o_p, o_p, PA[:, cs, NPRE:PADP], ALU.subtract))
            for c in range(c0, c0 + 2):
                d_s = dst[:, c, PADP:PADT].rearrange("p (b s) -> p b s", b=NB)[:, :, NPRE:PADS]
                a_s = PA[:, c, PADP:PADT].rearrange("p (b s) -> p b s", b=NB)[:, :, NPRE:PADS]
                last = v.scalar_tensor_tensor(out=POOLED[:, c, TP:T].rearrange("p (b t) -> p b t", b=NB), in0=d_s,
                                              scalar=1.0 / w, in1=a_s, op0=ALU.mult, op1=ALU.subtract)
                if (n, c) != (3, 7):
                    ch(last)
        last.then_inc(pooled_done, 1)

        for q in range(4):
            input_lo(4 + q, AOL, S1, AOH, q)
        dve.wait_ge(gb_back, 16)
        dve.wait_ge(gemm_evac, U_PROJ)
        v.tensor_tensor(S3[:], S3[:], GBS[:], ALU.mult).then_inc(gb_used, 1)
        dve.wait_ge(gb_used, 1)
        dve.wait_ge(ga_back, 16)
        dve.wait_ge(ps_out, 16 * (2 * NB + 1))
        with ch.loop(2, 24) as i:
            for u in range(8):
                dve.wait_ge(gemm_done, U_PROJ + u + 1 + 8 * i)
                dve.wait_ge(gemm_evac, U_PROJ + u + 8 * i)
                s3u = S3[:, bass.ds(8 * i + u, 1)].rearrange("p a t -> p (a t)")
                ch(v.tensor_tensor(SG[u % 2][:], bank[(U_PROJ + u) % 4][:, 0:T],
                                   S2[:, bass.ds(8 * i + u, 1)].rearrange("p a t -> p (a t)"), ALU.mult))
                ch(v.tensor_tensor(SG[u % 2][:], s3u, SG[u % 2][:], ALU.add))
                hi, lo = (x[:, bass.ds(8 * i + u, 1)].rearrange("p a t -> p (a t)") for x in (MGH, MGL))
                ch(v.tensor_copy(hi, SG[u % 2][:]))
                v.tensor_tensor(lo, SG[u % 2][:], hi.bitcast(F32), ALU.subtract).then_inc(gemm_evac, 1)
        dve.wait_ge(x_back, 16)
        with ch.loop(2, 16) as i:
            for u in range(8):
                f = 32 + u
                dve.wait_ge(gemm_done, U_OUT + u + 1 + 8 * i)
                xu = X[:, bass.ds(8 * i + u, 1)].rearrange("p a t -> p (a t)")
                ch(v.scalar_tensor_tensor(out=xu[:, 0:TP], in0=bank[(U_OUT + u) % 4][:, 0:TP],
                                          scalar=MOD[:, bass.ds(8 * i + f, 1), 0:1].rearrange("p a b -> p (a b)"),
                                          in1=xu[:, 0:TP], op0=ALU.mult, op1=ALU.add))
                ch(v.tensor_tensor(og[:].rearrange("p (b t) -> p b t", b=NB),
                                   bank[(U_OUT + u) % 4][:, TP:T].rearrange("p (b t) -> p b t", b=NB),
                                   b3(MOD[:, bass.ds(8 * i + f, 1), 1:NC].rearrange("p a b -> p (a b)").unsqueeze(2), [P, NB, NT]), ALU.mult))
                v.tensor_tensor(xu[:, TP:T], xu[:, TP:T], og[:], ALU.add).then_inc(gemm_evac, 1)
        norm(1, HH, 8)

        for tt, (t0, nt) in enumerate(TILES):
            dve.wait_ge(psc_copied, 2 * tt + 2)
            s_ = slice(0, nt)

            def best(values, index, rows, count):
                for r in range(2):
                    k8 = slice(8 * r, 8 * r + 8)
                    for a in range(count):
                        last = v.max(values[s_, a, k8], rows[s_, a])
                    ch(last)
                    for a in range(count):
                        last = v.max_index(index[s_, a, k8], values[s_, a, k8], rows[s_, a])
                    ch(last)
                    if r == 0:
                        for a in range(count):
                            last = v.match_replace(rows[s_, a], values[s_, a, k8], rows[s_, a], TAKEN)
                        ch(last)

            best(pv, pi, SS, 16)
            v.tensor_copy(pif[s_], pi[s_]).then_inc(ss_free, 1)
            dve.wait_ge(ss_free, tt + 1)
            halves = pv[s_].rearrange("t (h q) k -> t h q k", q=2)
            ch(v.tensor_tensor(CAND[s_].rearrange("t h (a b) -> t h a b", a=PK),
                               b3(halves[:, :, 0].unsqueeze(3), [nt, PH, PK, PK]),
                               b3(halves[:, :, 1].unsqueeze(2), [nt, PH, PK, PK]), ALU.add))
            if tt:
                dve.wait_ge(sl_turned, tt)
            best(wv, wi, CAND, PH)
            ch(v.tensor_copy(s8[s_], wv[s_, :, 0]))
            v.tensor_tensor(wv[s_], wv[s_], b3(s8[s_].unsqueeze(2), [nt, PH, PK]), ALU.subtract).then_inc(pex_done, 1)
            ch(v.tensor_scalar(wa[s_], wi[s_], 4, None, ALU.logical_shift_right))
            ch(v.tensor_copy(waf[s_], wa[s_]))
            ch(v.tensor_scalar(wa[s_], wi[s_], 15, None, ALU.bitwise_and))
            ch(v.tensor_copy(wbf[s_], wa[s_]))
            idx = pif[s_].rearrange("t (h q) k -> t h q k", q=2)
            for q, (wf, out) in enumerate(((waf, ei), (wbf, ej))):
                ch(v.tensor_tensor(EQ[s_], b3(wf[s_].rearrange("t h k -> t (h k)").unsqueeze(2), [nt, PH * PK, PK]),
                                   b3(iota[s_, 0:PK].unsqueeze(1), [nt, PH * PK, PK]), ALU.is_equal))
                e4 = EQ[s_].rearrange("t (h k) a -> t h k a", h=PH)
                ch(v.tensor_tensor(e4, e4, b3(idx[:, :, q].unsqueeze(2), [nt, PH, PK, PK]), ALU.mult))
                last = v.tensor_reduce(out[s_], EQ[s_], AX.X, ALU.add)
                ch(last)
            dve.wait_ge(pex_done, 2 * tt + 2)
            ch(v.tensor_reduce(s8[s_], wv[s_], AX.X, ALU.add))
            ch(v.reciprocal(s8[s_], s8[s_]))
            v.tensor_tensor(wv[s_], wv[s_], b3(s8[s_].unsqueeze(2), [nt, PH, PK]), ALU.mult).then_inc(pw_done, 1)
        dve.wait_ge(slot_copied, 9)
        v.tensor_copy(GP[0][:], GF[:]).then_inc(slots_done, 1)
        dve.wait_ge(slots_done, 1)
        v.tensor_tensor(GRr[:], GF[:], GP[0][:], ALU.subtract).then_inc(slots_done, 1)
        dve.wait_ge(slots_done, 2)
        v.tensor_copy(GP[1][:], GRr[:]).then_inc(slots_done, 1)
        dve.wait_ge(slots_done, 3)
        v.tensor_tensor(GRr[:], GRr[:], GP[1][:], ALU.subtract).then_inc(slots_done, 1)
        dve.wait_ge(slots_done, 4)
        v.tensor_copy(GP[2][:], GRr[:]).then_inc(slots_done, 1)
        dve.wait_ge(slots_done, 5)

        ch(v.tensor_copy(iob[:], b3(iota.unsqueeze(2), [P, P, 2])))
        full = [P, 2, NE, 2]

        def of_keys(ap):
            return b3(ap.unsqueeze(1), full)

        def of_tokens(ap):
            return b3(ap.rearrange("p (a t) -> p a t", a=2).unsqueeze(2), full)

        with ch.loop(T // 8, 2) as i:
            for par in range(2):
                dve.wait_ge(oh_used, 2 * i + par + 1)
                at = bass.ds(8 * i + 4 * par, 4)
                v.tensor_tensor(OA[par][:], of_keys(iob[:]), of_tokens(IB[:, at]), ALU.is_equal)
                ch(v.tensor_tensor(OQ[par][:], of_keys(iob[:]), of_tokens(JB[:, at]), ALU.is_equal))
                for k in range(3):
                    last = v.tensor_tensor(OBp[par][k][:], OQ[par][:], of_tokens(GP[k][:, at]), ALU.mult)
                last.then_inc(oh_ready, 1)
        dve.wait_ge(g_out[1], 16 * (GBODIES + 1))
        ch(v.memset(XS[:], 0.0))

        def expert_lo(i, b):
            dve.wait_ge(ut_hi, EB + 16 * i + b + 1)
            v.tensor_tensor(UTL[b % 4][:], bank[b % 4][:].rearrange("p (k i) -> p k i", k=4),
                            UTH[b % 4][:].bitcast(F32), ALU.subtract).then_inc(ut_lo, 1)

        def weigh(i, jj, act_in, a_hi=AH, a_lo=AL):
            if jj == 0:
                dve.wait_ge(g_in, 16 * i + 16)
            parts = (af[jj % 2][:], act_in, GH[:, :, jj])
            a, b = (x.rearrange("p (c t) -> p c t", c=GCHUNKS) for x in parts[:2])
            ch(v.tensor_tensor(a, b, parts[2], ALU.mult))
            ch(v.tensor_copy(a_hi[jj][:], af[jj % 2][:]))
            v.tensor_tensor(a_lo[jj][:], af[jj % 2][:], a_hi[jj][:].bitcast(F32), ALU.subtract).then_inc(aj_done, 1)

        def weigh_new(i, jj):
            dve.wait_ge(gelu_done, 4 * EARLY + 4 * i + jj + 2)
            if jj == 0:
                dve.wait_ge(o_done, 16 * i + 1)
            weigh(i, jj, gt[jj % 2][:])

        def weigh_scored(i, jj, par):
            if jj == 0:
                dve.wait_ge(ea_in, 16 * i + 16 - 16 * FULL)
                dve.wait_ge(o_done, 16 * i - 16 + 1)
            weigh(i, jj, EA[:, jj], *((AH2, AL2), (AH, AL))[par])

        def scored_lo(i, h, jj):
            dve.wait_ge(v_hi, 8 * i + 4 * h + jj + 1)
            v.tensor_tensor(VL[h][jj][:], VRAW[h][jj][:], VH[h][jj][:].bitcast(F32), ALU.subtract).then_inc(v_lo2, 1)

        def add_outputs(i, par=None, first=True, following=True):
            for m_ in range(KT):
                dve.wait_ge(o_done, 16 * i + m_ + 2)
                o = bank[6 + m_ % 2]
                v.scalar_tensor_tensor(out=X[:, m_, 0:TP], in0=o[:, 0:TP], scalar=MOD[:, 80 + m_, 0:1],
                                       in1=X[:, m_, 0:TP], op0=ALU.mult, op1=ALU.add)
                v.tensor_tensor(XS[:, m_], XS[:, m_], o[:, TP:T], ALU.add).then_inc(o_added, 1)
                if par is not None:
                    if m_ in (3, 5) and not first:
                        scored_lo(i, 1, m_ - 2)
                    if m_ in (6, 8, 9, 11) and following:
                        weigh_scored(i + 1, (6, 8, 9, 11).index(m_), par)
                    if m_ in (12, 14) and following:
                        scored_lo(i + 1, 0, m_ - 11)

        def dve_group(i, last):
            for b in range(14):
                expert_lo(i, b + 2)
                if b % 4 == 1 and b > 4:
                    weigh_new(i, b // 4 - 1)
            weigh_new(i, 3)
            if not last:
                expert_lo(i, 16)
                expert_lo(i, 17)
            dve.wait_ge(o_added, 16 * i + 1)
            if last:
                add_outputs(i, 0)
            else:
                add_outputs(i)

        expert_lo(0, 0)
        expert_lo(0, 1)
        with ch.loop(FULL - 1, 8) as i:
            dve_group(i, False)
        dve_group(FULL - 1, True)
        with ch.loop(EARLY // 2 - 1, 16) as i:
            add_outputs(2 * i + FULL, 1, False)
            add_outputs(2 * i + FULL + 1, 0, False)
        add_outputs(GROUPS - 2, 1, False)
        add_outputs(GROUPS - 1, 0, False, False)
        dve.wait_ge(o_added, 16 * GROUPS + 1)
        xs4 = XS[:].rearrange("p k (b t) -> p k b t", b=NB)
        ch(v.tensor_tensor(xs4, xs4, b3(MOD[:, 80:96, 1:NC].unsqueeze(3), [P, KT, NB, NT]), ALU.mult))
        v.tensor_tensor(X[:, :, TP:T], X[:, :, TP:T], XS[:], ALU.add).then_inc(xs_done, 1)
        for tt, (t0, nt) in enumerate(TILES):
            dve.wait_ge(y_turned, tt + 1)
            if tt == 2:
                dve.wait_ge(y_out[0], 16)
            for n in range(2, 4):
                last = v.tensor_copy(YS[tt % 2][0:nt, 512 * n:512 * (n + 1)], bank[n][0:nt, :])
            last.then_inc(y_dve, 1)

    ctx.close()


_INS = ['x_prompt', 'x_sample', 'cache_k', 'cache_v', 'cache_idx_k', 'state_pool', 'page_table', 'c_prompt', 'c_sample',
        'norm1_g', 'norm2_g', 'w_mod', 'b_mod', 'w_in', 'q_norm_g', 'k_norm_g', 'w_attn_proj', 'w_pool', 'pool_scale',
        'w_out', 'w_peer_q', 'peer_keys', 'peer_u', 'peer_v']
_OUTS = [(1, 256, 2048), (8, 4, 2048), (1, 256, 4, 128), (1, 256, 4, 128), (1, 256, 128), (1, 15, 1024),
         (8, 4, 4, 128), (8, 4, 4, 128), (8, 4, 128), (8, 15, 1024)]


def kernel(**inputs):
    import concourse.bacc as _bacc
    from concourse.bass_utils import run_bass_kernel_spmd as _run

    nc = _bacc.Bacc("TRN2", target_bir_lowering=False, num_devices=1)
    arrays, args = {}, []
    for name in _INS:
        a = np.ascontiguousarray(inputs[name])
        arrays[f"in_{name}"] = a
        args.append(nc.dram_tensor(f"in_{name}", a.shape, mybir.dt.from_np(a.dtype), kind="ExternalInput").ap())
    for name, a in zip(("keep", "mix"), constants()):
        arrays[f"in_{name}"] = a
        args.append(nc.dram_tensor(f"in_{name}", a.shape, F32, kind="ExternalInput").ap())
    for i, shape in enumerate(_OUTS):
        args.append(nc.dram_tensor(f"out_{i}", shape, F32, kind="ExternalOutput").ap())
    layer_kernel(nc, *args)
    r = _run(nc, [arrays], core_ids=[0])
    return tuple(r.results[0][f"out_{i}"] for i in range(len(_OUTS)))
```
